# Optimizing a Trainium2 kernel written in Bass

```python
import jax, jax.numpy as jnp
from jax import lax
import numpy as np

D_MODEL = 1024
BATCH = 1
SEQ = 512
DEPTH = 1
DEC_BATCH = 8
DEC_SEQ = 4
PAST_LEN = 4096
PAGE_SIZE = 128

RWKV_HEADS = 8
RWKV_HEAD_DIM = 64
RWKV_WIDTH = RWKV_HEADS * RWKV_HEAD_DIM
LORA_W = 64
LORA_A = 64
LORA_V = 32
LORA_G = 128
RWKV_SPLITS = (RWKV_WIDTH, 2 * RWKV_WIDTH, 3 * RWKV_WIDTH, 3 * RWKV_WIDTH + LORA_W, 3 * RWKV_WIDTH + LORA_W + LORA_A)
RWKV_COLS = 3 * RWKV_WIDTH + LORA_W + LORA_A + LORA_G
GN_EPS = RWKV_HEAD_DIM * 1e-5
CONV_WIDTH = 31
CONV_CH = 512
CONV_BUF = CONV_WIDTH - 1
N_MEM = 256
MEM_HEADS = 4
MEM_HEAD_DIM = 128
MEM_WIDTH = MEM_HEADS * MEM_HEAD_DIM
N_BRANCH = 3
OFF_GLU = RWKV_COLS
OFF_Q = OFF_GLU + 2 * CONV_CH
OFF_GATE = OFF_Q + MEM_WIDTH
IN_COLS = OFF_GATE + N_BRANCH * D_MODEL
N_EXPERTS = 128
TOP_K = 8
D_EXPERT = 256
D_SHARED = 256
ROUTED_SCALE = 2.5
MOE_BLOCK = 64
LN_EPS = 1e-5
ALPHA = (2 * DEPTH) ** 0.25
BETA = (8 * DEPTH) ** -0.25

kernel_name = 'rwkv7_conformer_memattn_moe_deepnorm_step'

def layer_norm(x, g, b, eps):
    xf = x.astype(jnp.float32)
    mu = jnp.mean(xf, axis=-1, keepdims=True)
    var = jnp.mean(jnp.square(xf - mu), axis=-1, keepdims=True)
    y = (xf - mu) * lax.rsqrt(var + eps) * g.astype(jnp.float32) + b.astype(jnp.float32)
    return y.astype(x.dtype)

def wkv7_scan(S0, r, decay, k, v, kk, a):
    def step(S, inp):
        r_t, w_t, k_t, v_t, kk_t, a_t = inp
        sa = jnp.einsum('bhvk,bhk->bhv', S, -kk_t)
        S = (S * w_t[:, :, None, :] + sa[..., None] * (kk_t * a_t)[:, :, None, :]
             + v_t[..., None] * k_t[:, :, None, :])
        return S, jnp.einsum('bhvk,bhk->bhv', S, r_t)
    xs = tuple(jnp.swapaxes(z, 0, 1) for z in (r, decay, k, v, kk, a))
    S, y = lax.scan(step, S0, xs)
    return S, jnp.swapaxes(y, 0, 1)

def rwkv7_branch(p_rwkv, p_vd, v_first, S0, prm, layer_idx):
    B, T, _ = p_rwkv.shape
    r, k, v, wd, ad, gd = jnp.split(p_rwkv, list(RWKV_SPLITS), axis=-1)
    log_w = -jax.nn.softplus(-(prm['w0'] + jnp.tanh(wd) @ prm['w_up'])) - 0.5
    decay = jnp.exp(-jnp.exp(log_w.astype(jnp.float32)))
    a = jax.nn.sigmoid(prm['a0'] + ad @ prm['a_up'])
    g = jax.nn.sigmoid(gd) @ prm['g_up']
    if layer_idx == 0:
        v_first = v
    else:
        v = v + (v_first - v) * jax.nn.sigmoid(prm['v0'] + p_vd @ prm['v_up'])

    def heads(z):
        return z.reshape(B, T, RWKV_HEADS, RWKV_HEAD_DIM).astype(jnp.float32)

    kk = heads(k * prm['k_k'])
    kk = kk / jnp.maximum(jnp.linalg.norm(kk, axis=-1, keepdims=True), 1e-12)
    k = k * (1.0 + (a - 1.0) * prm['k_a'])
    rh, kh, vh, ah = heads(r), heads(k), heads(v), heads(a)
    S, y = wkv7_scan(S0, rh, heads(decay), kh, vh, kk, ah)
    mu = jnp.mean(y, axis=-1, keepdims=True)
    var = jnp.mean(jnp.square(y - mu), axis=-1, keepdims=True)
    y = ((y - mu) * lax.rsqrt(var + GN_EPS)).reshape(B, T, RWKV_WIDTH)
    y = y * prm['lnx_g'].astype(jnp.float32) + prm['lnx_b'].astype(jnp.float32)
    bonus = (jnp.sum(rh * kh * prm['r_k'].astype(jnp.float32), axis=-1, keepdims=True) * vh).reshape(B, T, RWKV_WIDTH)
    out = ((y + bonus).astype(g.dtype) * g) @ prm['w_o_a']
    return out, S, v_first

def conv_module(p_glu, conv_buf, prm):
    glu = p_glu[..., :CONV_CH] * jax.nn.sigmoid(p_glu[..., CONV_CH:])
    ext = jnp.concatenate([conv_buf.astype(glu.dtype), glu], axis=1)
    h = lax.conv_general_dilated(ext, prm['conv_w'].astype(ext.dtype)[:, None, :],
                                 window_strides=(1,), padding='VALID',
                                 dimension_numbers=('NWC', 'WIO', 'NWC'),
                                 feature_group_count=CONV_CH)
    h = jax.nn.silu(layer_norm(h + prm['conv_b'], prm['cn_g'], prm['cn_b'], LN_EPS))
    return h @ prm['w_o_b'], ext[:, -CONV_BUF:]

def memory_attention(q, mem_k, mem_v, w_o_c):
    B, T, _ = q.shape
    q = q.reshape(B, T, MEM_HEADS, MEM_HEAD_DIM)
    s = jnp.einsum('bthd,bmhd->bhtm', q, mem_k.astype(q.dtype)).astype(jnp.float32) * (MEM_HEAD_DIM ** -0.5)
    pr = jax.nn.softmax(s, axis=-1).astype(q.dtype)
    o = jnp.einsum('bhtm,bmhd->bthd', pr, mem_v.astype(q.dtype)).reshape(B, T, MEM_WIDTH)
    return o @ w_o_c

def moe_ffn(x, prm):
    B, T, D = x.shape
    n_tok = B * T
    xt = x.reshape(n_tok, D)
    scores = jax.nn.sigmoid((xt @ prm['w_router']).astype(jnp.float32))
    _, idx = lax.top_k(scores + prm['b_router'].astype(jnp.float32), TOP_K)
    sel = jnp.take_along_axis(scores, idx, axis=-1)
    gate = sel / jnp.sum(sel, axis=-1, keepdims=True) * ROUTED_SCALE
    n_assign = n_tok * TOP_K
    flat_e = idx.reshape(-1)
    order = jnp.argsort(flat_e)
    e_sorted = flat_e[order]
    counts = jnp.zeros((N_EXPERTS,), jnp.int32).at[flat_e].add(1)
    padded = (counts + MOE_BLOCK - 1) // MOE_BLOCK * MOE_BLOCK
    start_sorted = jnp.cumsum(counts) - counts
    end_padded = jnp.cumsum(padded)
    start_padded = end_padded - padded
    dest = start_padded[e_sorted] + jnp.arange(n_assign, dtype=jnp.int32) - start_sorted[e_sorted]
    n_blocks = (n_assign + MOE_BLOCK - 1) // MOE_BLOCK + N_EXPERTS
    n_slots = n_blocks * MOE_BLOCK
    slot_tok = jnp.zeros((n_slots,), jnp.int32).at[dest].set((order // TOP_K).astype(jnp.int32))
    slot_w = jnp.zeros((n_slots,), jnp.float32).at[dest].set(gate.reshape(-1)[order])
    block_e = jnp.minimum(jnp.searchsorted(end_padded, jnp.arange(n_blocks, dtype=jnp.int32) * MOE_BLOCK, side='right'), N_EXPERTS - 1)

    def block_step(acc, blk):
        tok, w, e = blk
        xb = xt[tok]
        h = jax.nn.silu(xb @ prm['w_e1'][e]) * (xb @ prm['w_e3'][e])
        yb = (h @ prm['w_e2'][e]).astype(jnp.float32) * w[:, None]
        return acc.at[tok].add(yb), None

    routed, _ = lax.scan(block_step, jnp.zeros((n_tok, D), jnp.float32),
                         (slot_tok.reshape(n_blocks, MOE_BLOCK), slot_w.reshape(n_blocks, MOE_BLOCK), block_e))
    shared = (jax.nn.silu(xt @ prm['w_s1']) * (xt @ prm['w_s3'])) @ prm['w_s2']
    return (shared.astype(jnp.float32) + routed).astype(x.dtype).reshape(B, T, D)

def trunk_layer(x, mem_k, mem_v, S0, x_prev, conv_buf, v_first, prm, layer_idx):
    B, T, D = x.shape
    w_in = prm['w_in']
    if layer_idx > 0:
        w_in = jnp.concatenate([w_in, prm['w_in_vmix']], axis=1)
    proj = x @ w_in
    prev = x_prev.astype(x.dtype) @ w_in

    def shift_lerp(cur, before, mu):
        shifted = jnp.concatenate([before[:, None], cur[:, :-1]], axis=1)
        return cur + (shifted - cur) * mu

    p_rwkv = shift_lerp(proj[..., :RWKV_COLS], prev[:, :RWKV_COLS], prm['mu_shift'])
    p_vd = shift_lerp(proj[..., IN_COLS:], prev[:, IN_COLS:], prm['mu_vmix']) if layer_idx > 0 else None
    y_a, S_new, v_first = rwkv7_branch(p_rwkv, p_vd, v_first, S0, prm, layer_idx)
    y_b, conv_new = conv_module(proj[..., OFF_GLU:OFF_Q], conv_buf, prm)
    y_c = memory_attention(proj[..., OFF_Q:OFF_GATE], mem_k, mem_v, prm['w_o_c'])
    gates = jax.nn.sigmoid(proj[..., OFF_GATE:IN_COLS]).reshape(B, T, N_BRANCH, D)
    merged = gates[:, :, 0] * y_a + gates[:, :, 1] * y_b + gates[:, :, 2] * y_c
    h = layer_norm(ALPHA * x + merged @ prm['w_out'], prm['ln1_g'], prm['ln1_b'], LN_EPS)
    y = layer_norm(ALPHA * h + moe_ffn(h, prm), prm['ln2_g'], prm['ln2_b'], LN_EPS)
    return y, S_new, x[:, -1], conv_new, v_first

def setup_inputs(seed: int = 0) -> dict:
    key = jax.random.key(seed)
    keys = jax.random.split(key, 48)
    cnt = [0]

    def nxt():
        k = keys[cnt[0]]
        cnt[0] += 1
        return k

    def nrm(shape, scale):
        return scale * jax.random.normal(nxt(), shape, jnp.float32)

    def uni(shape, lo, hi):
        return jax.random.uniform(nxt(), shape, jnp.float32, lo, hi)

    L, Lm, D = DEPTH, DEPTH - 1, D_MODEL
    return {
        'x_prompt': nrm((BATCH, SEQ, D), 1.0),
        'x_sample': nrm((DEC_BATCH, DEC_SEQ, D), 1.0),
        'state_wkv': nrm((L, DEC_BATCH, RWKV_HEADS, RWKV_HEAD_DIM, RWKV_HEAD_DIM), 0.1),
        'state_shift': nrm((L, DEC_BATCH, D), 1.0),
        'state_conv': nrm((L, DEC_BATCH, CONV_BUF, CONV_CH), 0.5),
        'cache_mem_k': nrm((L, DEC_BATCH, N_MEM, MEM_HEADS, MEM_HEAD_DIM), 1.0),
        'cache_mem_v': nrm((L, DEC_BATCH, N_MEM, MEM_HEADS, MEM_HEAD_DIM), 1.0),
        'mem_prompt': nrm((BATCH, N_MEM, D), 1.0),
        'w_in': nrm((L, D, IN_COLS), D ** -0.5),
        'w_in_vmix': nrm((Lm, D, LORA_V), D ** -0.5),
        'mu_shift': uni((L, RWKV_COLS), 0.0, 1.0),
        'mu_vmix': uni((Lm, LORA_V), 0.0, 1.0),
        'w0': uni((L, RWKV_WIDTH), -6.0, -1.0),
        'w_up': nrm((L, LORA_W, RWKV_WIDTH), 0.1),
        'a0': nrm((L, RWKV_WIDTH), 0.1),
        'a_up': nrm((L, LORA_A, RWKV_WIDTH), 0.1),
        'v0': nrm((Lm, RWKV_WIDTH), 0.5),
        'v_up': nrm((Lm, LORA_V, RWKV_WIDTH), 0.1),
        'g_up': nrm((L, LORA_G, RWKV_WIDTH), LORA_G ** -0.5),
        'k_k': 0.85 + nrm((L, RWKV_WIDTH), 0.05),
        'k_a': 1.0 + nrm((L, RWKV_WIDTH), 0.05),
        'r_k': nrm((L, RWKV_HEADS, RWKV_HEAD_DIM), 0.1),
        'lnx_g': 1.0 + nrm((L, RWKV_WIDTH), 0.05),
        'lnx_b': nrm((L, RWKV_WIDTH), 0.02),
        'w_o_a': nrm((L, RWKV_WIDTH, D), RWKV_WIDTH ** -0.5),
        'conv_w': nrm((L, CONV_WIDTH, CONV_CH), CONV_WIDTH ** -0.5),
        'conv_b': nrm((L, CONV_CH), 0.02),
        'cn_g': 1.0 + nrm((L, CONV_CH), 0.05),
        'cn_b': nrm((L, CONV_CH), 0.02),
        'w_o_b': nrm((L, CONV_CH, D), CONV_CH ** -0.5),
        'w_mem_kv': nrm((L, D, 2 * MEM_WIDTH), D ** -0.5),
        'w_o_c': nrm((L, MEM_WIDTH, D), MEM_WIDTH ** -0.5),
        'w_out': nrm((L, D, D), BETA * D ** -0.5),
        'ln1_g': 1.0 + nrm((L, D), 0.05),
        'ln1_b': nrm((L, D), 0.02),
        'ln2_g': 1.0 + nrm((L, D), 0.05),
        'ln2_b': nrm((L, D), 0.02),
        'w_router': nrm((L, D, N_EXPERTS), D ** -0.5),
        'b_router': nrm((L, N_EXPERTS), 0.01),
        'w_e1': nrm((L, N_EXPERTS, D, D_EXPERT), D ** -0.5),
        'w_e3': nrm((L, N_EXPERTS, D, D_EXPERT), D ** -0.5),
        'w_e2': nrm((L, N_EXPERTS, D_EXPERT, D), BETA * D_EXPERT ** -0.5),
        'w_s1': nrm((L, D, D_SHARED), D ** -0.5),
        'w_s3': nrm((L, D, D_SHARED), D ** -0.5),
        'w_s2': nrm((L, D_SHARED, D), BETA * D_SHARED ** -0.5),
    }

def reference(x_prompt, x_sample, state_wkv, state_shift, state_conv, cache_mem_k, cache_mem_v, mem_prompt,
              w_in, w_in_vmix, mu_shift, mu_vmix, w0, w_up, a0, a_up, v0, v_up, g_up, k_k, k_a, r_k,
              lnx_g, lnx_b, w_o_a, conv_w, conv_b, cn_g, cn_b, w_o_b, w_mem_kv, w_o_c, w_out,
              ln1_g, ln1_b, ln2_g, ln2_b, w_router, b_router, w_e1, w_e3, w_e2, w_s1, w_s3, w_s2):
    Bp, Bs = x_prompt.shape[0], x_sample.shape[0]
    n_mem = mem_prompt.shape[1]
    xp, xs = x_prompt, x_sample
    vf_p, vf_s = None, None
    wkv_p, shift_p, conv_p, mk_list, mv_list = [], [], [], [], []
    wkv_s, shift_s, conv_s = [], [], []
    for l in range(DEPTH):
        prm = {'w_in': w_in[l], 'mu_shift': mu_shift[l], 'w0': w0[l], 'w_up': w_up[l], 'a0': a0[l],
               'a_up': a_up[l], 'g_up': g_up[l], 'k_k': k_k[l], 'k_a': k_a[l], 'r_k': r_k[l],
               'lnx_g': lnx_g[l], 'lnx_b': lnx_b[l], 'w_o_a': w_o_a[l], 'conv_w': conv_w[l],
               'conv_b': conv_b[l], 'cn_g': cn_g[l], 'cn_b': cn_b[l], 'w_o_b': w_o_b[l],
               'w_o_c': w_o_c[l], 'w_out': w_out[l], 'ln1_g': ln1_g[l], 'ln1_b': ln1_b[l],
               'ln2_g': ln2_g[l], 'ln2_b': ln2_b[l], 'w_router': w_router[l], 'b_router': b_router[l],
               'w_e1': w_e1[l], 'w_e3': w_e3[l], 'w_e2': w_e2[l],
               'w_s1': w_s1[l], 'w_s3': w_s3[l], 'w_s2': w_s2[l]}
        if l > 0:
            prm['w_in_vmix'] = w_in_vmix[l - 1]
            prm['mu_vmix'] = mu_vmix[l - 1]
            prm['v0'] = v0[l - 1]
            prm['v_up'] = v_up[l - 1]
        kv = mem_prompt.astype(xp.dtype) @ w_mem_kv[l]
        mk_p = kv[..., :MEM_WIDTH].reshape(Bp, n_mem, MEM_HEADS, MEM_HEAD_DIM)
        mv_p = kv[..., MEM_WIDTH:].reshape(Bp, n_mem, MEM_HEADS, MEM_HEAD_DIM)
        S0_p = jnp.zeros((Bp, RWKV_HEADS, RWKV_HEAD_DIM, RWKV_HEAD_DIM), jnp.float32)
        prev_p = jnp.zeros((Bp, D_MODEL), xp.dtype)
        buf_p = jnp.zeros((Bp, CONV_BUF, CONV_CH), xp.dtype)
        xp, S_p, sh_p, cb_p, vf_p = trunk_layer(xp, mk_p, mv_p, S0_p, prev_p, buf_p, vf_p, prm, l)
        xs, S_s, sh_s, cb_s, vf_s = trunk_layer(xs, cache_mem_k[l], cache_mem_v[l], state_wkv[l].astype(jnp.float32),
                                                state_shift[l], state_conv[l], vf_s, prm, l)
        wkv_p.append(S_p.astype(state_wkv.dtype))
        shift_p.append(sh_p.astype(state_shift.dtype))
        conv_p.append(cb_p.astype(state_conv.dtype))
        mk_list.append(mk_p.astype(cache_mem_k.dtype))
        mv_list.append(mv_p.astype(cache_mem_v.dtype))
        wkv_s.append(S_s.astype(state_wkv.dtype))
        shift_s.append(sh_s.astype(state_shift.dtype))
        conv_s.append(cb_s.astype(state_conv.dtype))
    return (xp, xs, jnp.stack(wkv_p), jnp.stack(shift_p), jnp.stack(conv_p), jnp.stack(mk_list), jnp.stack(mv_list),
            jnp.stack(wkv_s), jnp.stack(shift_s), jnp.stack(conv_s))


_drawn_inputs = setup_inputs


def setup_inputs(seed=0):
    import zlib

    import numpy as np

    out = dict(_drawn_inputs(seed))
    spreads = {}
    factors = {'lnx_b': 3.052, 'cn_b': 2.977, 'ln2_b': 2.691}
    for name, (base, spread) in spreads.items():
        noise = np.random.default_rng([zlib.crc32(name.encode()), seed]).standard_normal(out[name].shape)
        drawn = base * np.exp(spread * noise) if base else spread * noise
        out[name] = __import__('jax').numpy.asarray(drawn.astype(out[name].dtype))
    for name, factor in factors.items():
        out[name] = (out[name] * factor).astype(out[name].dtype)
    return out
```

```python
from contextlib import ExitStack

import concourse.bass as bass
from concourse import mybir

F32 = mybir.dt.float32
U32 = mybir.dt.uint32
I32 = mybir.dt.int32
ALU = mybir.AluOpType
ACT = mybir.ActivationFunctionType
AX = mybir.AxisListType
ds = bass.ds

P = 128
D = 1024
KD = D // P
SEQ, BS, TS = 512, 8, 4
SB = TS + 1
NS = BS * SB
NT = SEQ + NS
HALF = NT // 2
W = 512
KW = W // P
HD = 64
CH = 64
NCH = SEQ // CH
TAPS = 31
BUF = TAPS - 1
NM = 256
MT = NM // P
MH = 4
RW = 3 * W + 64 + 64 + 128
N_RW, N_GLU, N_Q = RW // P, 2 * W // P, W // P
OFF_GLU, OFF_Q = RW, RW + 2 * W
OFF_GATE = OFF_Q + W
NE, TOPK, DE = 128, 8, 256
ALPHA = 2.0 ** 0.25
LN_EPS = 1e-5
GN_EPS = HD * 1e-5
RATE = 0.6065306597126334
ROUTED = 2.5
SLOTS = 64
FAR = 8192.0
TILES = [(i * P, P) for i in range(SEQ // P)] + [(SEQ, NS)]
NTT = len(TILES)

T_GLU, T_RW = 0, N_GLU
T_R, T_K, T_V, T_WA, T_G = T_RW, T_RW + KW, T_RW + 2 * KW, T_RW + 3 * KW, T_RW + 3 * KW + 1
T_Q = T_RW + N_RW
N_PROJ = T_Q + N_Q
PW = NT + 1

V_MU, V_W0, V_A0, V_KK, V_KA, V_RK, V_LG, V_LB, V_CB, V_CG, V_CBB = 0, 14, 18, 22, 26, 30, 34, 38, 42, 46, 50
N_VEC = 54

ARENA = 50688
WEXP = 6 * 1024
O_XT = 0
O_PROJ = O_XT + KD * NT
O_RATE = O_PROJ + N_PROJ * PW
O_AGATE = O_RATE + KW * NT
O_OUTG = O_AGATE + KW * NT
O_KKEY = O_OUTG + KW * NT
O_BKEY = O_KKEY + KW * NT
O_EXT = O_BKEY + KW * NT
O_EXS = O_EXT + KW * (SEQ + BUF)
O_CONV = O_EXS + KW * BS * (TS + BUF)
O_WBUF = O_CONV + KW * NT
O_TMP = O_WBUF + 2 * D
O_TOP = ARENA - 2 * WEXP
assert O_TMP + NT <= O_TOP

OUT_LOAD = 3
OUT_PROJECT = OUT_LOAD + 1 + BS
OUT_WKV = OUT_PROJECT + 1
OUT_ATTEND = OUT_WKV + 2 * MT
OUT_ALL = OUT_ATTEND + NTT - 1 + TS


class Memory:

    def __init__(self, nc, ctx):
        self.nc, self.ctx, self.sems = nc, ctx, {}
        self.arena = self.sb("arena", [P, ARENA])
        self.ident = self.sb("ident", [P, P])
        self.fold = self.sb("fold", [P, HD])
        self.upper = self.sb("upper", [P, 2, P])
        self.lower = self.sb("lower", [P, P])
        self.ones = self.sb("ones", [P, P])
        self.heads = self.sb("heads", [P, P])
        self.vec = self.sb("vec", [P, N_VEC])
        self.taps = self.sb("taps", [P, TAPS * KW])
        self.slot = self.sb("slot", [P, SLOTS])
        self.row = self.sb("row", [P, NTT])
        self.valid = self.sb("valid", [P, 1])
        self.xlast = self.sb("xlast", [P, 64])
        self.rounds = self.sb("rounds", [P, 1], I32)
        self.index = self.sb("index", [P, 4, 2], U32)
        self.ps = [ctx.enter_context(nc.psum_tensor(f"bank{i}", [P, 512], F32)) for i in range(8)]

    def sb(self, name, shape, dt=F32):
        return self.ctx.enter_context(self.nc.sbuf_tensor(name, shape, dt))

    def sem(self, name):
        if name not in self.sems:
            self.sems[name] = self.nc.alloc_semaphore(name=name)
        return self.sems[name]

    def recycle(self, names):
        with self.nc.Block() as block:
            @block.gpsimd
            def _(pool):
                for name in names:
                    pool.sem_clear(self.sems[name])
        for name in names:
            self.nc.release_semaphore(self.sems.pop(name))

    def at(self, offset, *shape):
        n = 1
        for s in shape:
            n *= s
        assert offset + n <= ARENA
        v = self.arena[:, offset:offset + n]
        if len(shape) == 2:
            return v.rearrange("p (a b) -> p a b", a=shape[0])
        if len(shape) == 3:
            return v.rearrange("p (a b c) -> p a b c", a=shape[0], b=shape[1])
        if len(shape) == 4:
            return v.rearrange("p (a b c d) -> p a b c d", a=shape[0], b=shape[1], c=shape[2])
        return v


def sample_cols(ap):
    return ap.rearrange("p (b s) -> p b s", s=SB)[:, :, 1:SB]


def stage_load(nc, m, io):
    xtok = m.at(O_PROJ, NTT, D)
    vrows = m.at(O_PROJ + NTT * D, P)
    trows = m.at(O_PROJ + NTT * D + P, P)
    crows = m.at(O_PROJ + NTT * D + 2 * P, 2, W)
    xT = m.at(O_XT, KD, NT)
    exs = m.at(O_EXS, KW, BS, TS + BUF)
    ext = m.at(O_EXT, KW, SEQ + BUF)
    proj = m.at(O_PROJ, N_PROJ, PW)
    CR = BS * BUF // 2
    s_const, s_x = m.sem("constants_ready"), [m.sem(f"x_rows_{i}") for i in range(NTT)]
    s_v, s_cs = m.sem("vectors_loaded"), m.sem("conv_state_loaded")
    s_t, s_e = m.sem("turned"), m.sem("turned_copied")

    groups = []
    for i, (c0, n) in enumerate(TILES):
        for g in range(2):
            groups.append((s_x[i], 16 if i < NTT - 1 else 16 * (1 + TS), n,
                           [xtok[0:n, i, (4 * g + k) * P:(4 * g + k + 1) * P] for k in range(4)],
                           xT[:, 4 * g:4 * g + 4, c0:c0 + n]))
    for r in range(2):
        groups.append((s_cs, 32, CR, [crows[0:CR, r, j * P:(j + 1) * P] for j in range(KW)],
                       exs[:, :, 4 * r:4 * r + 4, 0:BUF]))
    vec_wait = 16 * 11 + 16
    groups.append((s_v, vec_wait, N_VEC, [vrows[0:N_VEC, :]], m.vec[:, :]))
    groups.append((s_v, vec_wait, TAPS * KW, [trows[0:TAPS * KW, :]], m.taps[:, :]))

    with nc.Block() as block:
        @block.sync
        def _(sp):
            for i in range(NTT - 1):
                sp.dma_start(xtok[:, i, :], io["x_prompt"][0, i * P:(i + 1) * P, :]).then_inc(s_x[i], 16)
            sp.dma_start(xtok[0:NS:SB, NTT - 1, :], io["state_shift"][0]).then_inc(s_x[-1], 16)
            for t in range(TS):
                sp.dma_start(xtok[1 + t:NS:SB, NTT - 1, :], io["x_sample"][:, t, :]).then_inc(s_x[-1], 16)

        @block.scalar
        def _(act):
            for at, name in ((V_MU, "mu_shift"), (V_W0, "w0"), (V_A0, "a0"), (V_KK, "k_k"), (V_KA, "k_a"),
                             (V_LG, "lnx_g"), (V_LB, "lnx_b"), (V_CB, "conv_b"), (V_CG, "cn_g"), (V_CBB, "cn_b")):
                v = io[name][0].rearrange("(j p) -> j p", p=P)
                act.dma_start(vrows[at:at + v.shape[0], :], v).then_inc(s_v, 16)
            act.dma_start(vrows[V_RK:V_RK + KW, :], io["r_k"][0].rearrange("(j h) n -> j (h n)", h=2)).then_inc(s_v, 16)
            act.dma_start(trows[0:TAPS * KW, :], io["conv_w"][0].rearrange("k (j p) -> (k j) p", p=P)).then_inc(s_v, 16)
            cs = io["state_conv"][0].rearrange("b i c -> (b i) c")
            for r in range(2):
                act.dma_start(crows[0:CR, r, :], cs[r * CR:(r + 1) * CR, :]).then_inc(s_cs, 16)
            act.dma_start(io["out_shift_p"][0], io["x_prompt"][:, SEQ - 1, :]).then_inc(m.sem("outputs_written"), 16)
            act.dma_start(io["out_shift_s"][0], io["x_sample"][:, TS - 1, :]).then_inc(m.sem("outputs_written"), 16)
            act.dma_start(io["out_conv_s"][0][:, 0:BUF - TS, :], io["state_conv"][0][:, TS:BUF, :])\
               .then_inc(m.sem("outputs_written"), 16)

        @block.gpsimd
        def _(pool):
            pool.memset(m.ident[:], 1.0)
            pool.memset(m.fold[:], 1.0)
            pool.memset(m.upper[:], 1.0)
            pool.memset(m.lower[:], 1.0)
            pool.memset(m.ones[:], 1.0)
            pool.memset(m.heads[:], 0.0)
            pool.memset(m.valid[:], 1.0)
            pool.memset(ext[:, :, 0:BUF], 0.0)
            pool.drain()
            pool.memset(m.heads[0:HD, 0:HD], 1.0)
            pool.memset(m.heads[HD:P, HD:P], 1.0)
            pool.drain()
            pool.affine_select(out=m.ident[:], in_=m.ident[:], compare_op=ALU.is_equal, fill=0.0, base=0,
                               pattern=[[-1, P]], channel_multiplier=1)
            pool.drain()
            pool.affine_select(out=m.fold[0:HD, :], in_=m.fold[0:HD, :], compare_op=ALU.is_equal, fill=0.0, base=0,
                               pattern=[[-1, HD]], channel_multiplier=1)
            pool.affine_select(out=m.fold[HD:P, :], in_=m.fold[HD:P, :], compare_op=ALU.is_equal, fill=0.0, base=0,
                               pattern=[[-1, HD]], channel_multiplier=1)
            pool.drain()
            pool.affine_select(out=m.upper[:, 0, :], in_=m.upper[:, 0, :], compare_op=ALU.is_gt, fill=0.0, base=0,
                               pattern=[[1, P]], channel_multiplier=-1)
            pool.affine_select(out=m.upper[:, 1, :], in_=m.upper[:, 1, :], compare_op=ALU.is_ge, fill=0.0, base=0,
                               pattern=[[1, P]], channel_multiplier=-1)
            pool.affine_select(out=m.lower[:], in_=m.lower[:], compare_op=ALU.is_gt, fill=0.0, base=0,
                               pattern=[[-1, P]], channel_multiplier=1)
            pool.iota(m.slot[:], pattern=[[1, SLOTS]], base=0, channel_multiplier=0, allow_small_or_imprecise_dtypes=True)
            pool.iota(m.row[:], pattern=[[P, NTT]], base=0, channel_multiplier=1, allow_small_or_imprecise_dtypes=True)
            pool.drain()
            pool.affine_select(out=m.valid[:], in_=m.valid[:], compare_op=ALU.is_gt, fill=0.0, base=NS,
                               pattern=[[0, 1]], channel_multiplier=-1)
            pool.drain()
            for b in range(BS):
                pool.affine_select(out=m.valid[:], in_=m.valid[:], compare_op=ALU.not_equal, fill=0.0, base=-SB * b,
                                   pattern=[[0, 1]], channel_multiplier=1)
                pool.drain()
            pool.memset(m.xlast[:], 0.0).then_inc(s_const, 1)

        @block.tensor
        def _(pe):
            pe.wait_ge(s_const, 1)
            for g, (sem, val, n, sources, _) in enumerate(groups):
                pe.wait_ge(sem, val)
                if g >= 8:
                    pe.wait_ge(s_e, g - 7)
                for k, src in enumerate(sources):
                    last = pe.transpose(m.ps[g % 8][:, k * n:(k + 1) * n] if src.shape[1] == P else None,
                                        src, m.ident[0:n, 0:n])
                last.then_inc(s_t, 1)

        @block.vector
        def _(dve):
            for g, (_, _, n, sources, out) in enumerate(groups):
                dve.wait_ge(s_t, g + 1)
                src = m.ps[g % 8][:, 0:n * len(sources)]
                if len(out.shape) == 3:
                    src = src.rearrange("p (k n) -> p k n", n=n)
                if len(out.shape) == 4:
                    src = src.rearrange("p (k b i) -> p k b i", k=KW, b=BS // 2)
                    for j in range(KW):
                        last = dve.tensor_copy(out[:, j], src[:, j])
                    last.then_inc(s_e, 1)
                    continue
                dve.tensor_copy(out, src).then_inc(s_e, 1)
            dve.wait_ge(s_e, len(groups))
            dve.memset(proj[:, :, 0:1], 0.0)


def stage_project(nc, m, io):
    xT, proj = m.at(O_XT, KD, NT), m.at(O_PROJ, N_PROJ, PW)
    ext, exs = m.at(O_EXT, KW, SEQ + BUF), m.at(O_EXS, KW, BS, TS + BUF)
    conv, wbuf, tmp = m.at(O_CONV, KW, NT), m.at(O_WBUF, 2, KD, P), m.at(O_TMP, NT)
    last_rows = m.at(O_TOP, 2, W)
    new_glu = m.at(O_TOP + 2 * W, KW, BS * TS)
    w_in = io["w_in"][0].rearrange("(k p) n -> p k n", p=P)
    s_w = [m.sem(f"w_in_loaded_{u}") for u in range(2)]
    s_mm, s_free = m.sem("column_tile_done"), m.sem("column_banks_free")
    s_ev = m.sem("column_tile_copied")
    s_glu, s_gt, s_gc = m.sem("glu_done"), m.sem("glu_tail_turned"), m.sem("glu_tail_copied")

    with nc.Block() as block:
        @block.sync
        def _(sp):
            def load(n, col):
                sp.dma_start(wbuf[:, n % 2], w_in[:, :, ds(col, P)]).then_inc(s_w[n % 2], 16)

            load(0, OFF_GLU)
            load(1, OFF_GLU + P)
            for t0, tn, col in ((2, N_GLU - 2, OFF_GLU + 2 * P), (T_RW, N_RW, 0), (T_Q, N_Q, OFF_Q)):
                with sp.Fori(0, tn // 2) as i:
                    for u in range(2):
                        sp.wait_ge(s_mm, 2 * i + t0 + u - 1)
                        sp.dma_start(wbuf[:, u], w_in[:, :, ds((2 * i + u) * P + col, P)]).then_inc(s_w[u], 16)
            sp.wait_ge(s_gc, 1)
            sp.dma_start(io["out_conv_p"][0, 0], last_rows[0:BUF, 0, :]).then_inc(m.sem("outputs_written"), 16)
            for b in range(BS):
                sp.dma_start(io["out_conv_s"][0, b, BUF - TS:BUF, :], last_rows[b * TS:(b + 1) * TS, 1, :])\
                  .then_inc(m.sem("outputs_written"), 16)
            sp.wait_ge(m.sem("outputs_written"), 16 * OUT_PROJECT)

        @block.tensor
        def _(pe):
            with pe.Fori(0, N_PROJ // 2) as i:
                for u in range(2):
                    pe.wait_ge(s_w[u], 16 * i + 16)
                    pe.wait_ge(s_free, 2 * i + u + 1)
                    for k in range(KD):
                        for h in range(2):
                            mm = pe.matmul(m.ps[2 * u + h][:, 0:HALF], wbuf[:, u, k, :],
                                           xT[:, k, h * HALF:(h + 1) * HALF], start=(k == 0), stop=(k == KD - 1))
                    mm.then_inc(s_mm, 1)
            pe.wait_ge(s_glu, 1)
            for j in range(KW):
                pe.transpose(m.ps[4][0:BUF, j * P:(j + 1) * P], ext[:, j, SEQ:SEQ + BUF], m.ident[:, :])
            for j in range(KW):
                last = pe.transpose(m.ps[5][0:BS * TS, j * P:(j + 1) * P], new_glu[:, j, :], m.ident[:, :])
            last.then_inc(s_gt, 1)

        @block.scalar
        def _(act):
            act.sem_inc(s_free, 2)

            def copy_tiles(first, count, func):
                with act.Fori(0, count // 2) as i:
                    for u in range(2):
                        act.wait_ge(s_mm, 2 * i + first + u + 1)
                        act.activation(proj[:, ds(2 * i + first + u, 1), 1:1 + HALF], m.ps[2 * u][:, 0:HALF], func)
                        act.activation(proj[:, ds(2 * i + first + u, 1), 1 + HALF:PW], m.ps[2 * u + 1][:, 0:HALF], func)\
                           .then_inc(s_ev, 1)
                        act.wait_ge(s_ev, 2 * i + first + u + 1)
                        act.sem_inc(s_free, 1)

            copy_tiles(T_GLU, KW, ACT.Copy)
            copy_tiles(T_GLU + KW, KW, ACT.Sigmoid)
            copy_tiles(T_RW, N_RW + N_Q, ACT.Copy)
            act.wait_ge(s_gt, 1)
            act.activation(last_rows[0:BUF, 0, :], m.ps[4][0:BUF, :], ACT.Copy)
            act.activation(last_rows[0:BS * TS, 1, :], m.ps[5][0:BS * TS, :], ACT.Copy).then_inc(s_gc, 1)

        @block.vector
        def _(dve):
            dve.wait_ge(s_ev, N_GLU)
            for j in range(KW):
                a, g = proj[:, T_GLU + j, :], proj[:, T_GLU + KW + j, :]
                dve.tensor_tensor(ext[:, j, BUF:], a[:, 1:1 + SEQ], g[:, 1:1 + SEQ], ALU.mult)
                dve.tensor_tensor(exs[:, j, :, BUF:], sample_cols(a[:, 1 + SEQ:PW]),
                                  sample_cols(g[:, 1 + SEQ:PW]), ALU.mult)
                last = dve.tensor_tensor(new_glu[:, j, :].rearrange("p (b t) -> p b t", b=BS),
                                         sample_cols(a[:, 1 + SEQ:PW]), sample_cols(g[:, 1 + SEQ:PW]), ALU.mult)
            last.then_inc(s_glu, 1)
            dve.memset(conv[:, :, SEQ:NT], 0.0)
            dve.wait_ge(s_glu, 1)
            dve.drain()
            for j in range(KW):
                dve.tensor_scalar(conv[:, j, 0:SEQ], ext[:, j, 0:SEQ], m.taps[:, j:j + 1],
                                  m.vec[:, V_CB + j:V_CB + j + 1], ALU.mult, ALU.add)
                dve.tensor_scalar(sample_cols(conv[:, j, SEQ:NT]), exs[:, j, :, 0:TS], m.taps[:, j:j + 1],
                                  m.vec[:, V_CB + j:V_CB + j + 1], ALU.mult, ALU.add)
            dve.drain()
            with dve.Fori(1, TAPS) as k:
                for j in range(KW):
                    tap = m.taps[:, ds(k * KW + j, 1)]
                    dve.scalar_tensor_tensor(out=conv[:, j, 0:SEQ], in0=ext[:, j, ds(k, SEQ)], scalar=tap,
                                             in1=conv[:, j, 0:SEQ], op0=ALU.mult, op1=ALU.add)
                    dve.scalar_tensor_tensor(out=sample_cols(conv[:, j, SEQ:NT]), in0=exs[:, j, :, ds(k, TS)], scalar=tap,
                                             in1=sample_cols(conv[:, j, SEQ:NT]), op0=ALU.mult, op1=ALU.add)
                dve.drain()
            with dve.Fori(0, N_RW) as j:
                dve.wait_ge(s_ev, j + T_RW + 1)
                tile = proj[:, ds(j + T_RW, 1), :]
                t = tmp.rearrange("p (a n) -> p a n", a=1)
                dve.tensor_tensor(t, tile[:, :, 0:NT], tile[:, :, 1:PW], ALU.subtract)
                dve.drain()
                dve.scalar_tensor_tensor(out=tile[:, :, 1:PW], in0=t, scalar=m.vec[:, ds(j + V_MU, 1)],
                                         in1=tile[:, :, 1:PW], op0=ALU.mult, op1=ALU.add)
                dve.drain()


O_UP = O_PROJ
O_DOWN = O_PROJ + KW * SEQ
O_BEFORE = O_EXT


def stage_prepare(nc, m, io):
    proj = m.at(O_PROJ, N_PROJ, PW)
    rec, key, val = (proj[:, t:t + KW, 1:PW] for t in (T_R, T_K, T_V))
    rate, agate, outg = m.at(O_RATE, KW, NT), m.at(O_AGATE, KW, NT), m.at(O_OUTG, KW, NT)
    kkey, bkey = m.at(O_KKEY, KW, NT), m.at(O_BKEY, KW, NT)
    up, down, before = m.at(O_UP, KW, SEQ), m.at(O_DOWN, KW, SEQ), m.at(O_BEFORE, KW, NT)
    t1 = before
    w_wa, w_g = m.at(O_WBUF, W), m.at(O_WBUF + W, W)
    restart, one_ka = m.at(O_WBUF + 2 * W, SEQ), m.at(O_TMP, KW)
    t2, decay_s = m.at(O_TOP, KW, NT), m.at(O_TOP + KW * NT, KW, NS)
    rows = m.at(O_TOP + KW * NT + KW * NS, 6, W)
    sem = m.sem
    s_w, s_in = sem("lora_weights"), sem("lora_inputs")
    s_mm, s_ev = sem("prepare_product"), sem("prepare_copied")
    halves = [(h * HALF, (h + 1) * HALF) for h in range(2)]

    with nc.Block() as block:
        @block.sync
        def _(sp):
            sp.dma_start(w_wa[0:64, :], io["w_up"][0]).then_inc(s_w, 16)
            sp.dma_start(w_wa[64:128, :], io["a_up"][0]).then_inc(s_w, 16)
            sp.dma_start(w_g, io["g_up"][0]).then_inc(s_w, 16)
            sp.wait_ge(sem("sample_rows_copied"), 6)
            for q in range(6):
                sp.dma_start(io["sample_vectors"][:, :, q, :].rearrange("h r i -> r h i"),
                             rows[0:NS, q, :].rearrange("r (h i) -> r h i", i=HD)).then_inc(sem("sample_vectors_out"), 16)
            sp.wait_ge(sem("sample_vectors_out"), 96)

        @block.tensor
        def _(pe):
            g = 0

            def banks():
                if g >= 4:
                    pe.wait_ge(s_ev, g - 3)
                return [m.ps[2 * (g % 4) + h][:, 0:HALF] for h in range(2)]

            pe.wait_ge(s_w, 48)
            pe.wait_ge(s_in, 1)
            for j in range(KW):
                for w, x, r in ((w_wa, T_WA, slice(0, 64)), (w_wa, T_WA, slice(64, 128)), (w_g, T_G, slice(0, 128))):
                    for out, (a, b) in zip(banks(), halves):
                        mm = pe.matmul(out, w[r, j * P:(j + 1) * P], proj[r, x, 1 + a:1 + b], start=True, stop=True)
                    mm.then_inc(s_mm, 1)
                    g += 1
            for ready, src in (("key_squares", t1), ("bonus_terms", t2)):
                pe.wait_ge(sem(ready), 1)
                for j in range(KW):
                    for out, (a, b) in zip(banks(), halves):
                        mm = pe.matmul(out, m.heads[:, :], src[:, j, a:b], start=True, stop=True)
                    mm.then_inc(s_mm, 1)
                    g += 1
            pe.wait_ge(s_ev, g)
            pe.wait_ge(sem("sample_decay"), 1)
            for q, src in enumerate((rec, None, key, val, kkey, bkey)):
                for j in range(KW):
                    mm = pe.transpose(m.ps[q][0:NS, j * P:(j + 1) * P],
                                      decay_s[:, j, :] if src is None else src[:, j, SEQ:NT], m.ident[:, :])
                mm.then_inc(sem("sample_rows"), 1)

        @block.scalar
        def _(act):
            act.activation(proj[0:64, T_WA, 1:PW], proj[0:64, T_WA, 1:PW], ACT.Tanh)
            act.activation(proj[:, T_G, 1:PW], proj[:, T_G, 1:PW], ACT.Sigmoid).then_inc(s_in, 1)
            g = 0
            for j in range(KW):
                for out, func, vec in ((rate, ACT.Sigmoid, V_W0), (agate, ACT.Sigmoid, V_A0), (outg, ACT.Copy, None)):
                    act.wait_ge(s_mm, g + 1)
                    for h, (a, b) in enumerate(halves):
                        src = m.ps[2 * (g % 4) + h][:, 0:HALF]
                        if vec is None:
                            last = act.activation(out[:, j, a:b], src, func)
                        else:
                            last = act.activation(out[:, j, a:b], src, func, bias=m.vec[:, vec + j:vec + j + 1])
                    last.then_inc(s_ev, 1)
                    g += 1
            act.wait_ge(sem("key_sums"), 1)
            act.activation(t1, t1, ACT.Sqrt).then_inc(sem("key_norms"), 1)
            act.wait_ge(sem("rates_cumulated"), 1)
            act.activation(up, t1[:, :, 0:SEQ], ACT.Exp)
            act.activation(down, t1[:, :, 0:SEQ], ACT.Exp, scale=-1.0)
            act.activation(decay_s, rate[:, :, SEQ:NT], ACT.Exp, scale=-1.0).then_inc(sem("sample_decay"), 1)
            act.wait_ge(sem("rates_before"), 1)
            act.drain()
            act.activation(before[:, :, 0:SEQ], t2[:, :, 0:SEQ], ACT.Exp, scale=-1.0)
            for q in range(6):
                act.wait_ge(sem("sample_rows"), q + 1)
                act.activation(rows[0:NS, q, :], m.ps[q][0:NS, :], ACT.Copy).then_inc(sem("sample_rows_copied"), 1)

        @block.vector
        def _(dve):
            for j in range(KW):
                dve.tensor_scalar(kkey[:, j, :], key[:, j, :], m.vec[:, V_KK + j:V_KK + j + 1], None, ALU.mult)
            dve.tensor_scalar(one_ka, m.vec[:, V_KA:V_KA + KW], -1.0, 1.0, ALU.mult, ALU.add)
            dve.memset(restart, 1.0)
            dve.drain()
            dve.memset(restart[:, 0:SEQ:CH], 0.0)
            dve.tensor_tensor(t1, kkey, kkey, ALU.mult).then_inc(sem("key_squares"), 1)
            dve.wait_ge(s_ev, 12)
            for j in range(KW):
                dve.tensor_scalar(t2[:, j, :], agate[:, j, :], m.vec[:, V_KA + j:V_KA + j + 1], one_ka[:, j:j + 1],
                                  ALU.mult, ALU.add)
            dve.tensor_scalar(rate, rate, RATE, None, ALU.mult)
            dve.drain()
            dve.tensor_tensor(key, key, t2, ALU.mult)
            for j in range(KW):
                dve.wait_ge(s_mm, 13 + j)
                for h, (a, b) in enumerate(halves):
                    last = dve.tensor_scalar(t1[:, j, a:b], m.ps[2 * ((12 + j) % 4) + h][:, 0:HALF], 1e-24, None, ALU.max)
                last.then_inc(s_ev, 1)
            dve.wait_ge(s_ev, 16)
            dve.sem_inc(sem("key_sums"), 1)
            dve.drain()
            dve.tensor_tensor(t2, rec, key, ALU.mult)
            dve.drain()
            for j in range(KW):
                last = dve.tensor_scalar(t2[:, j, :], t2[:, j, :], m.vec[:, V_RK + j:V_RK + j + 1], None, ALU.mult)
            last.then_inc(sem("bonus_terms"), 1)
            dve.wait_ge(sem("key_norms"), 1)
            dve.reciprocal(t1, t1)
            dve.drain()
            dve.tensor_tensor(kkey, kkey, t1, ALU.mult)
            dve.drain()
            dve.tensor_tensor(bkey, kkey, agate, ALU.mult)
            dve.drain()
            for j in range(KW):
                last = dve.tensor_tensor_scan(t1[:, j, 0:SEQ], restart, rate[:, j, 0:SEQ], 0.0, ALU.mult, ALU.add)
            last.then_inc(sem("rates_cumulated"), 1)
            for j in range(KW):
                dve.wait_ge(s_mm, 17 + j)
                for h, (a, b) in enumerate(halves):
                    last = dve.tensor_tensor(agate[:, j, a:b], m.ps[2 * ((16 + j) % 4) + h][:, 0:HALF], val[:, j, a:b],
                                             ALU.mult)
                last.then_inc(s_ev, 1)
            dve.wait_ge(s_ev, 20)
            dve.tensor_tensor(t2[:, :, 0:SEQ], t1[:, :, 0:SEQ], rate[:, :, 0:SEQ], ALU.subtract)\
               .then_inc(sem("rates_before"), 1)


def stage_wkv(nc, m, io):
    proj = m.at(O_PROJ, N_PROJ, PW)
    rec, key, val = (proj[:, t:t + KW, 1:PW] for t in (T_R, T_K, T_V))
    yout = rec
    kkey, bkey = m.at(O_KKEY, KW, NT), m.at(O_BKEY, KW, NT)
    up, down, before = m.at(O_UP, KW, SEQ), m.at(O_DOWN, KW, SEQ), m.at(O_BEFORE, KW, NT)
    o = O_TOP
    bd_qr = [m.at(o + u * 2560, KW, 2, P) for u in range(2)]
    bd_b = [m.at(o + u * 2560 + 1024, KW, P) for u in range(2)]
    bd_k = [m.at(o + u * 2560 + 1536, KW, P) for u in range(2)]
    bd_v = [m.at(o + u * 2560 + 2048, KW, P) for u in range(2)]
    o += 5120
    nr, o = m.at(o, KW, 2, P), o + 1024
    amat, o = m.at(o, KW, P), o + 512
    kr, o = m.at(o, KW, 2, P), o + 1024
    vb, o = m.at(o, KW, 3 * HD), o + 768
    kt, o = m.at(o, KW, P), o + 512
    rinv, o = m.at(o, KW, P), o + 512
    powers, o = [m.at(o + u * 1024, KW, 2, P) for u in range(2)], o + 2048
    rhs, o = m.at(o, KW, HD), o + 256
    sa, o = m.at(o, KW, HD), o + 256
    assert o <= ARENA
    state, sdec = m.at(O_WBUF, KW, HD), m.at(O_WBUF + 256, KW, HD)
    ydiag = m.at(O_WBUF + 512, KW, P)
    sout = m.at(O_WBUF + 1024, KW, P)
    LEVELS = 5
    sem = m.sem
    s_bd, s_v = sem("chunk_vectors"), sem("chunk_values")
    s_gram, s_mask, s_kr, s_vb = sem("gram"), sem("gram_masked"), sem("gram_kr"), sem("tokens_vb")
    s_sq, s_na, s_prod, s_r = sem("squared"), sem("squared_copied"), sem("inverse_product"), sem("inverse_grown")
    s_u, s_un, s_sa, s_sac = sem("rhs_done"), sem("rhs_copied"), sem("sa_done"), sem("sa_copied")
    s_y, s_yd, s_yt, s_yc = sem("y_done"), sem("y_spread"), sem("y_turned"), sem("y_copied")
    s_st, s_sd = sem("state_product"), sem("state_done")

    def a(p):
        return m.ps[p]

    def b(p):
        return m.ps[KW + p]

    def chunks(eng, body):
        with eng.Fori(0, NCH // 2 - 1) as i:
            for u in range(2):
                body(2 * i + u, u, True)
        body(NCH - 2, 0, True)
        body(NCH - 1, 1, False)

    with nc.Block() as block:
        @block.gpsimd
        def _(pool):
            for x in (*bd_qr, *bd_b, *bd_k, *bd_v, ydiag, state):
                pool.memset(x, 0.0)
            pool.drain()
            pool.memset(yout[:, :, SEQ:NT], 0.0).then_inc(sem("wkv_zeroed"), 1)

        @block.tensor
        def _(pe):
            def chunk(n, u, more):
                pe.wait_ge(s_bd, n + 1)
                pe.wait_ge(s_v, n + 1)
                for p in range(KW):
                    pe.wait_ge(s_sd, 4 * n + p + 1)
                    pe.matmul(a(p)[:, 0:256], bd_b[u][:, p, :], bd_qr[u][:, p].rearrange("p q t -> p (q t)"), start=True, stop=True)
                    pe.matmul(a(p)[:, 256:384], bd_qr[u][:, p, 0, :], bd_b[u][:, p, :], start=True, stop=True)
                    pe.transpose(a(p)[:, 384:512], bd_k[u][:, p, :], m.ident[:, :])
                    pe.wait_ge(s_yc, 4 * n + p + 1)
                    pe.matmul(b(p)[:, 0:256], bd_k[u][:, p, :], bd_qr[u][:, p].rearrange("p q t -> p (q t)"), start=True, stop=True)
                    pe.matmul(b(p)[:, 256:320], bd_v[u][:, p, :], m.fold[:, :], start=True, stop=True)
                    pe.transpose(b(p)[:, 320:448], bd_b[u][:, p, :], m.ident[:, :]).then_inc(s_gram, 1)
                for lv in range(LEVELS):
                    at = lv * KW + 1 - KW
                    for p in range(KW):
                        if lv == 0:
                            pe.wait_ge(s_mask, 4 * n + p + 1)
                            nn, aa = nr[:, p, 0, :], amat[:, p, :]
                        else:
                            pe.wait_ge(s_na, 20 * n + at + p)
                            nn, aa = powers[(lv - 1) % 2][:, p, 0, :], powers[(lv - 1) % 2][:, p, 1, :]
                        pe.matmul(a(p)[:, 0:128], aa, nn, start=True, stop=True)
                        pe.matmul(a(p)[:, 128:256], nn, aa, start=True, stop=True).then_inc(s_sq, 1)
                    for p in range(KW):
                        pe.wait_ge(s_na, 20 * n + at + KW + p)
                        if lv == 0:
                            pe.wait_ge(s_vb, 4 * n + p + 1)
                        else:
                            pe.wait_ge(s_r, 20 * n + at + p)
                        pe.matmul(b(p)[:, 0:128], powers[lv % 2][:, p, 1, :], rinv[:, p, :], start=True, stop=True)\
                          .then_inc(s_prod, 1)
                for p in range(KW):
                    pe.matmul(a(p)[:, 0:64], bd_qr[u][:, p, 0, :], state[:, p, :], start=True, stop=False)
                    pe.matmul(a(p)[:, 0:64], kr[:, p, 0, :], vb[:, p, 0:HD], start=False, stop=True).then_inc(s_u, 1)
                for p in range(KW):
                    pe.wait_ge(s_r, 20 * n + KW * (LEVELS - 1) + p + 1)
                    pe.matmul(b(p)[:, 0:64], bd_qr[u][:, p, 1, :], state[:, p, :], start=True, stop=False)
                    pe.matmul(b(p)[:, 0:64], kr[:, p, 1, :], vb[:, p, 0:HD], start=False, stop=False)
                    pe.wait_ge(s_un, 4 * n + p + 1)
                    pe.matmul(a(p)[:, 64:128], rinv[:, p, :], rhs[:, p, :], start=True, stop=True).then_inc(s_sa, 1)
                for p in range(KW):
                    pe.wait_ge(s_sac, 4 * n + p + 1)
                    pe.matmul(b(p)[:, 0:64], nr[:, p, 1, :], sa[:, p, :], start=False, stop=True).then_inc(s_y, 1)
                    pe.matmul(a(p)[:, 128:192], vb[:, p, HD:3 * HD], sa[:, p, :], start=True, stop=False)
                    pe.matmul(a(p)[:, 128:192], kt[:, p, :], vb[:, p, 0:HD], start=False, stop=True).then_inc(s_st, 1)
                for p in range(KW):
                    pe.wait_ge(s_yd, 4 * n + p + 1)
                    pe.matmul(b(p)[:, 64:128], ydiag[:, p, :], m.fold[:, :], start=True, stop=True).then_inc(s_yt, 1)

            pe.wait_ge(sem("wkv_zeroed"), 1)
            chunks(pe, chunk)
            pe.wait_ge(s_sd, 4 * NCH + 4)
            for p in range(KW):
                last = pe.transpose(m.ps[0][0:HD, p * P:(p + 1) * P], state[:, p, :], m.ident[:, :])
            last.then_inc(sem("state_turned"), 1)

        @block.scalar
        def _(act):
            def values(n, u):
                for h in range(2):
                    r = slice(h * HD, (h + 1) * HD)
                    last = act.activation(bd_v[u][r, :, r], val[r, :, ds(n * CH, CH)], ACT.Copy)
                last.then_inc(s_v, 1)

            def chunk(n, u, more):
                if more:
                    values(n + 1, 1 - u)
                for p in range(KW):
                    act.wait_ge(s_kr, 4 * n + p + 1)
                    act.activation(vb[:, p, :], b(p)[:, 256:448], ACT.Copy).then_inc(s_vb, 1)
                for lv in range(LEVELS):
                    for p in range(KW):
                        act.wait_ge(s_sq, 20 * n + KW * lv + p + 1)
                        act.activation(powers[lv % 2][:, p].rearrange("p q t -> p (q t)"), a(p)[:, 0:256], ACT.Copy)\
                           .then_inc(s_na, 1)
                for p in range(KW):
                    act.wait_ge(s_u, 4 * n + p + 1)
                    act.activation(rhs[:, p, :], a(p)[:, 0:64], ACT.Copy, scale=-1.0).then_inc(s_un, 1)
                for p in range(KW):
                    act.wait_ge(s_sa, 4 * n + p + 1)
                    act.activation(sa[:, p, :], a(p)[:, 64:128], ACT.Copy).then_inc(s_sac, 1)
                for p in range(KW):
                    act.wait_ge(s_y, 4 * n + p + 1)
                    act.activation(ydiag[0:HD, p, 0:HD], b(p)[0:HD, 0:64], ACT.Copy)
                    act.activation(ydiag[HD:P, p, HD:P], b(p)[HD:P, 0:64], ACT.Copy).then_inc(s_yd, 1)
                for p in range(KW):
                    act.wait_ge(s_yt, 4 * n + p + 1)
                    act.activation(yout[:, p, ds(n * CH, CH)], b(p)[:, 64:128], ACT.Copy).then_inc(s_yc, 1)

            act.sem_inc(s_yc, 4)
            act.wait_ge(sem("wkv_zeroed"), 1)
            values(0, 0)
            chunks(act, chunk)
            act.wait_ge(sem("state_turned"), 1)
            act.activation(sout[0:HD].rearrange("p a b -> p (a b)"), m.ps[0][0:HD, :], ACT.Copy).then_inc(sem("state_rows"), 1)
            act.wait_ge(sem("state_rows"), 1)
            act.dma_start(io["out_wkv_p"][0, 0].rearrange("h v k -> v h k"),
                          sout[0:HD].rearrange("p a (b k) -> p (a b) k", k=HD)).then_inc(sem("outputs_written"), 16)
            act.wait_ge(sem("outputs_written"), 16 * OUT_WKV)

        @block.vector
        def _(dve):
            def vectors(n, u):
                cols = ds(n * CH, CH)
                for h in range(2):
                    r = slice(h * HD, (h + 1) * HD)
                    dve.tensor_tensor(bd_b[u][r, :, r], bkey[r, :, cols], up[r, :, cols], ALU.mult)
                    dve.tensor_tensor(bd_k[u][r, :, r], key[r, :, cols], up[r, :, cols], ALU.mult)
                    dve.tensor_tensor(bd_qr[u][r, :, 0, r], kkey[r, :, cols], before[r, :, cols], ALU.mult)
                    last = dve.tensor_tensor(bd_qr[u][r, :, 1, r], rec[r, :, cols], down[r, :, cols], ALU.mult)
                last.then_inc(s_bd, 1)

            def chunk(n, u, more):
                for p in range(KW):
                    dve.wait_ge(s_gram, 4 * n + p + 1)
                    dve.tensor_tensor(nr[:, p], a(p)[:, 0:256].rearrange("p (q t) -> p q t", q=2), m.upper[:], ALU.mult)
                    dve.tensor_tensor(amat[:, p, :], a(p)[:, 256:384], m.lower[:], ALU.mult)
                    dve.tensor_copy(kt[:, p, :], a(p)[:, 384:512])
                    dve.drain()
                    dve.tensor_tensor(rinv[:, p, :], m.ident[:], nr[:, p, 0, :], ALU.subtract).then_inc(s_mask, 1)
                    dve.tensor_tensor(kr[:, p], b(p)[:, 0:256].rearrange("p (q t) -> p q t", q=2), m.upper[:], ALU.mult)\
                       .then_inc(s_kr, 1)
                if more:
                    vectors(n + 1, 1 - u)
                for lv in range(LEVELS):
                    for p in range(KW):
                        dve.wait_ge(s_prod, 20 * n + KW * lv + p + 1)
                        dve.tensor_tensor(rinv[:, p, :], b(p)[:, 0:128], rinv[:, p, :], ALU.add).then_inc(s_r, 1)
                for p in range(KW):
                    dve.tensor_scalar(sdec[:, p, :], state[:, p, :], down[:, p, ds(n * CH + CH - 1, 1)], None, ALU.mult)
                dve.drain()
                for p in range(KW):
                    dve.wait_ge(s_st, 4 * n + p + 1)
                    dve.scalar_tensor_tensor(out=state[:, p, :], in0=a(p)[:, 128:192],
                                             scalar=down[:, p, ds(n * CH + CH - 1, 1)],
                                             in1=sdec[:, p, :], op0=ALU.mult, op1=ALU.add).then_inc(s_sd, 1)

            dve.sem_inc(s_sd, 4)
            dve.wait_ge(sem("wkv_zeroed"), 1)
            vectors(0, 0)
            chunks(dve, chunk)


WKV_ONLY = ("chunk_vectors", "chunk_values", "gram", "gram_masked", "gram_kr", "tokens_vb", "squared", "squared_copied",
            "inverse_product", "inverse_grown", "rhs_done", "rhs_copied", "sa_done", "sa_copied", "y_done", "y_spread",
            "y_turned", "y_copied", "state_product", "state_done", "state_turned", "state_rows", "wkv_zeroed")


O_ATT = O_RATE


def stage_attend(nc, m, io):
    xT, proj = m.at(O_XT, KD, NT), m.at(O_PROJ, N_PROJ, PW)
    q = proj[:, T_Q:T_Q + MH, 1:PW]
    yv = proj[:, T_R:T_R + KW, 1:PW]
    att, conv = m.at(O_ATT, MH, NT), m.at(O_CONV, KW, NT)
    bonus, outg = m.at(O_AGATE, KW, NT), m.at(O_OUTG, KW, NT)
    vcache = m.at(O_TOP, BS, MT, W)
    kcache = [m.at(O_TOP + 8192 + u * 1024, MT, W) for u in range(2)]
    kcT = [m.at(O_TOP + 10240 + u * 1024, MH, NM) for u in range(2)]
    o = O_PROJ + T_K * PW
    memrow, memT = m.at(o, MT, D), m.at(o + MT * D, KD, NM)
    kvrow = m.at(o, MT, 2 * W)
    assert T_K * PW + 2 * MT * D <= T_Q * PW
    wkv = [m.at(O_PROJ + u * 2048, 4, W) for u in range(2)]
    o = O_KKEY
    kT, o = m.at(o, MH, NM), o + 1024
    probs, o = m.at(o, 4, NM), o + 1024
    probsT, o = m.at(o, MT, SEQ), o + 1024
    sT, o = m.at(o, MT, P), o + 256
    sprob, o = m.at(o, NM), o + 256
    sprobT, o = m.at(o, MT, P), o + 256
    assert o <= O_BKEY + KW * NT
    o = O_EXT
    sv, o = m.at(o, TS, 6, HD), o + 1536
    vh, o = m.at(o, TS, HD // 2), o + 128
    sy, o = m.at(o, TS, HD // 2), o + 128
    syrow, o = m.at(o, W), o + 512
    ssa, o = m.at(o, HD // 2), o + 32
    stats, o = m.at(o, 24), o + 24
    assert o <= O_CONV
    st = m.at(O_WBUF, HD // 2, HD)
    stmp = m.at(O_KKEY + 3840, 8, HD)
    t1 = m.at(O_EXT, KW, NT)
    SCALE = float(P) ** -0.5
    sem = m.sem
    R32 = HD // 2

    with nc.Block() as block:
        @block.sync
        def _(sp):
            for t in range(MT):
                sp.dma_start(memrow[:, t, :], io["mem_prompt"][0, t * P:(t + 1) * P, :]).then_inc(sem("mem_loaded"), 16)
            w = io["w_mem_kv"][0].rearrange("(k p) n -> p k n", p=P)
            n = 0
            for half in range(2):
                for kk in range(2):
                    if n >= 2:
                        sp.wait_ge(sem("mem_weights_used"), n - 1)
                    sp.dma_start(wkv[n % 2], w[:, 4 * kk:4 * kk + 4, half * W:(half + 1) * W])\
                      .then_inc(sem(f"mem_weights_{n % 2}"), 16)
                    n += 1
            kc = io["cache_mem_k"][0].rearrange("b (t p) h d -> b p t (h d)", p=P)
            vc = io["cache_mem_v"][0].rearrange("b (t p) h d -> b p t (h d)", p=P)
            for b in range(BS):
                if b >= 2:
                    sp.wait_ge(sem("key_cache_turned"), b - 1)
                sp.dma_start(kcache[b % 2], kc[b]).then_inc(sem(f"key_cache_{b % 2}"), 16)
                sp.dma_start(vcache[:, b], vc[b]).then_inc(sem("value_cache"), 16)
            sp.wait_ge(sem("mem_rows_copied"), 4)
            for t in range(MT):
                sp.dma_start(io["out_mk"][0, 0, t * P:(t + 1) * P].rearrange("m h d -> m (h d)"), kvrow[:, t, 0:W])\
                  .then_inc(sem("outputs_written"), 16)
                sp.dma_start(io["out_mv"][0, 0, t * P:(t + 1) * P].rearrange("m h d -> m (h d)"), kvrow[:, t, W:2 * W])\
                  .then_inc(sem("outputs_written"), 16)
            sp.wait_ge(sem("outputs_written"), 16 * OUT_ATTEND)

        @block.gpsimd
        def _(pool):
            sv_dram = io["sample_vectors"].rearrange("h (b s) q i -> (h b) (s q i)", s=SB)
            for v in range(2):
                pool.dma_start(sv[64 * v:64 * v + 64].rearrange("p t q i -> p (t q i)"), sv_dram[:, 6 * HD:])\
                    .then_inc(sem("sample_in"), 16)
                for h in range(8):
                    pool.dma_start(st[64 * v + 8 * h:64 * v + 8 * h + 8].rearrange("p a b -> p (a b)"),
                                   io["state_wkv"][0, :, h, v * R32:(v + 1) * R32, :].rearrange("b v k -> b (v k)"))\
                        .then_inc(sem("sample_in"), 16)
            pool.wait_ge(sem("sample_done"), 1)
            pool.dma_start(io["sample_y"].rearrange("v h b t i -> (v h b) (t i)"), sy.rearrange("p t i -> p (t i)"))\
                .then_inc(sem("sample_y_out"), 16)
            for v in range(2):
                for h in range(8):
                    pool.dma_start(io["out_wkv_s"][0, :, h, v * R32:(v + 1) * R32, :].rearrange("b v k -> b (v k)"),
                                   st[64 * v + 8 * h:64 * v + 8 * h + 8].rearrange("p a b -> p (a b)"))\
                        .then_inc(sem("sample_states_out"), 16)
            pool.wait_ge(sem("sample_y_out"), 16)
            for v in range(2):
                pool.dma_start(syrow[0:BS * TS].rearrange("p (h v i) -> p h v i", h=8, v=2)[:, :, v, :],
                               io["sample_y"][v].rearrange("h b t i -> (b t) h i")).then_inc(sem("sample_y_rows"), 16)
            pool.wait_ge(sem("sample_states_out"), 16 * 16)

        @block.tensor
        def _(pe):
            pe.wait_ge(sem("mem_loaded"), 32)
            for g in range(4):
                for k in range(4):
                    c = 4 * (g % 2) + k
                    mm = pe.transpose(m.ps[g][:, k * P:(k + 1) * P], memrow[:, g // 2, c * P:(c + 1) * P], m.ident[:, :])
                mm.then_inc(sem("mem_turned"), 1)
            pe.wait_ge(sem("memT_ready"), 4)
            n = 0
            for half in range(2):
                for kk in range(2):
                    pe.wait_ge(sem(f"mem_weights_{n % 2}"), 16 * (n // 2 + 1))
                    for t in range(MT):
                        for k in range(4):
                            mm = pe.matmul(m.ps[4 + 2 * half + t][:, :], memT[:, 4 * kk + k, t * P:(t + 1) * P],
                                           wkv[n % 2][:, k, :], start=(kk == 0 and k == 0), stop=(kk == 1 and k == 3))
                    mm.then_inc(sem("mem_weights_used"), 1)
                    n += 1
            pe.wait_ge(sem("mem_rows_copied"), 4)
            for h in range(MH):
                for t in range(MT):
                    mm = pe.transpose(m.ps[h // 2][:, (h % 2) * NM + t * P:(h % 2) * NM + (t + 1) * P],
                                      kvrow[:, t, h * P:(h + 1) * P], m.ident[:, :])
            mm.then_inc(sem("kT_turned"), 1)
            pe.wait_ge(sem("kT_ready"), 2)

            def scores(h):
                if h >= 1:
                    pe.wait_ge(sem("scores_read"), h)
                for i in range(4):
                    mm = pe.matmul(m.ps[2 + i // 2][:, (i % 2) * NM:(i % 2 + 1) * NM], q[:, h, i * P:(i + 1) * P],
                                   kT[:, h, :], start=True, stop=True)
                mm.then_inc(sem("scores_done"), 1)

            def turn_probs(h):
                pe.wait_ge(sem("probs_ready"), h + 1)
                if h >= 1:
                    pe.wait_ge(sem("probsT_ready"), 2 * h)
                for t in range(MT):
                    for i in range(4):
                        mm = pe.transpose(m.ps[4 + t][:, i * P:(i + 1) * P], probs[:, i, t * P:(t + 1) * P], m.ident[:, :])
                mm.then_inc(sem("probs_turned"), 1)

            def mix_values(h):
                pe.wait_ge(sem("probsT_ready"), 2 * h + 2)
                if h >= 1:
                    pe.wait_ge(sem("att_copied"), h)
                for t in range(MT):
                    mm = pe.matmul(m.ps[6][:, :], kvrow[:, t, W + h * P:W + (h + 1) * P], probsT[:, t, :],
                                   start=(t == 0), stop=(t == MT - 1))
                mm.then_inc(sem("att_done"), 1)

            def sample_scores(b):
                pe.wait_ge(sem(f"key_cache_{b % 2}"), 16 * (b // 2 + 1))
                if b >= 1:
                    pe.wait_ge(sem("key_cacheT_ready"), 2 * b)
                for h in range(MH):
                    for t in range(MT):
                        mm = pe.transpose(m.ps[h // 2][:, (h % 2) * NM + t * P:(h % 2) * NM + (t + 1) * P],
                                          kcache[b % 2][:, t, h * P:(h + 1) * P], m.ident[:, :])
                mm.then_inc(sem("key_cache_turned"), 1)
                pe.wait_ge(sem("key_cacheT_ready"), 2 * b + 2)
                for h in range(MH):
                    for t in range(MT):
                        at = t * P + (b * MH + h) * TS
                        mm = pe.matmul(m.ps[7][:, at:at + TS], kcT[b % 2][:, h, t * P:(t + 1) * P],
                                       q[:, h, SEQ + SB * b + 1:SEQ + SB * b + SB], start=True, stop=True)
                if b == BS - 1:
                    mm.then_inc(sem("sample_scores"), 1)

            for h in range(MH):
                scores(h)
                sample_scores(2 * h)
                turn_probs(h)
                sample_scores(2 * h + 1)
                mix_values(h)
            pe.wait_ge(sem("sT_ready"), 1)
            pe.wait_ge(sem("scores_read"), MH)
            for t in range(MT):
                mm = pe.transpose(m.ps[2][:, t * P:(t + 1) * P], sT[:, t, :], m.ident[:, :])
            mm.then_inc(sem("sample_scores_turned"), 1)
            pe.wait_ge(sem("sprob_ready"), 1)
            for t in range(MT):
                mm = pe.transpose(m.ps[3][:, t * P:(t + 1) * P], sprob[:, t * P:(t + 1) * P], m.ident[:, :])
            mm.then_inc(sem("sprob_turned"), 1)
            pe.wait_ge(sem("sprobT_ready"), 1)
            pe.wait_ge(sem("value_cache"), 16 * BS)
            for b in range(BS):
                for h in range(MH):
                    at = (b * MH + h) * TS
                    for t in range(MT):
                        mm = pe.matmul(m.ps[7][:, at:at + TS], vcache[:, b, t, h * P:(h + 1) * P],
                                       sprobT[:, t, at:at + TS], start=(t == 0), stop=(t == MT - 1))
            mm.then_inc(sem("sample_att"), 1)
            pe.wait_ge(sem("sample_y_rows"), 32)
            for j in range(KW):
                mm = pe.transpose(m.ps[0][:, j * 32:(j + 1) * 32], syrow[0:32, j * P:(j + 1) * P], m.ident[0:32, 0:32])
            mm.then_inc(sem("sample_y_turned"), 1)
            pe.wait_ge(sem("sample_att_copied"), 1)
            for r, (name, src, mask) in enumerate((("y_whole", yv, m.heads), ("conv_whole", conv, m.ones),
                                                   ("y_squares", None, m.heads), ("conv_squares", None, m.ones))):
                pe.wait_ge(sem(name), 1)
                x = t1 if src is None else src
                for j in range(KW):
                    for h in range(2):
                        if mask is m.heads:
                            mm = pe.matmul(m.ps[2 * j + h][:, 0:HALF], mask[:, :], x[:, j, h * HALF:(h + 1) * HALF],
                                           start=True, stop=True)
                        else:
                            mm = pe.matmul(m.ps[h][:, 0:HALF], mask[:, :], x[:, j, h * HALF:(h + 1) * HALF],
                                           start=(j == 0), stop=(j == KW - 1))
                mm.then_inc(sem("norm_sums"), 1)

        @block.scalar
        def _(act):
            for g in range(4):
                act.wait_ge(sem("mem_turned"), g + 1)
                act.activation(memT[:, 4 * (g % 2):4 * (g % 2) + 4, (g // 2) * P:(g // 2 + 1) * P],
                               m.ps[g][:, :].rearrange("p (k n) -> p k n", k=4), ACT.Copy).then_inc(sem("memT_ready"), 1)
            for half in range(2):
                act.wait_ge(sem("mem_weights_used"), 2 * half + 2)
                for t in range(MT):
                    act.activation(kvrow[:, t, half * W:(half + 1) * W], m.ps[4 + 2 * half + t][:, :], ACT.Copy)\
                       .then_inc(sem("mem_rows_copied"), 1)
            act.wait_ge(sem("kT_turned"), 1)
            for g in range(2):
                act.activation(kT[:, 2 * g:2 * g + 2, :], m.ps[g][:, :].rearrange("p (k n) -> p k n", k=2), ACT.Copy)\
                   .then_inc(sem("kT_ready"), 1)

            def key_cacheT(b):
                act.wait_ge(sem("key_cache_turned"), b + 1)
                for g in range(2):
                    act.activation(kcT[b % 2][:, 2 * g:2 * g + 2, :], m.ps[g][:, :].rearrange("p (k n) -> p k n", k=2),
                                   ACT.Copy).then_inc(sem("key_cacheT_ready"), 1)

            for h in range(MH):
                key_cacheT(2 * h)
                act.wait_ge(sem("maxima"), h + 1)
                for i in range(4):
                    last = act.activation(probs[:, i, :], m.ps[2 + i // 2][:, (i % 2) * NM:(i % 2 + 1) * NM], ACT.Exp,
                                          bias=stats[:, i:i + 1], scale=SCALE, accum_out=stats[:, 8 + i:9 + i])
                last.then_inc(sem("scores_read"), 1)
                key_cacheT(2 * h + 1)
                act.wait_ge(sem("probs_turned"), h + 1)
                for t in range(MT):
                    act.activation(probsT[:, t, :], m.ps[4 + t][:, :], ACT.Copy).then_inc(sem("probsT_ready"), 1)
                act.wait_ge(sem("att_done"), h + 1)
                act.activation(att[:, h, 0:SEQ], m.ps[6][:, :], ACT.Copy).then_inc(sem("att_copied"), 1)
            act.wait_ge(sem("sample_scores"), 1)
            act.activation(sT, m.ps[7][:, 0:NM].rearrange("p (t n) -> p t n", t=MT), ACT.Copy).then_inc(sem("sT_ready"), 1)
            act.wait_ge(sem("sample_maxima"), 1)
            act.activation(sprob, m.ps[2][:, 0:NM], ACT.Exp, bias=stats[:, 16:17], scale=SCALE, accum_out=stats[:, 17:18])\
               .then_inc(sem("sprob_raw"), 1)
            act.wait_ge(sem("sprob_turned"), 1)
            act.activation(sprobT, m.ps[3][:, 0:NM].rearrange("p (t n) -> p t n", t=MT), ACT.Copy)\
               .then_inc(sem("sprobT_ready"), 1)
            act.wait_ge(sem("sample_att"), 1)
            for h in range(MH):
                last = act.activation(sample_cols(att[:, h, SEQ:NT]),
                                      m.ps[7][:, 0:P].rearrange("p (b h t) -> p h b t", b=BS, h=MH)[:, h], ACT.Copy)
            last.then_inc(sem("sample_att_copied"), 1)
            act.wait_ge(sem("y_variance"), 1)
            act.activation(t1, t1, ACT.Sqrt).then_inc(sem("y_deviation"), 1)
            act.wait_ge(sem("conv_variance"), 1)
            act.activation(t1[:, 0, :], t1[:, 0, :], ACT.Sqrt).then_inc(sem("conv_deviation"), 1)
            act.wait_ge(sem("conv_normed"), 1)
            for j in range(KW):
                act.activation(conv[:, j, :], conv[:, j, :], ACT.Silu, scale=m.vec[:, V_CG + j:V_CG + j + 1],
                               bias=m.vec[:, V_CBB + j:V_CBB + j + 1])

        @block.vector
        def _(dve):
            def softmax_head(h):
                dve.wait_ge(sem("scores_done"), h + 1)
                for g in range(2):
                    dve.tensor_reduce(stats[:, 4 + 2 * g:6 + 2 * g], m.ps[2 + g][:, :].rearrange("p (k n) -> p k n", k=2),
                                      AX.X, ALU.max)
                dve.drain()
                if h >= 1:
                    dve.wait_ge(sem("probs_turned"), h)
                dve.tensor_scalar(stats[:, 0:4], stats[:, 4:8], -SCALE, None, ALU.mult).then_inc(sem("maxima"), 1)

            def normalise_head(h):
                dve.wait_ge(sem("scores_read"), h + 1)
                dve.reciprocal(stats[:, 12:16], stats[:, 8:12])
                dve.drain()
                for i in range(4):
                    last = dve.tensor_scalar(probs[:, i, :], probs[:, i, :], stats[:, 12 + i:13 + i], None, ALU.mult)
                last.then_inc(sem("probs_ready"), 1)

            def sample_step(t):
                def bk(q_):
                    return sv[:, t, q_:q_ + 1, :].to_broadcast([P, 8, HD])

                for g in range(4):
                    rows = slice(8 * g, 8 * g + 8)
                    s = st[:, rows, :]

                    def bv(x):
                        return x.rearrange("p (v o) -> p v o", o=1).to_broadcast([P, 8, HD])

                    dve.tensor_tensor(stmp, s, bk(4), ALU.mult)
                    dve.drain()
                    dve.tensor_reduce(ssa[:, rows], stmp, AX.X, ALU.add)
                    dve.tensor_tensor(s, s, bk(1), ALU.mult)
                    dve.drain()
                    dve.tensor_tensor(stmp, bk(5), bv(ssa[:, rows]), ALU.mult)
                    dve.drain()
                    dve.tensor_tensor(s, s, stmp, ALU.subtract)
                    dve.drain()
                    dve.tensor_tensor(stmp, bk(2), bv(vh[:, t, rows]), ALU.mult)
                    dve.drain()
                    dve.tensor_tensor(s, s, stmp, ALU.add)
                    dve.drain()
                    dve.tensor_tensor(stmp, s, bk(0), ALU.mult)
                    dve.drain()
                    last = dve.tensor_reduce(sy[:, t, rows], stmp, AX.X, ALU.add)
                    dve.drain()
                return last

            dve.memset(att[:, :, SEQ:NT], 0.0)
            dve.wait_ge(sem("sample_in"), 16 * 18)
            for v in range(2):
                dve.tensor_copy(vh[64 * v:64 * v + 64], sv[64 * v:64 * v + 64, :, 3, v * R32:(v + 1) * R32])
            dve.drain()
            for h in range(MH):
                if h == 0:
                    sample_step(0)
                    sample_step(1)
                softmax_head(h)
                normalise_head(h)
                if h == 0:
                    sample_step(2)
                if h == 1:
                    sample_step(3)
                    dve.drain()
                    dve.sem_inc(sem("sample_done"), 1)
            dve.wait_ge(sem("sample_scores_turned"), 1)
            dve.tensor_reduce(stats[:, 18:19], m.ps[2][:, 0:NM], AX.X, ALU.max)
            dve.drain()
            dve.tensor_scalar(stats[:, 16:17], stats[:, 18:19], -SCALE, None, ALU.mult).then_inc(sem("sample_maxima"), 1)
            dve.wait_ge(sem("sprob_raw"), 1)
            dve.reciprocal(stats[:, 19:20], stats[:, 17:18])
            dve.drain()
            dve.tensor_scalar(sprob, sprob, stats[:, 19:20], None, ALU.mult).then_inc(sem("sprob_ready"), 1)
            dve.wait_ge(sem("sample_y_turned"), 1)
            for j in range(KW):
                last = dve.tensor_copy(sample_cols(yv[:, j, SEQ:NT]),
                                       m.ps[0][:, j * 32:(j + 1) * 32].rearrange("p (b t) -> p b t", b=BS))
            last.then_inc(sem("y_whole"), 1)
            dve.wait_ge(sem("norm_sums"), 1)
            for j in range(KW):
                for h in range(2):
                    a, b = h * HALF, (h + 1) * HALF
                    last = dve.scalar_tensor_tensor(out=yv[:, j, a:b], in0=m.ps[2 * j + h][:, 0:HALF], scalar=-1.0 / HD,
                                                    in1=yv[:, j, a:b], op0=ALU.mult, op1=ALU.add)
            last.then_inc(sem("conv_whole"), 1)
            dve.drain()
            dve.tensor_tensor(t1, yv, yv, ALU.mult)
            dve.wait_ge(sem("norm_sums"), 2)
            for j in range(KW):
                for h in range(2):
                    a, b = h * HALF, (h + 1) * HALF
                    last = dve.scalar_tensor_tensor(out=conv[:, j, a:b], in0=m.ps[h][:, 0:HALF], scalar=-1.0 / W,
                                                    in1=conv[:, j, a:b], op0=ALU.mult, op1=ALU.add)
            last.then_inc(sem("y_squares"), 1)
            dve.wait_ge(sem("norm_sums"), 3)
            for j in range(KW):
                for h in range(2):
                    last = dve.tensor_scalar(t1[:, j, h * HALF:(h + 1) * HALF], m.ps[2 * j + h][:, 0:HALF], 1.0 / HD, GN_EPS,
                                             ALU.mult, ALU.add)
            last.then_inc(sem("y_variance"), 1)
            dve.wait_ge(sem("y_deviation"), 1)
            dve.reciprocal(t1, t1)
            dve.drain()
            dve.tensor_tensor(yv, yv, t1, ALU.mult)
            dve.drain()
            dve.tensor_tensor(t1, conv, conv, ALU.mult).then_inc(sem("conv_squares"), 1)
            for j in range(KW):
                dve.tensor_scalar(yv[:, j, :], yv[:, j, :], m.vec[:, V_LG + j:V_LG + j + 1],
                                  m.vec[:, V_LB + j:V_LB + j + 1], ALU.mult, ALU.add)
            dve.drain()
            dve.tensor_tensor(yv, yv, bonus, ALU.add)
            dve.drain()
            dve.tensor_tensor(yv, yv, outg, ALU.mult)
            dve.wait_ge(sem("norm_sums"), 4)
            for h in range(2):
                last = dve.tensor_scalar(t1[:, 0, h * HALF:(h + 1) * HALF], m.ps[h][:, 0:HALF], 1.0 / W, LN_EPS,
                                         ALU.mult, ALU.add)
            last.then_inc(sem("conv_variance"), 1)
            dve.wait_ge(sem("conv_deviation"), 1)
            dve.reciprocal(t1[:, 0, :], t1[:, 0, :])
            dve.drain()
            for j in range(KW):
                last = dve.tensor_tensor(conv[:, j, :], conv[:, j, :], t1[:, 0, :], ALU.mult)
            last.then_inc(sem("conv_normed"), 1)


O_GW = O_AGATE
O_OW = O_GW + 3 * D
O_GATE = O_OW + 3 * W
O_GTMP = O_GATE + 2 * NT
O_MERGED = O_GTMP + NT
assert O_MERGED + KD * NT <= O_CONV


def prefetch_expert(sp, m, io, e, buf, at, sem):
    w = m.at(at, 3, 2 * D)
    for x, name in enumerate(("w_e1", "w_e3", "w_e2")):
        c = KD if x < 2 else 2
        src = io[name][0][ds(e, 1)].rearrange("e (p c) n -> p (e c n)", c=c)
        sp.dma_start(w[:, x, :], src).then_inc(sem(f"expert_weights_{buf}"), 16)


def stage_merge(nc, m, io):
    xT, proj = m.at(O_XT, KD, NT), m.at(O_PROJ, N_PROJ, PW)
    branch = [proj[:, T_R:T_R + KW, 1:PW], m.at(O_CONV, KW, NT), m.at(O_ATT, KW, NT)]
    gw = [m.at(O_GW + b * D, KD, P) for b in range(3)]
    ow = [m.at(O_OW + b * W, KW, P) for b in range(3)]
    gate, gtmp = m.at(O_GATE, 2, NT), m.at(O_GTMP, NT)
    merged = m.at(O_MERGED, KD, NT)
    w_in = io["w_in"][0].rearrange("(k p) n -> p k n", p=P)
    w_o = [io[n][0].rearrange("(k p) n -> p k n", p=P) for n in ("w_o_a", "w_o_b", "w_o_c")]
    sem = m.sem
    s_g, s_o = sem("gate_product"), sem("branch_product")
    s_sig, s_free, s_m = sem("gates_ready"), sem("merge_banks_free"), sem("branch_merged")

    with nc.Block() as block:
        @block.sync
        def _(sp):
            def load(j, b):
                sp.dma_start(gw[b], w_in[:, :, ds(j * P + OFF_GATE + b * D, P)]).then_inc(sem(f"branch_weights_{b}"), 16)
                sp.dma_start(ow[b], w_o[b][:, :, ds(j * P, P)]).then_inc(sem(f"branch_weights_{b}"), 16)

            for b in range(3):
                load(0, b)
            with sp.Fori(1, KD) as j:
                for b in range(3):
                    sp.wait_ge(s_o, 3 * j + b - 2)
                    load(j, b)
            for e in range(2):
                prefetch_expert(sp, m, io, e, e, O_TOP + e * WEXP, sem)

        @block.tensor
        def _(pe):
            with pe.Fori(0, KD // 2) as i:
                for step in range(6):
                    u, b = divmod(step, 3)
                    bank = 4 * (step % 2)
                    pe.wait_ge(sem(f"branch_weights_{b}"), 64 * i + 32 * u + 32)
                    pe.wait_ge(s_free, 6 * i + step + 1)
                    for k in range(KD):
                        for h in range(2):
                            mm = pe.matmul(m.ps[bank + h][:, 0:HALF], gw[b][:, k, :], xT[:, k, h * HALF:(h + 1) * HALF],
                                           start=(k == 0), stop=(k == KD - 1))
                    mm.then_inc(s_g, 1)
                    for k in range(KW):
                        for h in range(2):
                            mm = pe.matmul(m.ps[bank + 2 + h][:, 0:HALF], ow[b][:, k, :],
                                           branch[b][:, k, h * HALF:(h + 1) * HALF], start=(k == 0), stop=(k == KW - 1))
                    mm.then_inc(s_o, 1)

        @block.scalar
        def _(act):
            with act.Fori(0, KD // 2) as i:
                for step in range(6):
                    bank = 4 * (step % 2)
                    act.wait_ge(s_g, 6 * i + step + 1)
                    act.wait_ge(s_free, 6 * i + step + 1)
                    for h in range(2):
                        last = act.activation(gate[:, step % 2, h * HALF:(h + 1) * HALF], m.ps[bank + h][:, 0:HALF], ACT.Sigmoid)
                    last.then_inc(s_sig, 1)

        @block.vector
        def _(dve):
            dve.sem_inc(s_free, 2)
            with dve.Fori(0, KD // 2) as i:
                for step in range(6):
                    u, b = divmod(step, 3)
                    bank = 4 * (step % 2)
                    dst = merged[:, ds(2 * i + u, 1), :].rearrange("p a n -> p (a n)")
                    dve.wait_ge(s_sig, 6 * i + step + 1)
                    dve.wait_ge(s_o, 6 * i + step + 1)
                    for h in range(2):
                        cols = slice(h * HALF, (h + 1) * HALF)
                        last = dve.tensor_tensor(dst[:, cols] if b == 0 else gtmp[:, cols], m.ps[bank + 2 + h][:, 0:HALF],
                                                 gate[:, step % 2, cols], ALU.mult)
                    last.then_inc(s_m, 1)
                    dve.wait_ge(s_m, 6 * i + step + 1)
                    dve.sem_inc(s_free, 1)
                    if b:
                        dve.tensor_tensor(dst, dst, gtmp, ALU.add)
                        dve.drain()


O_WOUT = O_PROJ
O_ROWS = O_WOUT + 8 * D
O_LNZ = O_ROWS + 2 * D
O_LNP = O_LNZ + 2 * D
assert O_LNP + 2 * D <= O_RATE
O_JUNK = O_RATE
O_W2S = O_RATE + D
O_WR = O_W2S + 2 * D
O_BR = O_WR + D
O_MSTAT = O_BR + NE
assert O_MSTAT + 64 <= O_MERGED
O_HT = O_MERGED + KD * NT
O_WS = O_XT
assert O_HT + KD * NT <= O_TOP
O_SCORE = O_MSTAT + 64
assert O_SCORE >= 2 * WEXP and O_SCORE + NTT * NE <= O_MERGED


def stage_mix(nc, m, io):
    merged, hT = m.at(O_MERGED, KD, NT), m.at(O_HT, KD, NT)
    wout, xr, z = m.at(O_WOUT, KD, D), m.at(O_ROWS, 2, D), m.at(O_LNZ, 2, D)
    lnp, junk, w2s, wr = m.at(O_LNP, 2, D), m.at(O_JUNK, D), m.at(O_W2S, 2, D), m.at(O_WR, KD, NE)
    ws = m.at(O_WS, 2, KD, DE)
    sact = m.at(O_MERGED, 2, NT)
    ssil = m.at(O_MERGED + 2 * NT, 2, NT)
    stats, score = m.at(O_MSTAT, NTT, 8), m.at(O_SCORE, NTT, NE)
    sem = m.sem
    s_z, s_mean, s_sq = sem("z_product"), sem("z_mean"), sem("z_squares")
    s_var, s_dev, s_h, s_zf = sem("z_variance"), sem("z_deviation"), sem("h_rows_ready"), sem("z_banks_read")
    s_ht, s_hc, s_rt, s_rc = sem("h_turned"), sem("h_turned_copied"), sem("router_done"), sem("router_copied")

    with nc.Block() as block:
        @block.sync
        def _(sp):
            w = io["w_out"][0].rearrange("(k p) n -> p k n", p=P)
            for k in range(0, KD, 4):
                sp.dma_start(wout[:, k:k + 4, :], w[:, k:k + 4, :]).then_inc(sem("w_out_loaded"), 16)
            sp.dma_start(wr, io["w_router"][0].rearrange("(k p) n -> p k n", p=P)).then_inc(sem("router_loaded"), 16)
            for x, name in enumerate(("w_s1", "w_s3")):
                sp.dma_start(ws[:, x], io[name][0].rearrange("(k p) n -> p k n", p=P)).then_inc(sem("shared_loaded"), 16)
            sp.dma_start(w2s, io["w_s2"][0].rearrange("(k p) n -> p k n", p=P)).then_inc(sem("shared_loaded"), 16)
            for i, (c0, n) in enumerate(TILES):
                sp.wait_ge(s_h, i + 1)
                sp.dma_start(io["h_rows"][c0:c0 + n, :], z[0:n, i % 2, :]).then_inc(sem(f"h_rows_out_{i % 2}"), 16)
            for i, (c0, n) in enumerate(TILES):
                sp.wait_ge(sem("shared_rows_added"), i + 1)
                sp.dma_start(io["residual"][c0:c0 + n, :], xr[0:n, i % 2, :]).then_inc(sem(f"residual_out_{i % 2}"), 16)
            sp.wait_ge(sem("residual_out_0"), 48)
            sp.wait_ge(sem("residual_out_1"), 32)
            sp.wait_ge(sem("h_rows_out_0"), 48)
            sp.wait_ge(sem("h_rows_out_1"), 32)

        @block.gpsimd
        def _(pool):
            pool.memset(score[:, NTT - 1, :], 1.0).then_inc(sem("score_zeroed"), 1)
            for x, name in enumerate(("ln1_g", "ln1_b")):
                pool.dma_start(lnp[:, x, :], io[name][0:1, :].to_broadcast([P, D]))\
                    .then_inc(sem("ln1_loaded"), 16)
            for i, (c0, n) in enumerate(TILES):
                if i >= 2:
                    pool.wait_ge(s_mean, i - 1)
                if i < NTT - 1:
                    pool.dma_start(xr[:, i % 2, :], io["x_prompt"][0, c0:c0 + n, :]).then_inc(sem(f"x_again_{i % 2}"), 16)
                else:
                    pool.dma_start(xr[0:NS:SB, i % 2, :], io["state_shift"][0]).then_inc(sem(f"x_again_{i % 2}"), 16)
                    for t in range(TS):
                        pool.dma_start(xr[1 + t:NS:SB, i % 2, :], io["x_sample"][:, t, :])\
                            .then_inc(sem(f"x_again_{i % 2}"), 16)
            for i, (c0, n) in enumerate(TILES):
                if i == 0:
                    pool.wait_ge(s_mean, NTT)
                if i >= 2:
                    pool.wait_ge(sem(f"residual_out_{i % 2}"), 16 * (i // 2))
                pool.wait_ge(sem(f"h_rows_out_{i % 2}"), 16 * (i // 2 + 1))
                pool.dma_start(xr[0:n, i % 2, :], io["h_rows"][c0:c0 + n, :]).then_inc(sem(f"h_again_{i % 2}"), 16)

        @block.tensor
        def _(pe):
            def product(i):
                c0, n = TILES[i]
                if i >= 2:
                    pe.wait_ge(s_mean, i - 1)
                for k in range(KD):
                    for h in range(2):
                        mm = pe.matmul(m.ps[2 * (i % 2) + h][0:n, :], merged[:, k, c0:c0 + n],
                                       wout[:, k, h * 512:(h + 1) * 512], start=(k == 0), stop=(k == KD - 1))
                mm.then_inc(s_z, 1)

            def turn(i):
                c0, n = TILES[i]
                pe.wait_ge(s_h, i + 1)
                if i >= 1:
                    pe.wait_ge(s_hc, i)
                for k in range(KD):
                    mm = pe.transpose(m.ps[4 + k // 4][:, (k % 4) * n:(k % 4 + 1) * n], z[0:n, i % 2, k * P:(k + 1) * P],
                                      m.ident[0:n, 0:n])
                mm.then_inc(s_ht, 1)

            def route(i):
                c0, n = TILES[i]
                pe.wait_ge(s_hc, i + 1)
                if i >= 1:
                    pe.wait_ge(s_rc, i)
                for k in range(KD):
                    mm = pe.matmul(m.ps[6][0:n, 0:NE], hT[:, k, c0:c0 + n], wr[:, k, :], start=(k == 0), stop=(k == KD - 1))
                mm.then_inc(s_rt, 1)

            pe.wait_ge(sem("w_out_loaded"), 32)
            pe.wait_ge(sem("router_loaded"), 16)
            product(0)
            for i in range(NTT):
                if i + 1 < NTT:
                    product(i + 1)
                turn(i)
                route(i)
            pe.wait_ge(sem("shared_loaded"), 48)
            pe.wait_ge(s_rc, NTT)
            for j in range(2):
                for x in range(2):
                    for k in range(KD):
                        for h in range(2):
                            mm = pe.matmul(m.ps[4 * j + 2 * x + h][:, 0:HALF], ws[:, x, k, j * P:(j + 1) * P],
                                           hT[:, k, h * HALF:(h + 1) * HALF], start=(k == 0), stop=(k == KD - 1))
                    mm.then_inc(sem("shared_hidden"), 1)
            pe.wait_ge(sem("shared_act"), 2)
            for i, (c0, n) in enumerate(TILES):
                if i >= 2:
                    pe.wait_ge(sem("shared_rows_added"), i - 1)
                for h in range(2):
                    for j in range(2):
                        mm = pe.matmul(m.ps[2 * (i % 2) + h][0:n, :], sact[:, j, c0:c0 + n], w2s[:, j, h * 512:(h + 1) * 512],
                                       start=(j == 0), stop=(j == 1))
                mm.then_inc(sem("shared_rows"), 1)

        @block.scalar
        def _(act):
            def copy_turned(i):
                c0, n = TILES[i]
                act.wait_ge(s_ht, i + 1)
                for g in range(2):
                    last = act.activation(hT[:, 4 * g:4 * g + 4, c0:c0 + n],
                                          m.ps[4 + g][:, 0:4 * n].rearrange("p (k n) -> p k n", k=4), ACT.Copy)
                last.then_inc(s_hc, 1)
                act.wait_ge(s_rt, i + 1)
                act.activation(score[0:n, i, :], m.ps[6][0:n, 0:NE], ACT.Copy).then_inc(s_rc, 1)

            act.wait_ge(sem("score_zeroed"), 1)
            for i, (c0, n) in enumerate(TILES):
                act.wait_ge(s_mean, i + 1)
                act.activation(junk[0:n, :], z[0:n, i % 2, :], ACT.Square, bias=stats[0:n, i, 3:4], accum_out=stats[0:n, i, 4:5])\
                   .then_inc(s_sq, 1)
                act.wait_ge(s_var, i + 1)
                act.activation(stats[0:n, i, 6:7], stats[0:n, i, 5:6], ACT.Sqrt).then_inc(s_dev, 1)
                copy_turned(i)
            act.drain()
            for i, (c0, n) in enumerate(TILES):
                act.activation(score[0:n, i, :], score[0:n, i, :], ACT.Sigmoid)
            for j in range(2):
                act.wait_ge(sem("shared_hidden"), 2 * j + 1)
                for h in range(2):
                    last = act.activation(ssil[:, j, h * HALF:(h + 1) * HALF], m.ps[4 * j + h][:, 0:HALF], ACT.Silu)
                last.then_inc(sem("shared_silu"), 1)

        @block.vector
        def _(dve):
            dve.wait_ge(sem("ln1_loaded"), 32)
            for i, (c0, n) in enumerate(TILES):
                x, zi, st = xr[0:n, i % 2, :], z[0:n, i % 2, :], stats[0:n, i, :]
                dve.wait_ge(s_z, i + 1)
                dve.wait_ge(sem(f"x_again_{i % 2}"), 16 * (i // 2 + 1) if i < NTT - 1 else 16 * (i // 2 + 1 + TS))
                if i >= 2:
                    dve.wait_ge(sem(f"h_rows_out_{i % 2}"), 16 * (i // 2))
                    dve.wait_ge(s_ht, i - 1)
                for h in range(2):
                    cols = slice(h * 512, (h + 1) * 512)
                    dve.scalar_tensor_tensor(out=zi[:, cols], in0=x[:, cols], scalar=ALPHA, in1=m.ps[2 * (i % 2) + h][0:n, :],
                                             op0=ALU.mult, op1=ALU.add, accum_out=st[:, h:h + 1])
                dve.drain()
                dve.tensor_tensor(st[:, 2:3], st[:, 0:1], st[:, 1:2], ALU.add)
                dve.drain()
                dve.tensor_scalar(st[:, 3:4], st[:, 2:3], -1.0 / D, None, ALU.mult).then_inc(s_mean, 1)
                dve.wait_ge(s_sq, i + 1)
                dve.tensor_scalar(st[:, 5:6], st[:, 4:5], 1.0 / D, LN_EPS, ALU.mult, ALU.add).then_inc(s_var, 1)
                dve.wait_ge(s_dev, i + 1)
                dve.reciprocal(st[:, 7:8], st[:, 6:7])
                dve.drain()
                dve.tensor_scalar(zi, zi, st[:, 3:4], st[:, 7:8], ALU.add, ALU.mult)
                dve.drain()
                dve.tensor_tensor(zi, zi, lnp[0:n, 0, :], ALU.mult)
                dve.drain()
                dve.tensor_tensor(zi, zi, lnp[0:n, 1, :], ALU.add).then_inc(s_h, 1)
            for j in range(2):
                dve.wait_ge(sem("shared_silu"), j + 1)
                dve.wait_ge(sem("shared_hidden"), 2 * j + 2)
                for h in range(2):
                    last = dve.tensor_tensor(sact[:, j, h * HALF:(h + 1) * HALF], m.ps[4 * j + 2 + h][:, 0:HALF],
                                             ssil[:, j, h * HALF:(h + 1) * HALF], ALU.mult)
                last.then_inc(sem("shared_act"), 1)
            for i, (c0, n) in enumerate(TILES):
                dve.wait_ge(sem(f"h_again_{i % 2}"), 16 * (i // 2 + 1))
                dve.wait_ge(sem("shared_rows"), i + 1)
                for h in range(2):
                    cols = slice(h * 512, (h + 1) * 512)
                    last = dve.scalar_tensor_tensor(out=xr[0:n, i % 2, cols], in0=xr[0:n, i % 2, cols], scalar=ALPHA,
                                                    in1=m.ps[2 * (i % 2) + h][0:n, :], op0=ALU.mult, op1=ALU.add)
                last.then_inc(sem("shared_rows_added"), 1)


O_WEXP = (O_TOP, O_TOP + WEXP, 0, WEXP)
NEP = NE + 2
O_PLACE = 2 * WEXP
O_INFO = O_PLACE + NTT * NEP
O_XG = O_INFO + NTT * NEP * 3
O_XTE = O_XG + 2 * D
O_YG = O_XTE + 2 * KD * SLOTS
O_OH = O_YG + 2 * D
O_HE = O_OH + 2 * NTT * SLOTS
O_SE = O_HE + 2 * 2 * SLOTS
O_GC = O_SE + 2 * 2 * SLOTS
assert O_GC + 4 <= O_SCORE
ABSENT = 4096.0
MAX_ROUNDS = (BS * TS + SEQ + SLOTS - 1) // SLOTS


def stage_route(nc, m, io):
    score = m.at(O_SCORE, NTT, NE)
    place, info = m.at(O_PLACE, NTT, NEP), m.at(O_INFO, NTT, NEP, 3)
    o = O_XG
    sel, rest, picked, rank = (m.at(o + x * NTT * NE, NTT, NE) for x in range(4))
    o += 4 * NTT * NE
    gated = m.at(o, NTT, NE)
    o += NTT * NE
    bias, top8, small = m.at(o, NE), m.at(o + NE, NTT, 8), m.at(o + NE + 8 * NTT, 32)
    assert o + NE + 8 * NTT + 32 <= O_SCORE
    sem = m.sem
    s_pick, s_pos = sem("experts_picked"), sem("queue_places")
    with nc.Block() as block:
        @block.sync
        def _(sp):
            sp.dma_start(bias, io["b_router"][0:1, :].to_broadcast([P, NE])).then_inc(sem("router_bias_loaded"), 16)
            for e in (2, 3):
                prefetch_expert(sp, m, io, e, e, O_WEXP[e], sem)

        @block.tensor
        def _(pe):
            pe.wait_ge(s_pick, 1)
            for i in range(NTT):
                out = m.ps[i // 4][:, (i % 4) * NE:(i % 4 + 1) * NE]
                for k in range(i):
                    pe.matmul(out, m.ones[:, :], picked[:, k, :], start=(k == 0), stop=False)
                pe.matmul(out, m.upper[:, 0, :], picked[:, i, :], start=(i == 0), stop=True)
            for k in range(NTT):
                mm = pe.matmul(m.ps[2][:, 0:NE], m.ones[:, :], picked[:, k, :], start=(k == 0), stop=(k == NTT - 1))
            mm.then_inc(s_pos, 1)

        @block.vector
        def _(dve):
            dve.wait_ge(sem("router_bias_loaded"), 16)
            for i in range(NTT):
                dve.tensor_tensor(sel[:, i, :], score[:, i, :], bias, ALU.add)
            dve.drain()
            for i in range(NTT):
                dve.max(top8[:, i, :], sel[:, i, :])
            dve.drain()
            for i in range(NTT):
                dve.match_replace(rest[:, i, :], top8[:, i, :], sel[:, i, :], -1e30)
            dve.drain()
            dve.tensor_tensor(picked, rest, sel, ALU.not_equal)
            dve.drain()
            dve.tensor_scalar(picked[:, NTT - 1, :], picked[:, NTT - 1, :], m.valid[:, 0:1], None, ALU.mult)
            dve.drain()
            dve.tensor_tensor(gated, picked, score, ALU.mult).then_inc(s_pick, 1)
            for i in range(NTT):
                dve.tensor_tensor_scan(rank[:, i, :], m.ones[:, :], picked[:, i, :], 0.0, ALU.mult, ALU.add)
            dve.drain()
            den, scale = small[:, 0:NTT], small[:, 8:8 + NTT]
            dve.tensor_reduce(den, gated, AX.X, ALU.add)
            dve.drain()
            dve.tensor_scalar(den, den, 1e-30, 1.0 / ROUTED, ALU.max, ALU.mult)
            dve.drain()
            dve.reciprocal(scale, den)
            dve.drain()
            rows8 = small[:, 16:16 + NTT]
            dve.tensor_scalar(rows8, m.row[:, :], float(TOPK), -1.0 - FAR, ALU.mult, ALU.add)
            dve.memset(info[:, :, NE:NEP, :], 0.0)
            dve.memset(place[:, :, NE:NEP], ABSENT)
            dve.drain()
            for i in range(NTT):
                dve.tensor_scalar(info[:, i, 0:NE, 0], m.ones[:, :], m.row[:, i:i + 1], -FAR, ALU.mult, ALU.add)
                dve.tensor_scalar(info[:, i, 0:NE, 1], rank[:, i, :], rows8[:, i:i + 1], None, ALU.add)
                dve.tensor_scalar(info[:, i, 0:NE, 2], gated[:, i, :], scale[:, i:i + 1], None, ALU.mult)
            dve.wait_ge(s_pos, 1)
            dve.tensor_scalar(rest, picked, -ABSENT, ABSENT, ALU.mult, ALU.add)
            dve.drain()
            dve.tensor_tensor(place[:, 0:4, 0:NE], m.ps[0][:, :].rearrange("p (a n) -> p a n", a=4), rest[:, 0:4, :], ALU.add)
            dve.tensor_tensor(place[:, 4, 0:NE], m.ps[1][:, 0:NE], rest[:, 4, :], ALU.add)
            most, more = small[:, 24:25], small[:, 25:26]
            dve.tensor_reduce(most, m.ps[2][:, 0:NE], AX.X, ALU.max)
            dve.drain()
            dve.tensor_scalar(top8[:, 0, 0:MAX_ROUNDS - 1], m.slot[:, 1:MAX_ROUNDS], float(SLOTS), most, ALU.mult, ALU.is_lt)
            dve.drain()
            dve.tensor_reduce(more, top8[:, 0, 0:MAX_ROUNDS - 1], AX.X, ALU.add)
            dve.drain()
            dve.tensor_scalar(m.rounds[:, :], more, 1.0, None, ALU.add)


def stage_experts(nc, m, io):
    place, info = m.at(O_PLACE, NTT, NEP), m.at(O_INFO, NTT, NEP, 3)
    xg, yg = m.at(O_XG, 2, D), m.at(O_YG, 2, D)
    xt, onehot = m.at(O_XTE, 2, KD, SLOTS), m.at(O_OH, 2, NTT, SLOTS)
    hid, sil, gatec = m.at(O_HE, 2, 2, SLOTS), m.at(O_SE, 2, 2 * SLOTS), m.at(O_GC, 4)
    weights = [m.at(o, 3, 2 * D) for o in O_WEXP]
    w1 = [w[:, 0, :].rearrange("p (c n) -> p c n", c=KD) for w in weights]
    w3 = [w[:, 1, :].rearrange("p (c n) -> p c n", c=KD) for w in weights]
    w2 = [w[:, 2, :].rearrange("p (c n) -> p c n", c=2) for w in weights]
    sem = m.sem
    s_oh, s_slot, s_idx = sem("one_hot_ready"), sem("slots_found"), sem("slot_indices_ready")
    s_in = [sem(f"rows_gathered_{u}") for u in range(2)]
    s_out = [sem(f"rows_scattered_{u}") for u in range(2)]
    s_t, s_xt = sem("expert_rows_turned"), sem("expert_rows_copied")
    s_gu, s_sil, s_hid, s_y = sem("expert_products"), sem("expert_silu"), sem("expert_hidden"), sem("expert_output")
    s_yv, s_ya = sem("output_scaled_vector"), sem("output_scaled_scalar")
    S = SLOTS

    def rounds(eng):
        return eng.value_load(m.rounds[0:1, 0:1], min_val=1, max_val=MAX_ROUNDS)

    with nc.Block() as block:
        @block.sync
        def _(sp):
            count = rounds(sp)

            def load(r, first, u, e):
                sp.wait_ge(s_y, NE * r + first + u + 1)
                prefetch_expert(sp, m, io, e, u, O_WEXP[u], sem)

            with sp.Fori(0, count) as r:
                with sp.Fori(0, NE // 4 - 1) as i:
                    for u in range(4):
                        load(r, 4 * i, u, 4 * i + 4 + u)
                with sp.If(r < count - 1):
                    for u in range(4):
                        load(r, NE - 4, u, u)

        @block.gpsimd
        def _(pool):
            count = rounds(pool)
            for u in range(2):
                pool.dma_start(xg[0:S, u, :], io["h_rows"][0:S, :]).then_inc(s_out[u], 16)
            for u in range(2):
                pool.wait_ge(s_out[u], 16)

            def gather(r, n, i, u):
                pool.wait_ge(s_idx, NEP * r + n + 2)
                pool.sem_inc(sem("gathers_begun"), 1)
                pool.indirect_dma_start(xg[0:S, u % 2, :], None, io["h_rows"][:, :],
                                        bass.IndirectOffsetOnAxis(ap=m.index[0:S, u, 0:1], axis=0),
                                        bounds_check=NT - 1, oob_is_err=False).then_inc(s_in[u % 2], 16)

            with pool.Fori(0, count) as r:
                for n in range(2):
                    gather(r, n, 0, n)
                with pool.Fori(0, NE // 4) as i:
                    for u in range(4):
                        n = 4 * i + u
                        pool.wait_ge(s_t, (NE + 1) * r + n + 1)
                        gather(r, n + 2, i, (u + 2) % 4)
                        pool.wait_ge(s_yv, NE * r + n + 3)
                        pool.wait_ge(s_ya, NE * r + n + 3)
                        pool.sem_inc(sem("scatters_begun"), 1)
                        pool.indirect_dma_start(io["routed_rows"][:, :],
                                                bass.IndirectOffsetOnAxis(ap=m.index[0:S, u, 1:2], axis=0),
                                                yg[0:S, u % 2, :], None,
                                                bounds_check=NT * TOPK - 1, oob_is_err=False).then_inc(s_out[u % 2], 16)

        @block.tensor
        def _(pe):
            count = rounds(pe)

            def find_slots(r, n, u):
                pe.wait_ge(s_oh, NEP * r + n + 1)
                pe.wait_ge(s_idx, NEP * r + n + 1)
                for i in range(NTT):
                    mm = pe.matmul(m.ps[0][0:S, 0:3], onehot[:, u % 2, i, :],
                                   info[:, i, ds(n, 1), :], start=(i == 0), stop=(i == NTT - 1))
                mm.then_inc(s_slot, 1)

            def turn(u):
                for c in range(KD):
                    mm = pe.transpose(m.ps[1][:, c * S:(c + 1) * S], xg[0:S, u % 2, c::KD], m.ident[0:S, 0:S])
                mm.then_inc(s_t, 1)

            with pe.Fori(0, count) as r:
                find_slots(r, 0, 0)
                pe.wait_ge(s_in[0], (16 * NEP // 2) * r + 16)
                pe.wait_ge(s_xt, (NE + 1) * r + 1)
                find_slots(r, 1, 1)
                turn(0)
                with pe.Fori(0, NE // 4) as i:
                    for u in range(4):
                        n = 4 * i + u
                        prod = m.ps[2 + u % 2]
                        pe.wait_ge(sem(f"expert_weights_{u}"), (48 * NE // 4) * r + 48 * i + 48)
                        pe.wait_ge(s_xt, (NE + 1) * r + n + 2)
                        for x, w in enumerate((w1[u], w3[u])):
                            for j in range(2):
                                q = 2 * x + j
                                for c in range(KD):
                                    mm = pe.matmul(prod[:, q * S:(q + 1) * S], w[:, c, j::2], xt[:, u % 2, c, :],
                                                   start=(c == 0), stop=(c == KD - 1))
                        mm.then_inc(s_gu, 1)
                        pe.wait_ge(s_in[(u + 1) % 2], (16 * NEP // 2) * r + 32 * i + 16 * ((u + 1) // 2) + 16)
                        find_slots(r, n + 2, u)
                        turn(u + 1)
                        pe.wait_ge(s_hid, NE * r + n + 1)
                        pe.wait_ge(s_yv, NE * r + n + 1)
                        pe.wait_ge(s_ya, NE * r + n + 1)
                        for h in range(2):
                            for j in range(2):
                                mm = pe.matmul(m.ps[4 + 2 * (u % 2) + h][0:S, :], hid[:, u % 2, j, :],
                                               w2[u][:, j, h * 512:(h + 1) * 512], start=(j == 0), stop=(j == 1))
                        mm.then_inc(s_y, 1)

        @block.scalar
        def _(act):
            count = rounds(act)
            act.sem_inc(s_ya, 2)
            act.sem_inc(s_xt, 1)

            def copy_turned(r, n, u):
                act.wait_ge(s_t, (NE + 1) * r + n + 1)
                act.activation(xt[:, u % 2, :, :], m.ps[1][:, :].rearrange("p (c s) -> p c s", c=KD), ACT.Copy)\
                   .then_inc(s_xt, 1)

            with act.Fori(0, count) as r:
                copy_turned(r, 0, 0)
                with act.Fori(0, NE // 4) as i:
                    for u in range(4):
                        n = 4 * i + u
                        act.wait_ge(s_gu, NE * r + n + 1)
                        act.activation(sil[:, u % 2, :], m.ps[2 + u % 2][:, 0:2 * S], ACT.Silu).then_inc(s_sil, 1)
                        copy_turned(r, n + 1, u + 1)
                        act.wait_ge(s_y, NE * r + n + 1)
                        act.wait_ge(s_out[u % 2], (16 * NE // 2) * r + 32 * i + 16 * (u // 2) + 16)
                        act.activation(yg[0:S, u % 2, 512:D], m.ps[5 + 2 * (u % 2)][0:S, :], ACT.Copy,
                                       scale=gatec[0:S, u:u + 1]).then_inc(s_ya, 1)

        @block.vector
        def _(dve):
            count = rounds(dve)
            dve.sem_inc(s_yv, 2)
            dve.sem_inc(s_idx, 1)

            def one_hot(n, u):
                for i in range(NTT):
                    last = dve.tensor_scalar(onehot[:, u % 2, i, :], m.slot[:, :], place[:, i, ds(n, 1)], None, ALU.is_equal)
                last.then_inc(s_oh, 1)

            def indices(r, n, u):
                dve.wait_ge(s_slot, NEP * r + n + 1)
                dve.tensor_scalar(m.index[0:S, u, :], m.ps[0][0:S, 0:2], FAR, None, ALU.add)
                dve.tensor_copy(gatec[0:S, u:u + 1], m.ps[0][0:S, 2:3]).then_inc(s_idx, 1)

            with dve.Fori(0, count) as r:
                for n in range(2):
                    one_hot(n, n)
                    indices(r, n, n)
                with dve.Fori(0, NE // 4) as i:
                    for u in range(4):
                        n = 4 * i + u
                        one_hot(n + 2, u)
                        dve.wait_ge(s_sil, NE * r + n + 1)
                        dve.tensor_tensor(hid[:, u % 2, :, :].rearrange("p j s -> p (j s)"), m.ps[2 + u % 2][:, 2 * S:4 * S],
                                          sil[:, u % 2, :], ALU.mult).then_inc(s_hid, 1)
                        dve.wait_ge(s_out[u % 2], (16 * NE // 2) * r + 32 * i + 16 * (u // 2) + 16)
                        indices(r, n + 2, (u + 2) % 4)
                        dve.wait_ge(s_y, NE * r + n + 1)
                        dve.tensor_scalar(yg[0:S, u % 2, 0:512], m.ps[4 + 2 * (u % 2)][0:S, :], gatec[0:S, u:u + 1], None, ALU.mult)\
                           .then_inc(s_yv, 1)
                for u in range(2):
                    dve.wait_ge(s_out[u], (16 * NE // 2) * r + 16 * NE // 2 + 16)
                    dve.wait_ge(s_in[u], (16 * NEP // 2) * r + 16 * NEP // 2)
                dve.tensor_scalar(place, place, -float(S), None, ALU.add)
                dve.drain()


O_PART = 0
O_RES = O_PART + NTT * TOPK * D
O_LN2 = O_RES + NTT * D
O_CSTAT = O_LN2 + 2 * D
assert O_CSTAT + 8 * NTT <= ARENA


def stage_combine(nc, m, io):
    part, z = m.at(O_PART, NTT, TOPK, D), m.at(O_RES, NTT, D)
    lnp, stats = m.at(O_LN2, 2, D), m.at(O_CSTAT, NTT, 8)
    squares = m.at(O_PART, NTT, TOPK * D)
    sem = m.sem
    s_sum, s_sq, s_var, s_dev, s_y = (sem(f"final_{x}") for x in ("sum", "squares", "variance", "deviation", "rows"))
    with nc.Block() as block:
        @block.sync
        def _(sp):
            routed = io["routed_rows"].rearrange("(t k) d -> t k d", k=TOPK)
            for x, name in enumerate(("ln2_g", "ln2_b")):
                sp.dma_start(lnp[:, x, :], io[name][0:1, :].to_broadcast([P, D])).then_inc(sem("ln2_loaded"), 16)
            for i, (c0, n) in enumerate(TILES[:-1]):
                for k in range(0, TOPK, 4):
                    sp.dma_start(part[:, i, k:k + 4, :], routed[c0:c0 + n, k:k + 4, :]).then_inc(sem(f"parts_loaded_{i}"), 16)
                sp.dma_start(z[:, i, :], io["residual"][c0:c0 + n, :]).then_inc(sem(f"parts_loaded_{i}"), 16)
            sp.wait_ge(sem("rows_cleared"), 1)
            for t in range(1, SB):
                sp.dma_start(part[t:NS:SB, NTT - 1, :, :], routed[SEQ + t:NT:SB, :, :]).then_inc(sem("parts_loaded_4"), 16)
            sp.dma_start(z[0:NS, NTT - 1, :], io["residual"][SEQ:NT, :]).then_inc(sem("parts_loaded_4"), 16)
            for i, (c0, n) in enumerate(TILES):
                sp.wait_ge(s_y, i + 1)
                if i < NTT - 1:
                    sp.dma_start(io["out_y_p"][0, c0:c0 + n, :], z[:, i, :]).then_inc(sem("outputs_written"), 16)
                else:
                    for t in range(TS):
                        sp.dma_start(io["out_y_s"][:, t, :], z[1 + t:NS:SB, i, :]).then_inc(sem("outputs_written"), 16)
            sp.wait_ge(sem("outputs_written"), 16 * OUT_ALL)

        @block.gpsimd
        def _(pool):
            pool.memset(part[0:NS, NTT - 1, :, :], 0.0).then_inc(sem("rows_cleared"), 1)

        @block.scalar
        def _(act):
            for i, (c0, n) in enumerate(TILES):
                act.wait_ge(s_sum, i + 1)
                act.activation(squares[0:n, i, 0:D], z[0:n, i, :], ACT.Square, bias=stats[0:n, i, 1:2],
                               accum_out=stats[0:n, i, 2:3]).then_inc(s_sq, 1)
                act.wait_ge(s_var, i + 1)
                act.activation(stats[0:n, i, 4:5], stats[0:n, i, 3:4], ACT.Sqrt).then_inc(s_dev, 1)

        @block.vector
        def _(dve):
            for i, (c0, n) in enumerate(TILES):
                zi, st, rows = z[0:n, i, :], stats[0:n, i, :], part[0:n, i, :, :].rearrange("p k d -> p (k d)")
                dve.wait_ge(sem(f"parts_loaded_{i}"), 16 * (3 if i < NTT - 1 else 1 + TS))
                for width in (4 * D, 2 * D, D):
                    dve.tensor_tensor(rows[:, 0:width], rows[:, 0:width], rows[:, width:2 * width], ALU.add)
                    dve.drain()
                dve.scalar_tensor_tensor(out=zi, in0=zi, scalar=1.0, in1=rows[:, 0:D], op0=ALU.mult, op1=ALU.add,
                                         accum_out=st[:, 0:1])
                dve.drain()
                dve.tensor_scalar(st[:, 1:2], st[:, 0:1], -1.0 / D, None, ALU.mult).then_inc(s_sum, 1)
                dve.wait_ge(s_sq, i + 1)
                dve.tensor_scalar(st[:, 3:4], st[:, 2:3], 1.0 / D, LN_EPS, ALU.mult, ALU.add).then_inc(s_var, 1)
                dve.wait_ge(s_dev, i + 1)
                dve.reciprocal(st[:, 5:6], st[:, 4:5])
                dve.drain()
                dve.tensor_scalar(zi, zi, st[:, 1:2], st[:, 5:6], ALU.add, ALU.mult)
                if i == 0:
                    dve.wait_ge(sem("ln2_loaded"), 32)
                dve.drain()
                dve.tensor_tensor(zi, zi, lnp[0:n, 0, :], ALU.mult)
                dve.drain()
                dve.tensor_tensor(zi, zi, lnp[0:n, 1, :], ALU.add).then_inc(s_y, 1)


STAGES = (stage_load, stage_project, stage_prepare, stage_wkv, stage_attend, stage_merge, stage_mix, stage_route,
          stage_experts, stage_combine)


SHAPES = {
    "x_prompt": (1, SEQ, D), "x_sample": (BS, TS, D), "state_wkv": (1, BS, 8, HD, HD), "state_shift": (1, BS, D),
    "state_conv": (1, BS, BUF, W), "cache_mem_k": (1, BS, NM, MH, P), "cache_mem_v": (1, BS, NM, MH, P),
    "mem_prompt": (1, NM, D), "w_in": (1, D, OFF_GATE + 3 * D), "mu_shift": (1, RW), "w0": (1, W),
    "w_up": (1, 64, W), "a0": (1, W), "a_up": (1, 64, W), "g_up": (1, 128, W), "k_k": (1, W), "k_a": (1, W),
    "r_k": (1, 8, HD), "lnx_g": (1, W), "lnx_b": (1, W), "w_o_a": (1, W, D), "conv_w": (1, TAPS, W),
    "conv_b": (1, W), "cn_g": (1, W), "cn_b": (1, W), "w_o_b": (1, W, D), "w_mem_kv": (1, D, 2 * W),
    "w_o_c": (1, W, D), "w_out": (1, D, D), "ln1_g": (1, D), "ln1_b": (1, D), "ln2_g": (1, D), "ln2_b": (1, D),
    "w_router": (1, D, NE), "b_router": (1, NE), "w_e1": (1, NE, D, DE), "w_e3": (1, NE, D, DE),
    "w_e2": (1, NE, DE, D), "w_s1": (1, D, DE), "w_s3": (1, D, DE), "w_s2": (1, DE, D),
}
OUTPUTS = [
    ("out_y_p", (1, SEQ, D)), ("out_y_s", (BS, TS, D)), ("out_wkv_p", (1, 1, 8, HD, HD)), ("out_shift_p", (1, 1, D)),
    ("out_conv_p", (1, 1, BUF, W)), ("out_mk", (1, 1, NM, MH, P)), ("out_mv", (1, 1, NM, MH, P)),
    ("out_wkv_s", (1, BS, 8, HD, HD)), ("out_shift_s", (1, BS, D)), ("out_conv_s", (1, BS, BUF, W)),
]


def build(nc):
    io = {n: nc.dram_tensor(f"in_{n}", s, F32, kind="ExternalInput").ap() for n, s in SHAPES.items()}
    io |= {n: nc.dram_tensor(n, s, F32, kind="ExternalOutput").ap() for n, s in OUTPUTS}
    io["sample_vectors"] = nc.dram_tensor("sample_vectors", (8, NS, 6, HD), F32, kind="Internal").ap()
    io["sample_y"] = nc.dram_tensor("sample_y", (2, 8, BS, TS, HD // 2), F32, kind="Internal").ap()
    io["h_rows"] = nc.dram_tensor("h_rows", (NT, D), F32, kind="Internal").ap()
    io["residual"] = nc.dram_tensor("residual", (NT, D), F32, kind="Internal").ap()
    io["routed_rows"] = nc.dram_tensor("routed_rows", (NT * TOPK, D), F32, kind="Internal").ap()
    with ExitStack() as ctx:
        m = Memory(nc, ctx)
        for stage in STAGES:
            stage(nc, m, io)
            if stage is stage_wkv:
                m.recycle(WKV_ONLY)


def kernel(**inputs):
    import numpy as np
    import concourse.bacc as bacc
    from concourse.bass_utils import run_bass_kernel_spmd

    nc = bacc.Bacc("TRN2", target_bir_lowering=False, num_devices=1)
    build(nc)
    arrays = {f"in_{n}": np.ascontiguousarray(inputs[n]) for n in SHAPES}
    got = run_bass_kernel_spmd(nc, [arrays], core_ids=[0]).results[0]
    return tuple(got[n] for n, _ in OUTPUTS)
```

```python
from contextlib import ExitStack

import concourse.bass as bass
from concourse import mybir

F32 = mybir.dt.float32
U32 = mybir.dt.uint32
I32 = mybir.dt.int32
ALU = mybir.AluOpType
ACT = mybir.ActivationFunctionType
AX = mybir.AxisListType
ds = bass.ds

P = 128
D = 1024
KD = D // P
SEQ, BS, TS = 512, 8, 4
SB = TS + 1
NS = BS * SB
NT = SEQ + NS
HALF = NT // 2
W = 512
KW = W // P
HD = 64
CH = 64
NCH = SEQ // CH
TAPS = 31
BUF = TAPS - 1
NM = 256
MT = NM // P
MH = 4
RW = 3 * W + 64 + 64 + 128
N_RW, N_GLU, N_Q = RW // P, 2 * W // P, W // P
OFF_GLU, OFF_Q = RW, RW + 2 * W
OFF_GATE = OFF_Q + W
NE, TOPK, DE = 128, 8, 256
ALPHA = 2.0 ** 0.25
LN_EPS = 1e-5
GN_EPS = HD * 1e-5
RATE = 0.6065306597126334
ROUTED = 2.5
SLOTS = 64
FAR = 8192.0
TILES = [(i * P, P) for i in range(SEQ // P)] + [(SEQ, NS)]
NTT = len(TILES)

T_GLU, T_RW = 0, N_GLU
T_R, T_K, T_V, T_WA, T_G = T_RW, T_RW + KW, T_RW + 2 * KW, T_RW + 3 * KW, T_RW + 3 * KW + 1
T_Q = T_RW + N_RW
N_PROJ = T_Q + N_Q
PW = NT + 1

V_MU, V_W0, V_A0, V_KK, V_KA, V_RK, V_LG, V_LB, V_CB, V_CG, V_CBB = 0, 14, 18, 22, 26, 30, 34, 38, 42, 46, 50
N_VEC = 54

ARENA = 50688
WEXP = 6 * 1024
O_XT = 0
O_PROJ = O_XT + KD * NT
O_RATE = O_PROJ + N_PROJ * PW
O_AGATE = O_RATE + KW * NT
O_OUTG = O_AGATE + KW * NT
O_KKEY = O_OUTG + KW * NT
O_BKEY = O_KKEY + KW * NT
O_EXT = O_BKEY + KW * NT
O_EXS = O_EXT + KW * (SEQ + BUF)
O_CONV = O_EXS + KW * BS * (TS + BUF)
O_WBUF = O_CONV + KW * NT
O_TMP = O_WBUF + 2 * D
O_TOP = ARENA - 2 * WEXP
assert O_TMP + NT <= O_TOP

OUT_LOAD = 3
OUT_PROJECT = OUT_LOAD + 1 + BS + 2 * MT
OUT_WKV = OUT_PROJECT + 1
OUT_ALL = OUT_WKV + NTT - 1 + TS


class Memory:

    def __init__(self, nc, ctx):
        self.nc, self.ctx, self.sems = nc, ctx, {}
        self.arena = self.sb("arena", [P, ARENA])
        self.ident = self.sb("ident", [P, P])
        self.fold = self.sb("fold", [P, HD])
        self.upper = self.sb("upper", [P, 2, P])
        self.lower = self.sb("lower", [P, P])
        self.ones = self.sb("ones", [P, P])
        self.heads = self.sb("heads", [P, P])
        self.vec = self.sb("vec", [P, N_VEC])
        self.taps = self.sb("taps", [P, TAPS * KW])
        self.slot = self.sb("slot", [P, 2 * SLOTS])
        self.half = self.sb("half", [P, 1])
        self.row = self.sb("row", [P, NTT])
        self.valid = self.sb("valid", [P, 1])
        self.xlast = self.sb("xlast", [P, 64])
        self.sample_tmp = self.sb("sample_tmp", [P, 8, HD])
        self.eps = self.sb("eps", [P, 2])
        self.rounds = self.sb("rounds", [P, 1], I32)
        self.index = self.sb("index", [P, 4, 2], U32)
        self.ps = [ctx.enter_context(nc.psum_tensor(f"bank{i}", [P, 512], F32)) for i in range(8)]

    def sb(self, name, shape, dt=F32):
        return self.ctx.enter_context(self.nc.sbuf_tensor(name, shape, dt))

    def sem(self, name):
        if name not in self.sems:
            self.sems[name] = self.nc.alloc_semaphore(name=name)
        return self.sems[name]

    def recycle(self, names):
        with self.nc.Block() as block:
            @block.gpsimd
            def _(pool):
                for name in names:
                    pool.sem_clear(self.sems[name])
        for name in names:
            self.nc.release_semaphore(self.sems.pop(name))

    def at(self, offset, *shape):
        n = 1
        for s in shape:
            n *= s
        assert offset + n <= ARENA
        v = self.arena[:, offset:offset + n]
        if len(shape) == 2:
            return v.rearrange("p (a b) -> p a b", a=shape[0])
        if len(shape) == 3:
            return v.rearrange("p (a b c) -> p a b c", a=shape[0], b=shape[1])
        if len(shape) == 4:
            return v.rearrange("p (a b c d) -> p a b c d", a=shape[0], b=shape[1], c=shape[2])
        return v


def sample_cols(ap):
    return ap.rearrange("p (b s) -> p b s", s=SB)[:, :, 1:SB]


def stage_load(nc, m, io):
    xtok = m.at(O_PROJ, NTT, D)
    vrows = m.at(O_PROJ + NTT * D, P)
    trows = m.at(O_PROJ + NTT * D + P, P)
    crows = m.at(O_PROJ + NTT * D + 2 * P, 2, W)
    xT = m.at(O_XT, KD, NT)
    exs = m.at(O_EXS, KW, BS, TS + BUF)
    ext = m.at(O_EXT, KW, SEQ + BUF)
    proj = m.at(O_PROJ, N_PROJ, PW)
    CR = BS * BUF // 2
    s_const, s_x = m.sem("constants_ready"), [m.sem(f"x_rows_{i}") for i in range(NTT)]
    s_v, s_cs = m.sem("vectors_loaded"), m.sem("conv_state_loaded")
    s_t, s_e = m.sem("turned"), m.sem("turned_copied")

    groups = []
    for i, (c0, n) in enumerate(TILES):
        for g in range(2):
            groups.append((s_x[i], 16 if i < NTT - 1 else 16 * (1 + TS), n,
                           [xtok[0:n, i, (4 * g + k) * P:(4 * g + k + 1) * P] for k in range(4)],
                           xT[:, 4 * g:4 * g + 4, c0:c0 + n]))
    for r in range(2):
        groups.append((s_cs, 32, CR, [crows[0:CR, r, j * P:(j + 1) * P] for j in range(KW)],
                       exs[:, :, 4 * r:4 * r + 4, 0:BUF]))
    vec_wait = 16 * 11 + 16
    groups.append((s_v, vec_wait, N_VEC, [vrows[0:N_VEC, :]], m.vec[:, :]))
    groups.append((s_v, vec_wait, TAPS * KW, [trows[0:TAPS * KW, :]], m.taps[:, :]))

    with nc.Block() as block:
        @block.sync
        def _(sp):
            for i in range(NTT - 1):
                sp.dma_start(xtok[:, i, :], io["x_prompt"][0, i * P:(i + 1) * P, :]).then_inc(s_x[i], 16)
            sp.dma_start(xtok[0:NS:SB, NTT - 1, :], io["state_shift"][0]).then_inc(s_x[-1], 16)
            for t in range(TS):
                sp.dma_start(xtok[1 + t:NS:SB, NTT - 1, :], io["x_sample"][:, t, :]).then_inc(s_x[-1], 16)

        @block.scalar
        def _(act):
            for at, name in ((V_MU, "mu_shift"), (V_W0, "w0"), (V_A0, "a0"), (V_KK, "k_k"), (V_KA, "k_a"),
                             (V_LG, "lnx_g"), (V_LB, "lnx_b"), (V_CB, "conv_b"), (V_CG, "cn_g"), (V_CBB, "cn_b")):
                v = io[name][0].rearrange("(j p) -> j p", p=P)
                act.dma_start(vrows[at:at + v.shape[0], :], v).then_inc(s_v, 16)
            act.dma_start(vrows[V_RK:V_RK + KW, :], io["r_k"][0].rearrange("(j h) n -> j (h n)", h=2)).then_inc(s_v, 16)
            act.dma_start(trows[0:TAPS * KW, :], io["conv_w"][0].rearrange("k (j p) -> (k j) p", p=P)).then_inc(s_v, 16)
            cs = io["state_conv"][0].rearrange("b i c -> (b i) c")
            for r in range(2):
                act.dma_start(crows[0:CR, r, :], cs[r * CR:(r + 1) * CR, :]).then_inc(s_cs, 16)
            act.dma_start(io["out_shift_p"][0], io["x_prompt"][:, SEQ - 1, :]).then_inc(m.sem("outputs_written"), 16)
            act.dma_start(io["out_shift_s"][0], io["x_sample"][:, TS - 1, :]).then_inc(m.sem("outputs_written"), 16)
            act.dma_start(io["out_conv_s"][0][:, 0:BUF - TS, :], io["state_conv"][0][:, TS:BUF, :])\
               .then_inc(m.sem("outputs_written"), 16)

        @block.gpsimd
        def _(pool):
            pool.memset(m.ident[:], 1.0)
            pool.memset(m.fold[:], 1.0)
            pool.memset(m.upper[:], 1.0)
            pool.memset(m.lower[:], 1.0)
            pool.memset(m.ones[:], 1.0)
            pool.memset(m.heads[:], 0.0)
            pool.memset(m.eps[:, 0:1], GN_EPS)
            pool.memset(m.eps[:, 1:2], LN_EPS)
            pool.memset(m.valid[:], 1.0)
            pool.memset(ext[:, :, 0:BUF], 0.0)
            pool.drain()
            pool.memset(m.half[0:SLOTS, :], 2 * FAR)
            pool.memset(m.half[SLOTS:P, :], 2 * FAR + 1)
            pool.memset(m.heads[0:HD, 0:HD], 1.0)
            pool.memset(m.heads[HD:P, HD:P], 1.0)
            pool.drain()
            pool.affine_select(out=m.ident[:], in_=m.ident[:], compare_op=ALU.is_equal, fill=0.0, base=0,
                               pattern=[[-1, P]], channel_multiplier=1)
            pool.drain()
            pool.affine_select(out=m.fold[0:HD, :], in_=m.fold[0:HD, :], compare_op=ALU.is_equal, fill=0.0, base=0,
                               pattern=[[-1, HD]], channel_multiplier=1)
            pool.affine_select(out=m.fold[HD:P, :], in_=m.fold[HD:P, :], compare_op=ALU.is_equal, fill=0.0, base=0,
                               pattern=[[-1, HD]], channel_multiplier=1)
            pool.drain()
            pool.affine_select(out=m.upper[:, 0, :], in_=m.upper[:, 0, :], compare_op=ALU.is_gt, fill=0.0, base=0,
                               pattern=[[1, P]], channel_multiplier=-1)
            pool.affine_select(out=m.upper[:, 1, :], in_=m.upper[:, 1, :], compare_op=ALU.is_ge, fill=0.0, base=0,
                               pattern=[[1, P]], channel_multiplier=-1)
            pool.affine_select(out=m.lower[:], in_=m.lower[:], compare_op=ALU.is_gt, fill=0.0, base=0,
                               pattern=[[-1, P]], channel_multiplier=1)
            pool.iota(m.slot[:], pattern=[[0, 2], [1, SLOTS]], base=0, channel_multiplier=0, allow_small_or_imprecise_dtypes=True)
            pool.iota(m.row[:], pattern=[[P, NTT]], base=0, channel_multiplier=1, allow_small_or_imprecise_dtypes=True)
            pool.drain()
            pool.affine_select(out=m.valid[:], in_=m.valid[:], compare_op=ALU.is_gt, fill=0.0, base=NS,
                               pattern=[[0, 1]], channel_multiplier=-1)
            pool.drain()
            for b in range(BS):
                pool.affine_select(out=m.valid[:], in_=m.valid[:], compare_op=ALU.not_equal, fill=0.0, base=-SB * b,
                                   pattern=[[0, 1]], channel_multiplier=1)
                pool.drain()
            pool.memset(m.xlast[:], 0.0).then_inc(s_const, 1)

        @block.tensor
        def _(pe):
            pe.wait_ge(s_const, 1)
            for g, (sem, val, n, sources, _) in enumerate(groups):
                pe.wait_ge(sem, val)
                if g >= 8:
                    pe.wait_ge(s_e, g - 7)
                for k, src in enumerate(sources):
                    last = pe.transpose(m.ps[g % 8][:, k * n:(k + 1) * n] if src.shape[1] == P else None,
                                        src, m.ident[0:n, 0:n])
                last.then_inc(s_t, 1)

        @block.vector
        def _(dve):
            for g, (_, _, n, sources, out) in enumerate(groups):
                dve.wait_ge(s_t, g + 1)
                src = m.ps[g % 8][:, 0:n * len(sources)]
                if len(out.shape) == 3:
                    src = src.rearrange("p (k n) -> p k n", n=n)
                if len(out.shape) == 4:
                    src = src.rearrange("p (k b i) -> p k b i", k=KW, b=BS // 2)
                    for j in range(KW):
                        last = dve.tensor_copy(out[:, j], src[:, j])
                    last.then_inc(s_e, 1)
                    continue
                dve.tensor_copy(out, src).then_inc(s_e, 1)
            dve.wait_ge(s_e, len(groups))
            dve.memset(proj[:, :, 0:1], 0.0)


def stage_project(nc, m, io):
    xT, proj = m.at(O_XT, KD, NT), m.at(O_PROJ, N_PROJ, PW)
    ext, exs = m.at(O_EXT, KW, SEQ + BUF), m.at(O_EXS, KW, BS, TS + BUF)
    conv, wbuf, tmp = m.at(O_CONV, KW, NT), m.at(O_WBUF, 2, KD, P), m.at(O_TMP, NT)
    last_rows = m.at(O_TOP, 2, W)
    new_glu = m.at(O_TOP + 2 * W, KW, BS * TS)
    o = O_RATE
    memrow, memT = m.at(o, MT, D), m.at(o + MT * D, KD, NM)
    wkv = [m.at(o + 2 * MT * D + u * 4 * W, 4, W) for u in range(2)]
    kvrow = m.at(o + 2 * MT * D + 8 * W, MT, 2 * W)
    assert 3 * MT * D + 8 * W <= O_EXT - O_RATE
    w_in = io["w_in"][0].rearrange("(k p) n -> p k n", p=P)
    s_w = [m.sem(f"w_in_loaded_{u}") for u in range(2)]
    s_mm, s_free = m.sem("column_tile_done"), m.sem("column_banks_free")
    s_ev = m.sem("column_tile_copied")
    s_glu, s_gt, s_gc = m.sem("glu_done"), m.sem("glu_tail_turned"), m.sem("glu_tail_copied")

    with nc.Block() as block:
        @block.sync
        def _(sp):
            def load(n, col):
                sp.dma_start(wbuf[:, n % 2], w_in[:, :, ds(col, P)]).then_inc(s_w[n % 2], 16)

            load(0, OFF_GLU)
            load(1, OFF_GLU + P)
            for t0, tn, col in ((2, N_GLU - 2, OFF_GLU + 2 * P), (T_RW, N_RW, 0), (T_Q, N_Q, OFF_Q)):
                with sp.Fori(0, tn // 2) as i:
                    for u in range(2):
                        sp.wait_ge(s_mm, 2 * i + t0 + u - 1)
                        sp.dma_start(wbuf[:, u], w_in[:, :, ds((2 * i + u) * P + col, P)]).then_inc(s_w[u], 16)
            for t in range(MT):
                sp.dma_start(memrow[:, t, :], io["mem_prompt"][0, t * P:(t + 1) * P, :]).then_inc(m.sem("mem_loaded"), 16)
            w = io["w_mem_kv"][0].rearrange("(k p) n -> p k n", p=P)
            for n in range(4):
                if n >= 2:
                    sp.wait_ge(m.sem("mem_weights_used"), n - 1)
                sp.dma_start(wkv[n % 2], w[:, 4 * (n % 2):4 * (n % 2) + 4, (n // 2) * W:(n // 2 + 1) * W])\
                  .then_inc(m.sem(f"mem_weights_{n % 2}"), 16)
            sp.wait_ge(s_gc, 1)
            sp.dma_start(io["out_conv_p"][0, 0], last_rows[0:BUF, 0, :]).then_inc(m.sem("outputs_written"), 16)
            for b in range(BS):
                sp.dma_start(io["out_conv_s"][0, b, BUF - TS:BUF, :], last_rows[b * TS:(b + 1) * TS, 1, :])\
                  .then_inc(m.sem("outputs_written"), 16)
            sp.wait_ge(m.sem("mem_rows_copied"), 4)
            for t in range(MT):
                for x, name in enumerate(("out_mk", "out_mv")):
                    sp.dma_start(io[name][0, 0, t * P:(t + 1) * P].rearrange("m h d -> m (h d)"),
                                 kvrow[:, t, x * W:(x + 1) * W]).then_inc(m.sem("outputs_written"), 16)
            sp.wait_ge(m.sem("outputs_written"), 16 * OUT_PROJECT)

        @block.tensor
        def _(pe):
            with pe.Fori(0, N_PROJ // 2) as i:
                for u in range(2):
                    pe.wait_ge(s_w[u], 16 * i + 16)
                    pe.wait_ge(s_free, 2 * i + u + 1)
                    for k in range(KD):
                        for h in range(2):
                            mm = pe.matmul(m.ps[2 * u + h][:, 0:HALF], wbuf[:, u, k, :],
                                           xT[:, k, h * HALF:(h + 1) * HALF], start=(k == 0), stop=(k == KD - 1))
                    mm.then_inc(s_mm, 1)
            pe.wait_ge(s_glu, 1)
            for j in range(KW):
                pe.transpose(m.ps[4][0:BUF, j * P:(j + 1) * P], ext[:, j, SEQ:SEQ + BUF], m.ident[:, :])
            for j in range(KW):
                last = pe.transpose(m.ps[5][0:BS * TS, j * P:(j + 1) * P], new_glu[:, j, :], m.ident[:, :])
            last.then_inc(s_gt, 1)
            pe.wait_ge(m.sem("mem_loaded"), 32)
            pe.wait_ge(s_ev, N_PROJ)
            for g in range(4):
                for k in range(4):
                    c = 4 * (g % 2) + k
                    mm = pe.transpose(m.ps[g][:, k * P:(k + 1) * P], memrow[:, g // 2, c * P:(c + 1) * P], m.ident[:, :])
                mm.then_inc(m.sem("mem_turned"), 1)
            pe.wait_ge(m.sem("memT_ready"), 4)
            pe.wait_ge(s_gc, 1)
            for n in range(4):
                pe.wait_ge(m.sem(f"mem_weights_{n % 2}"), 16 * (n // 2 + 1))
                for t in range(MT):
                    for k in range(4):
                        mm = pe.matmul(m.ps[4 + 2 * (n // 2) + t][:, :], memT[:, 4 * (n % 2) + k, t * P:(t + 1) * P],
                                       wkv[n % 2][:, k, :], start=(n % 2 == 0 and k == 0), stop=(n % 2 == 1 and k == 3))
                mm.then_inc(m.sem("mem_weights_used"), 1)

        @block.scalar
        def _(act):
            act.sem_inc(s_free, 2)

            def copy_tiles(first, count, func):
                with act.Fori(0, count // 2) as i:
                    for u in range(2):
                        act.wait_ge(s_mm, 2 * i + first + u + 1)
                        act.activation(proj[:, ds(2 * i + first + u, 1), 1:1 + HALF], m.ps[2 * u][:, 0:HALF], func)
                        act.activation(proj[:, ds(2 * i + first + u, 1), 1 + HALF:PW], m.ps[2 * u + 1][:, 0:HALF], func)\
                           .then_inc(s_ev, 1)
                        act.wait_ge(s_ev, 2 * i + first + u + 1)
                        act.sem_inc(s_free, 1)

            copy_tiles(T_GLU, KW, ACT.Copy)
            copy_tiles(T_GLU + KW, KW, ACT.Sigmoid)
            copy_tiles(T_RW, N_RW + N_Q, ACT.Copy)
            act.wait_ge(s_gt, 1)
            act.activation(last_rows[0:BUF, 0, :], m.ps[4][0:BUF, :], ACT.Copy)
            act.activation(last_rows[0:BS * TS, 1, :], m.ps[5][0:BS * TS, :], ACT.Copy).then_inc(s_gc, 1)
            for g in range(4):
                act.wait_ge(m.sem("mem_turned"), g + 1)
                act.activation(memT[:, 4 * (g % 2):4 * (g % 2) + 4, (g // 2) * P:(g // 2 + 1) * P],
                               m.ps[g][:, :].rearrange("p (k n) -> p k n", k=4), ACT.Copy).then_inc(m.sem("memT_ready"), 1)
            for half in range(2):
                act.wait_ge(m.sem("mem_weights_used"), 2 * half + 2)
                for t in range(MT):
                    act.activation(kvrow[:, t, half * W:(half + 1) * W], m.ps[4 + 2 * half + t][:, :], ACT.Copy)\
                       .then_inc(m.sem("mem_rows_copied"), 1)

        @block.vector
        def _(dve):
            dve.wait_ge(s_ev, N_GLU)
            for j in range(KW):
                a, g = proj[:, T_GLU + j, :], proj[:, T_GLU + KW + j, :]
                dve.tensor_tensor(ext[:, j, BUF:], a[:, 1:1 + SEQ], g[:, 1:1 + SEQ], ALU.mult)
                dve.tensor_tensor(exs[:, j, :, BUF:], sample_cols(a[:, 1 + SEQ:PW]),
                                  sample_cols(g[:, 1 + SEQ:PW]), ALU.mult)
                last = dve.tensor_tensor(new_glu[:, j, :].rearrange("p (b t) -> p b t", b=BS),
                                         sample_cols(a[:, 1 + SEQ:PW]), sample_cols(g[:, 1 + SEQ:PW]), ALU.mult)
            last.then_inc(s_glu, 1)
            dve.memset(conv[:, :, SEQ:NT], 0.0)
            dve.wait_ge(s_glu, 1)
            dve.drain()
            for j in range(KW):
                dve.tensor_scalar(conv[:, j, 0:SEQ], ext[:, j, 0:SEQ], m.taps[:, j:j + 1],
                                  m.vec[:, V_CB + j:V_CB + j + 1], ALU.mult, ALU.add)
                dve.tensor_scalar(sample_cols(conv[:, j, SEQ:NT]), exs[:, j, :, 0:TS], m.taps[:, j:j + 1],
                                  m.vec[:, V_CB + j:V_CB + j + 1], ALU.mult, ALU.add)
            dve.drain()
            with dve.Fori(1, TAPS) as k:
                for j in range(KW):
                    tap = m.taps[:, ds(k * KW + j, 1)]
                    dve.scalar_tensor_tensor(out=conv[:, j, 0:SEQ], in0=ext[:, j, ds(k, SEQ)], scalar=tap,
                                             in1=conv[:, j, 0:SEQ], op0=ALU.mult, op1=ALU.add)
                    dve.scalar_tensor_tensor(out=sample_cols(conv[:, j, SEQ:NT]), in0=exs[:, j, :, ds(k, TS)], scalar=tap,
                                             in1=sample_cols(conv[:, j, SEQ:NT]), op0=ALU.mult, op1=ALU.add)
                dve.drain()
            with dve.Fori(0, N_RW) as j:
                dve.wait_ge(s_ev, j + T_RW + 1)
                tile = proj[:, ds(j + T_RW, 1), :]
                t = tmp.rearrange("p (a n) -> p a n", a=1)
                dve.tensor_tensor(t, tile[:, :, 0:NT], tile[:, :, 1:PW], ALU.subtract)
                dve.drain()
                dve.scalar_tensor_tensor(out=tile[:, :, 1:PW], in0=t, scalar=m.vec[:, ds(j + V_MU, 1)],
                                         in1=tile[:, :, 1:PW], op0=ALU.mult, op1=ALU.add)
                dve.drain()


O_UP = O_PROJ
O_DOWN = O_PROJ + KW * SEQ
O_BEFORE = O_EXT
SVALS = 6 * HD
O_SV = (O_PROJ + T_WA * PW, O_CONV - 2 * SVALS)
O_SVH = O_SV[0] + 2 * SVALS
O_SY = O_SV[1] - TS * HD // 2
O_SSTATE = O_WBUF + 1024
assert O_SY >= O_EXT + KW * NT and O_SSTATE + HD * HD // 2 <= O_TOP
assert O_SVH + (TS + 1) * HD // 2 <= O_PROJ + (T_G + 1) * PW


def stage_prepare(nc, m, io):
    proj = m.at(O_PROJ, N_PROJ, PW)
    rec, key, val = (proj[:, t:t + KW, 1:PW] for t in (T_R, T_K, T_V))
    rate, agate, outg = m.at(O_RATE, KW, NT), m.at(O_AGATE, KW, NT), m.at(O_OUTG, KW, NT)
    kkey, bkey = m.at(O_KKEY, KW, NT), m.at(O_BKEY, KW, NT)
    up, down, before = m.at(O_UP, KW, SEQ), m.at(O_DOWN, KW, SEQ), m.at(O_BEFORE, KW, NT)
    t1 = before
    w_wa, w_g = m.at(O_WBUF, W), m.at(O_WBUF + W, W)
    restart, one_ka = m.at(O_WBUF + 2 * W, SEQ), m.at(O_TMP, KW)
    t2, decay_s = m.at(O_TOP, KW, NT), m.at(O_TOP + KW * NT, KW, NS)
    rows = m.at(O_TOP + KW * NT + KW * NS, 6, W)
    sem = m.sem
    s_w, s_in = sem("lora_weights"), sem("lora_inputs")
    s_mm, s_ev = sem("prepare_product"), sem("prepare_copied")
    halves = [(h * HALF, (h + 1) * HALF) for h in range(2)]

    with nc.Block() as block:
        @block.sync
        def _(sp):
            sp.dma_start(w_wa[0:64, :], io["w_up"][0]).then_inc(s_w, 16)
            sp.dma_start(w_wa[64:128, :], io["a_up"][0]).then_inc(s_w, 16)
            sp.dma_start(w_g, io["g_up"][0]).then_inc(s_w, 16)
            sp.wait_ge(sem("sample_rows_copied"), 6)
            for q in range(6):
                sp.dma_start(io["sample_vectors"][:, :, q, :].rearrange("h r i -> r h i"),
                             rows[0:NS, q, :].rearrange("r (h i) -> r h i", i=HD)).then_inc(sem("sample_vectors_out"), 16)
            sp.wait_ge(sem("sample_vectors_out"), 96)

        @block.tensor
        def _(pe):
            g = 0

            def banks():
                if g >= 4:
                    pe.wait_ge(s_ev, g - 3)
                return [m.ps[2 * (g % 4) + h][:, 0:HALF] for h in range(2)]

            pe.wait_ge(s_w, 48)
            pe.wait_ge(s_in, 1)
            for j in range(KW):
                for w, x, r in ((w_wa, T_WA, slice(0, 64)), (w_wa, T_WA, slice(64, 128)), (w_g, T_G, slice(0, 128))):
                    for out, (a, b) in zip(banks(), halves):
                        mm = pe.matmul(out, w[r, j * P:(j + 1) * P], proj[r, x, 1 + a:1 + b], start=True, stop=True)
                    mm.then_inc(s_mm, 1)
                    g += 1
            for ready, src in (("key_squares", t1), ("bonus_terms", t2)):
                pe.wait_ge(sem(ready), 1)
                for j in range(KW):
                    for out, (a, b) in zip(banks(), halves):
                        mm = pe.matmul(out, m.heads[:, :], src[:, j, a:b], start=True, stop=True)
                    mm.then_inc(s_mm, 1)
                    g += 1
            pe.wait_ge(s_ev, g)
            pe.wait_ge(sem("sample_decay"), 1)
            for q, src in enumerate((rec, None, key, val, kkey, bkey)):
                for j in range(KW):
                    mm = pe.transpose(m.ps[q][0:NS, j * P:(j + 1) * P],
                                      decay_s[:, j, :] if src is None else src[:, j, SEQ:NT], m.ident[:, :])
                mm.then_inc(sem("sample_rows"), 1)

        @block.scalar
        def _(act):
            act.activation(proj[0:64, T_WA, 1:PW], proj[0:64, T_WA, 1:PW], ACT.Tanh)
            act.activation(proj[:, T_G, 1:PW], proj[:, T_G, 1:PW], ACT.Sigmoid).then_inc(s_in, 1)
            g = 0
            for j in range(KW):
                for out, func, vec in ((rate, ACT.Sigmoid, V_W0), (agate, ACT.Sigmoid, V_A0), (outg, ACT.Copy, None)):
                    act.wait_ge(s_mm, g + 1)
                    for h, (a, b) in enumerate(halves):
                        src = m.ps[2 * (g % 4) + h][:, 0:HALF]
                        if vec is None:
                            last = act.activation(out[:, j, a:b], src, func)
                        else:
                            last = act.activation(out[:, j, a:b], src, func, bias=m.vec[:, vec + j:vec + j + 1])
                    last.then_inc(s_ev, 1)
                    g += 1
            act.wait_ge(sem("key_sums"), 1)
            act.activation(t1, t1, ACT.Sqrt).then_inc(sem("key_norms"), 1)
            act.wait_ge(sem("rates_cumulated"), 1)
            act.activation(up, t1[:, :, 0:SEQ], ACT.Exp)
            act.activation(down, t1[:, :, 0:SEQ], ACT.Exp, scale=-1.0)
            act.activation(decay_s, rate[:, :, SEQ:NT], ACT.Exp, scale=-1.0).then_inc(sem("sample_decay"), 1)
            act.wait_ge(sem("rates_before"), 1)
            act.drain()
            act.activation(before[:, :, 0:SEQ], t2[:, :, 0:SEQ], ACT.Exp, scale=-1.0)
            for q in range(6):
                act.wait_ge(sem("sample_rows"), q + 1)
                act.activation(rows[0:NS, q, :], m.ps[q][0:NS, :], ACT.Copy).then_inc(sem("sample_rows_copied"), 1)

        @block.vector
        def _(dve):
            for j in range(KW):
                dve.tensor_scalar(kkey[:, j, :], key[:, j, :], m.vec[:, V_KK + j:V_KK + j + 1], None, ALU.mult)
            dve.tensor_scalar(one_ka, m.vec[:, V_KA:V_KA + KW], -1.0, 1.0, ALU.mult, ALU.add)
            dve.memset(restart, 1.0)
            dve.drain()
            dve.memset(restart[:, 0:SEQ:CH], 0.0)
            dve.tensor_tensor(t1, kkey, kkey, ALU.mult).then_inc(sem("key_squares"), 1)
            dve.wait_ge(s_ev, 12)
            for j in range(KW):
                dve.tensor_scalar(t2[:, j, :], agate[:, j, :], m.vec[:, V_KA + j:V_KA + j + 1], one_ka[:, j:j + 1],
                                  ALU.mult, ALU.add)
            dve.tensor_scalar(rate, rate, RATE, None, ALU.mult)
            dve.drain()
            dve.tensor_tensor(key, key, t2, ALU.mult)
            for j in range(KW):
                dve.wait_ge(s_mm, 13 + j)
                for h, (a, b) in enumerate(halves):
                    last = dve.tensor_scalar(t1[:, j, a:b], m.ps[2 * ((12 + j) % 4) + h][:, 0:HALF], 1e-24, None, ALU.max)
                last.then_inc(s_ev, 1)
            dve.wait_ge(s_ev, 16)
            dve.sem_inc(sem("key_sums"), 1)
            dve.drain()
            dve.tensor_tensor(t2, rec, key, ALU.mult)
            dve.drain()
            for j in range(KW):
                last = dve.tensor_scalar(t2[:, j, :], t2[:, j, :], m.vec[:, V_RK + j:V_RK + j + 1], None, ALU.mult)
            last.then_inc(sem("bonus_terms"), 1)
            dve.wait_ge(sem("key_norms"), 1)
            dve.reciprocal(t1, t1)
            dve.drain()
            dve.tensor_tensor(kkey, kkey, t1, ALU.mult)
            dve.drain()
            dve.tensor_tensor(bkey, kkey, agate, ALU.mult)
            dve.drain()
            for j in range(KW):
                last = dve.tensor_tensor_scan(t1[:, j, 0:SEQ], restart, rate[:, j, 0:SEQ], 0.0, ALU.mult, ALU.add)
            last.then_inc(sem("rates_cumulated"), 1)
            for j in range(KW):
                dve.wait_ge(s_mm, 17 + j)
                for h, (a, b) in enumerate(halves):
                    last = dve.tensor_tensor(agate[:, j, a:b], m.ps[2 * ((16 + j) % 4) + h][:, 0:HALF], val[:, j, a:b],
                                             ALU.mult)
                last.then_inc(s_ev, 1)
            dve.wait_ge(s_ev, 20)
            dve.tensor_tensor(t2[:, :, 0:SEQ], t1[:, :, 0:SEQ], rate[:, :, 0:SEQ], ALU.subtract)\
               .then_inc(sem("rates_before"), 1)


def stage_wkv(nc, m, io):
    proj = m.at(O_PROJ, N_PROJ, PW)
    rec, key, val = (proj[:, t:t + KW, 1:PW] for t in (T_R, T_K, T_V))
    yout = rec
    kkey, bkey = m.at(O_KKEY, KW, NT), m.at(O_BKEY, KW, NT)
    up, down, before = m.at(O_UP, KW, SEQ), m.at(O_DOWN, KW, SEQ), m.at(O_BEFORE, KW, NT)
    o = O_TOP
    bd_qr = [m.at(o + u * 2560, KW, 2, P) for u in range(2)]
    bd_b = [m.at(o + u * 2560 + 1024, KW, P) for u in range(2)]
    bd_k = [m.at(o + u * 2560 + 1536, KW, P) for u in range(2)]
    bd_v = [m.at(o + u * 2560 + 2048, KW, P) for u in range(2)]
    o += 5120
    nr, o = m.at(o, KW, 2, P), o + 1024
    amat, o = m.at(o, KW, P), o + 512
    kr, o = m.at(o, KW, 2, P), o + 1024
    vb, o = m.at(o, KW, 3 * HD), o + 768
    kt, o = m.at(o, KW, P), o + 512
    rinv, o = m.at(o, KW, P), o + 512
    powers, o = [m.at(o + u * 1024, KW, 2, P) for u in range(2)], o + 2048
    rhs, o = m.at(o, KW, HD), o + 256
    sa, o = m.at(o, KW, HD), o + 256
    assert o <= ARENA
    state, sdec = m.at(O_WBUF, KW, HD), m.at(O_WBUF + 256, KW, HD)
    ydiag = m.at(O_WBUF + 512, KW, P)
    sout = m.at(O_TOP, KW, P)
    LEVELS = 5
    sem = m.sem
    s_bd, s_v = sem("chunk_vectors"), sem("chunk_values")
    s_gram, s_mask, s_kr, s_vb = sem("gram"), sem("gram_masked"), sem("gram_kr"), sem("tokens_vb")
    s_sq, s_na, s_prod, s_r = sem("squared"), sem("squared_copied"), sem("inverse_product"), sem("inverse_grown")
    s_u, s_un, s_sa, s_sac = sem("rhs_done"), sem("rhs_copied"), sem("sa_done"), sem("sa_copied")
    s_y, s_yd, s_yt, s_yc = sem("y_done"), sem("y_spread"), sem("y_turned"), sem("y_copied")
    s_st, s_sd = sem("state_product"), sem("state_done")

    def a(p):
        return m.ps[p]

    def b(p):
        return m.ps[KW + p]

    def chunks(eng, body):
        with eng.Fori(0, NCH // 2 - 1) as i:
            for u in range(2):
                body(2 * i + u, u, True)
        body(NCH - 2, 0, True)
        body(NCH - 1, 1, False)

    R32 = HD // 2
    sv2 = [m.at(x, 2, 6, HD) for x in O_SV]
    vh, ssa = m.at(O_SVH, TS, R32), m.at(O_SVH + TS * R32, R32)
    sy, st, stmp = m.at(O_SY, TS, R32), m.at(O_SSTATE, R32, HD), m.sample_tmp

    with nc.Block() as block:
        @block.sync
        def _(sp):
            vectors = io["sample_vectors"].rearrange("h (b s) q i -> (h b) (s q i)", s=SB)
            for v in range(2):
                for x in range(2):
                    sp.dma_start(sv2[x][64 * v:64 * v + 64].rearrange("p t q i -> p (t q i)"),
                                 vectors[:, (1 + 2 * x) * SVALS:(3 + 2 * x) * SVALS]).then_inc(sem("sample_in"), 16)
                for h in range(8):
                    sp.dma_start(st[64 * v + 8 * h:64 * v + 8 * h + 8].rearrange("p a b -> p (a b)"),
                                 io["state_wkv"][0, :, h, v * R32:(v + 1) * R32, :].rearrange("b v k -> b (v k)"))\
                      .then_inc(sem("sample_in"), 16)

        @block.gpsimd
        def _(pool):
            for x in (*bd_qr, *bd_b, *bd_k, *bd_v, ydiag, state):
                pool.memset(x, 0.0)
            pool.drain()
            pool.memset(yout[:, :, SEQ:NT], 0.0).then_inc(sem("wkv_zeroed"), 1)

            def row_sums(out):
                n = HD // 2
                while n > 1:
                    pool.tensor_tensor(stmp[:, :, 0:n], stmp[:, :, 0:n], stmp[:, :, n:2 * n], ALU.add)
                    pool.drain()
                    n //= 2
                pool.tensor_tensor(out, stmp[:, :, 0], stmp[:, :, 1], ALU.add)

            def sample_step(t):
                sv = sv2[t // 2]

                def bk(q_):
                    return sv[:, t % 2, q_:q_ + 1, :].to_broadcast([P, 8, HD])

                for g in range(4):
                    rows = slice(8 * g, 8 * g + 8)
                    s = st[:, rows, :]

                    def bv(x):
                        return x.rearrange("p (v o) -> p v o", o=1).to_broadcast([P, 8, HD])

                    pool.tensor_tensor(stmp[:], s, bk(4), ALU.mult)
                    pool.drain()
                    pool.tensor_tensor(s, s, bk(1), ALU.mult)
                    row_sums(ssa[:, rows])
                    pool.drain()
                    pool.tensor_tensor(stmp[:], bk(5), bv(ssa[:, rows]), ALU.mult)
                    pool.drain()
                    pool.tensor_tensor(s, s, stmp[:], ALU.subtract)
                    pool.drain()
                    pool.tensor_tensor(stmp[:], bk(2), bv(vh[:, t, rows]), ALU.mult)
                    pool.drain()
                    pool.tensor_tensor(s, s, stmp[:], ALU.add)
                    pool.drain()
                    pool.tensor_tensor(stmp[:], s, bk(0), ALU.mult)
                    pool.drain()
                    row_sums(sy[:, t, rows])
                    pool.drain()

            pool.wait_ge(sem("sample_in"), 16 * 20)
            for v in range(2):
                pool.drain()
                for t in range(TS):
                    pool.tensor_copy(vh[64 * v:64 * v + 64, t], sv2[t // 2][64 * v:64 * v + 64, t % 2, 3, v * R32:(v + 1) * R32])
            pool.drain()
            for t in range(TS):
                sample_step(t)

        @block.tensor
        def _(pe):
            def chunk(n, u, more):
                pe.wait_ge(s_bd, n + 1)
                pe.wait_ge(s_v, n + 1)
                for p in range(KW):
                    pe.wait_ge(s_sd, 4 * n + p + 1)
                    pe.matmul(a(p)[:, 0:256], bd_b[u][:, p, :], bd_qr[u][:, p].rearrange("p q t -> p (q t)"), start=True, stop=True)
                    pe.matmul(a(p)[:, 256:384], bd_qr[u][:, p, 0, :], bd_b[u][:, p, :], start=True, stop=True)
                    pe.transpose(a(p)[:, 384:512], bd_k[u][:, p, :], m.ident[:, :])
                    pe.wait_ge(s_yc, 4 * n + p + 1)
                    pe.matmul(b(p)[:, 0:256], bd_k[u][:, p, :], bd_qr[u][:, p].rearrange("p q t -> p (q t)"), start=True, stop=True)
                    pe.matmul(b(p)[:, 256:320], bd_v[u][:, p, :], m.fold[:, :], start=True, stop=True)
                    pe.transpose(b(p)[:, 320:448], bd_b[u][:, p, :], m.ident[:, :]).then_inc(s_gram, 1)
                for lv in range(LEVELS):
                    at = lv * KW + 1 - KW
                    for p in range(KW):
                        if lv == 0:
                            pe.wait_ge(s_mask, 4 * n + p + 1)
                            nn, aa = nr[:, p, 0, :], amat[:, p, :]
                        else:
                            pe.wait_ge(s_na, 20 * n + at + p)
                            nn, aa = powers[(lv - 1) % 2][:, p, 0, :], powers[(lv - 1) % 2][:, p, 1, :]
                        pe.matmul(a(p)[:, 0:128], aa, nn, start=True, stop=True)
                        pe.matmul(a(p)[:, 128:256], nn, aa, start=True, stop=True).then_inc(s_sq, 1)
                    for p in range(KW):
                        pe.wait_ge(s_na, 20 * n + at + KW + p)
                        if lv == 0:
                            pe.wait_ge(s_vb, 4 * n + p + 1)
                        else:
                            pe.wait_ge(s_r, 20 * n + at + p)
                        pe.matmul(b(p)[:, 0:128], powers[lv % 2][:, p, 1, :], rinv[:, p, :], start=True, stop=True)\
                          .then_inc(s_prod, 1)
                for p in range(KW):
                    pe.matmul(a(p)[:, 0:64], bd_qr[u][:, p, 0, :], state[:, p, :], start=True, stop=False)
                    pe.matmul(a(p)[:, 0:64], kr[:, p, 0, :], vb[:, p, 0:HD], start=False, stop=True).then_inc(s_u, 1)
                for p in range(KW):
                    pe.wait_ge(s_r, 20 * n + KW * (LEVELS - 1) + p + 1)
                    pe.matmul(b(p)[:, 0:64], bd_qr[u][:, p, 1, :], state[:, p, :], start=True, stop=False)
                    pe.matmul(b(p)[:, 0:64], kr[:, p, 1, :], vb[:, p, 0:HD], start=False, stop=False)
                    pe.wait_ge(s_un, 4 * n + p + 1)
                    pe.matmul(a(p)[:, 64:128], rinv[:, p, :], rhs[:, p, :], start=True, stop=True).then_inc(s_sa, 1)
                for p in range(KW):
                    pe.wait_ge(s_sac, 4 * n + p + 1)
                    pe.matmul(b(p)[:, 0:64], nr[:, p, 1, :], sa[:, p, :], start=False, stop=True).then_inc(s_y, 1)
                    pe.matmul(a(p)[:, 128:192], vb[:, p, HD:3 * HD], sa[:, p, :], start=True, stop=False)
                    pe.matmul(a(p)[:, 128:192], kt[:, p, :], vb[:, p, 0:HD], start=False, stop=True).then_inc(s_st, 1)
                for p in range(KW):
                    pe.wait_ge(s_yd, 4 * n + p + 1)
                    pe.matmul(b(p)[:, 64:128], ydiag[:, p, :], m.fold[:, :], start=True, stop=True).then_inc(s_yt, 1)

            pe.wait_ge(sem("wkv_zeroed"), 1)
            chunks(pe, chunk)
            pe.wait_ge(s_sd, 4 * NCH + 4)
            for p in range(KW):
                last = pe.transpose(m.ps[0][0:HD, p * P:(p + 1) * P], state[:, p, :], m.ident[:, :])
            last.then_inc(sem("state_turned"), 1)

        @block.scalar
        def _(act):
            def values(n, u):
                for h in range(2):
                    r = slice(h * HD, (h + 1) * HD)
                    last = act.activation(bd_v[u][r, :, r], val[r, :, ds(n * CH, CH)], ACT.Copy)
                last.then_inc(s_v, 1)

            def chunk(n, u, more):
                if more:
                    values(n + 1, 1 - u)
                for p in range(KW):
                    act.wait_ge(s_kr, 4 * n + p + 1)
                    act.activation(vb[:, p, :], b(p)[:, 256:448], ACT.Copy).then_inc(s_vb, 1)
                for lv in range(LEVELS):
                    for p in range(KW):
                        act.wait_ge(s_sq, 20 * n + KW * lv + p + 1)
                        act.activation(powers[lv % 2][:, p].rearrange("p q t -> p (q t)"), a(p)[:, 0:256], ACT.Copy)\
                           .then_inc(s_na, 1)
                for p in range(KW):
                    act.wait_ge(s_u, 4 * n + p + 1)
                    act.activation(rhs[:, p, :], a(p)[:, 0:64], ACT.Copy, scale=-1.0).then_inc(s_un, 1)
                for p in range(KW):
                    act.wait_ge(s_sa, 4 * n + p + 1)
                    act.activation(sa[:, p, :], a(p)[:, 64:128], ACT.Copy).then_inc(s_sac, 1)
                for p in range(KW):
                    act.wait_ge(s_y, 4 * n + p + 1)
                    act.activation(ydiag[0:HD, p, 0:HD], b(p)[0:HD, 0:64], ACT.Copy)
                    act.activation(ydiag[HD:P, p, HD:P], b(p)[HD:P, 0:64], ACT.Copy).then_inc(s_yd, 1)
                for p in range(KW):
                    act.wait_ge(s_yt, 4 * n + p + 1)
                    act.activation(yout[:, p, ds(n * CH, CH)], b(p)[:, 64:128], ACT.Copy).then_inc(s_yc, 1)

            act.sem_inc(s_yc, 4)
            act.wait_ge(sem("wkv_zeroed"), 1)
            values(0, 0)
            chunks(act, chunk)
            act.wait_ge(sem("state_turned"), 1)
            act.activation(sout[0:HD].rearrange("p a b -> p (a b)"), m.ps[0][0:HD, :], ACT.Copy).then_inc(sem("state_rows"), 1)
            act.wait_ge(sem("state_rows"), 1)
            act.dma_start(io["out_wkv_p"][0, 0].rearrange("h v k -> v h k"),
                          sout[0:HD].rearrange("p a (b k) -> p (a b) k", k=HD)).then_inc(sem("outputs_written"), 16)
            act.wait_ge(sem("outputs_written"), 16 * OUT_WKV)

        @block.vector
        def _(dve):
            def vectors(n, u):
                cols = ds(n * CH, CH)
                for h in range(2):
                    r = slice(h * HD, (h + 1) * HD)
                    dve.tensor_tensor(bd_b[u][r, :, r], bkey[r, :, cols], up[r, :, cols], ALU.mult)
                    dve.tensor_tensor(bd_k[u][r, :, r], key[r, :, cols], up[r, :, cols], ALU.mult)
                    dve.tensor_tensor(bd_qr[u][r, :, 0, r], kkey[r, :, cols], before[r, :, cols], ALU.mult)
                    last = dve.tensor_tensor(bd_qr[u][r, :, 1, r], rec[r, :, cols], down[r, :, cols], ALU.mult)
                last.then_inc(s_bd, 1)

            def chunk(n, u, more):
                for p in range(KW):
                    dve.wait_ge(s_gram, 4 * n + p + 1)
                    dve.tensor_tensor(nr[:, p], a(p)[:, 0:256].rearrange("p (q t) -> p q t", q=2), m.upper[:], ALU.mult)
                    dve.tensor_tensor(amat[:, p, :], a(p)[:, 256:384], m.lower[:], ALU.mult)
                    dve.tensor_copy(kt[:, p, :], a(p)[:, 384:512])
                    dve.drain()
                    dve.tensor_tensor(rinv[:, p, :], m.ident[:], nr[:, p, 0, :], ALU.subtract).then_inc(s_mask, 1)
                    dve.tensor_tensor(kr[:, p], b(p)[:, 0:256].rearrange("p (q t) -> p q t", q=2), m.upper[:], ALU.mult)\
                       .then_inc(s_kr, 1)
                if more:
                    vectors(n + 1, 1 - u)
                for lv in range(LEVELS):
                    for p in range(KW):
                        dve.wait_ge(s_prod, 20 * n + KW * lv + p + 1)
                        dve.tensor_tensor(rinv[:, p, :], b(p)[:, 0:128], rinv[:, p, :], ALU.add).then_inc(s_r, 1)
                for p in range(KW):
                    dve.tensor_scalar(sdec[:, p, :], state[:, p, :], down[:, p, ds(n * CH + CH - 1, 1)], None, ALU.mult)
                dve.drain()
                for p in range(KW):
                    dve.wait_ge(s_st, 4 * n + p + 1)
                    dve.scalar_tensor_tensor(out=state[:, p, :], in0=a(p)[:, 128:192],
                                             scalar=down[:, p, ds(n * CH + CH - 1, 1)],
                                             in1=sdec[:, p, :], op0=ALU.mult, op1=ALU.add).then_inc(s_sd, 1)

            dve.sem_inc(s_sd, 4)
            dve.wait_ge(sem("wkv_zeroed"), 1)
            vectors(0, 0)
            chunks(dve, chunk)


WKV_ONLY = ("chunk_vectors", "chunk_values", "gram", "gram_masked", "gram_kr", "tokens_vb", "squared", "squared_copied",
            "inverse_product", "inverse_grown", "rhs_done", "rhs_copied", "sa_done", "sa_copied", "y_done", "y_spread",
            "y_turned", "y_copied", "state_product", "state_done", "state_turned", "state_rows", "wkv_zeroed",
            "lora_inputs", "prepare_product", "prepare_copied", "key_squares", "key_sums", "key_norms", "rates_before",
            "rates_cumulated", "sample_decay", "sample_rows", "sample_rows_copied", "bonus_terms")


O_ATT = O_RATE


def stage_attend(nc, m, io):
    proj = m.at(O_PROJ, N_PROJ, PW)
    q = proj[:, T_Q:T_Q + MH, 1:PW]
    yv = proj[:, T_R:T_R + KW, 1:PW]
    att = m.at(O_ATT, MH, NT)
    vcache = m.at(O_TOP, BS, MT, W)
    kcache = [m.at(O_TOP + 8192 + u * 1024, MT, W) for u in range(2)]
    kcT = [m.at(O_TOP + 10240 + u * 1024, MH, NM) for u in range(2)]
    kvrow = m.at(O_PROJ + T_K * PW, MT, 2 * W)
    assert T_K * PW + MT * D <= T_Q * PW
    o = O_KKEY
    kT, o = m.at(o, MH, NM), o + 1024
    probs, o = m.at(o, 4, NM), o + 1024
    probsT, o = m.at(o, MT, SEQ), o + 1024
    srows, o = m.at(o, BS, P), o + 1024
    assert o <= O_BKEY + KW * NT
    sy, st = m.at(O_SY, TS, HD // 2), m.at(O_SSTATE, HD // 2, HD)
    syrow = m.at(O_EXT, W)
    stats = m.at(O_EXT + KW * NT, 24)
    smax, sneg, ssum, sinv = (m.at(O_EXT + W + x * BS, BS) for x in range(4))
    sprob = m.at(O_PROJ, BS, NM)
    sprobT = m.at(O_PROJ + BS * NM, BS, MT, P)
    assert 2 * BS * NM <= 2 * KW * PW
    WIN = 32
    assert O_EXT + KW * NT + 24 <= O_SY
    SCALE = float(P) ** -0.5
    sem = m.sem
    R32 = HD // 2

    with nc.Block() as block:
        @block.sync
        def _(sp):
            for t in range(MT):
                for x, name in enumerate(("out_mk", "out_mv")):
                    sp.dma_start(kvrow[:, t, x * W:(x + 1) * W],
                                 io[name][0, 0, t * P:(t + 1) * P].rearrange("m h d -> m (h d)")).then_inc(sem("mem_rows_loaded"), 16)
            sp.dma_start(io["sample_y"].rearrange("v h b t i -> (v h b) (t i)"), sy.rearrange("p t i -> p (t i)"))\
              .then_inc(sem("sample_y_out"), 16)
            kc = io["cache_mem_k"][0].rearrange("b (t p) h d -> b p t (h d)", p=P)
            vc = io["cache_mem_v"][0].rearrange("b (t p) h d -> b p t (h d)", p=P)
            for b in range(BS):
                if b >= 2:
                    sp.wait_ge(sem("key_cache_turned"), b - 1)
                sp.dma_start(kcache[b % 2], kc[b]).then_inc(sem(f"key_cache_{b % 2}"), 16)
                sp.dma_start(vcache[:, b], vc[b]).then_inc(sem("value_cache"), 16)
                if b == 3:
                    sp.wait_ge(sem("sample_y_out"), 16)
                    for v in range(2):
                        sp.dma_start(syrow[0:BS * TS].rearrange("p (h v i) -> p h v i", h=8, v=2)[:, :, v, :],
                                     io["sample_y"][v].rearrange("h b t i -> (b t) h i")).then_inc(sem("sample_y_rows"), 16)
            for v in range(2):
                for h in range(8):
                    sp.dma_start(io["out_wkv_s"][0, :, h, v * R32:(v + 1) * R32, :].rearrange("b v k -> b (v k)"),
                                 st[64 * v + 8 * h:64 * v + 8 * h + 8].rearrange("p a b -> p (a b)"))\
                      .then_inc(sem("sample_states_out"), 16)
            sp.wait_ge(sem("sample_states_out"), 16 * 16)

        @block.tensor
        def _(pe):
            pe.wait_ge(sem("mem_rows_loaded"), 64)
            for h in range(MH):
                for t in range(MT):
                    mm = pe.transpose(m.ps[h // 2][:, (h % 2) * NM + t * P:(h % 2) * NM + (t + 1) * P],
                                      kvrow[:, t, h * P:(h + 1) * P], m.ident[:, :])
            mm.then_inc(sem("kT_turned"), 1)
            pe.wait_ge(sem("kT_ready"), 2)

            def scores(h):
                if h >= 1:
                    pe.wait_ge(sem("scores_read"), h)
                for i in range(4):
                    mm = pe.matmul(m.ps[2 + i // 2][:, (i % 2) * NM:(i % 2 + 1) * NM], q[:, h, i * P:(i + 1) * P],
                                   kT[:, h, :], start=True, stop=True)
                mm.then_inc(sem("scores_done"), 1)

            def turn_probs(h):
                pe.wait_ge(sem("probs_ready"), h + 1)
                if h >= 1:
                    pe.wait_ge(sem("probsT_ready"), 2 * h)
                for t in range(MT):
                    for i in range(4):
                        mm = pe.transpose(m.ps[4 + t][:, i * P:(i + 1) * P], probs[:, i, t * P:(t + 1) * P], m.ident[:, :])
                mm.then_inc(sem("probs_turned"), 1)

            def mix_values(h):
                pe.wait_ge(sem("probsT_ready"), 2 * h + 2)
                if h >= 1:
                    pe.wait_ge(sem("att_copied"), h)
                for t in range(MT):
                    mm = pe.matmul(m.ps[6][:, :], kvrow[:, t, W + h * P:W + (h + 1) * P], probsT[:, t, :],
                                   start=(t == 0), stop=(t == MT - 1))
                mm.then_inc(sem("att_done"), 1)

            def sample_scores(b):
                pe.wait_ge(sem(f"key_cache_{b % 2}"), 16 * (b // 2 + 1))
                if b >= 1:
                    pe.wait_ge(sem("key_cacheT_ready"), 2 * b)
                for h in range(MH):
                    for t in range(MT):
                        mm = pe.transpose(m.ps[h // 2][:, (h % 2) * NM + t * P:(h % 2) * NM + (t + 1) * P],
                                          kcache[b % 2][:, t, h * P:(h + 1) * P], m.ident[:, :])
                mm.then_inc(sem("key_cache_turned"), 1)
                pe.wait_ge(sem("key_cacheT_ready"), 2 * b + 2)
                if b >= 2:
                    pe.wait_ge(sem("sprob_raw"), b - 1)
                end = SEQ + SB * (b + 1)
                for h in range(MH):
                    mm = pe.matmul(m.ps[7][h * WIN:(h + 1) * WIN, (b % 2) * NM:(b % 2 + 1) * NM], q[:, h, end - WIN:end],
                                   kcT[b % 2][:, h, :], start=True, stop=True)
                mm.then_inc(sem("sample_scores"), 1)

            for h in range(MH):
                scores(h)
                sample_scores(2 * h)
                turn_probs(h)
                sample_scores(2 * h + 1)
                mix_values(h)
            pe.wait_ge(sem("scores_read"), MH)
            pe.wait_ge(sem("probsT_ready"), 2 * MH)
            for g in range(4):
                pe.wait_ge(sem("sprob_ready"), 2 * g + 2)
                for b in (2 * g, 2 * g + 1):
                    for t in range(MT):
                        at = ((b % 2) * MT + t) * P
                        mm = pe.transpose(m.ps[2 + g][:, at:at + P], sprob[:, b, t * P:(t + 1) * P], m.ident[:, :])
                mm.then_inc(sem("sprob_turned"), 1)
            pe.wait_ge(sem("sprobT_ready"), 4)
            pe.wait_ge(sem("value_cache"), 16 * BS)
            for b in range(BS):
                for t in range(MT):
                    for h in range(MH):
                        mm = pe.matmul(m.ps[b // 4][h * WIN:(h + 1) * WIN, (b % 4) * P:(b % 4 + 1) * P],
                                       sprobT[:, b, t, h * WIN:(h + 1) * WIN], vcache[:, b, t, h * P:(h + 1) * P],
                                       start=(t == 0), stop=(t == MT - 1))
                if b % 4 == 3:
                    mm.then_inc(sem("sample_att"), 1)
            pe.wait_ge(sem("att_copied"), MH)
            pe.wait_ge(sem("sprob_raw"), BS)
            for b in range(BS):
                if b % 4 == 0:
                    pe.wait_ge(sem("sample_att_copied"), b // 4 + 1)
                mm = pe.transpose(m.ps[6 + b // 4][:, (b % 4) * P:(b % 4 + 1) * P], srows[:, b, :], m.ident[:, :])
                if b % 4 == 3:
                    mm.then_inc(sem("sample_att_turned"), 1)
            pe.wait_ge(sem("sample_y_rows"), 32)
            for j in range(KW):
                mm = pe.transpose(m.ps[0][:, j * 32:(j + 1) * 32], syrow[0:32, j * P:(j + 1) * P], m.ident[0:32, 0:32])
            mm.then_inc(sem("sample_y_turned"), 1)

        @block.scalar
        def _(act):
            act.wait_ge(sem("kT_turned"), 1)
            for g in range(2):
                act.activation(kT[:, 2 * g:2 * g + 2, :], m.ps[g][:, :].rearrange("p (k n) -> p k n", k=2), ACT.Copy)\
                   .then_inc(sem("kT_ready"), 1)

            def key_cacheT(b):
                act.wait_ge(sem("key_cache_turned"), b + 1)
                for g in range(2):
                    act.activation(kcT[b % 2][:, 2 * g:2 * g + 2, :], m.ps[g][:, :].rearrange("p (k n) -> p k n", k=2),
                                   ACT.Copy).then_inc(sem("key_cacheT_ready"), 1)

            def sample_exp(b):
                act.wait_ge(sem("sample_maxima"), b + 1)
                act.activation(sprob[:, b, :], m.ps[7][:, (b % 2) * NM:(b % 2 + 1) * NM], ACT.Exp, bias=sneg[:, b:b + 1],
                               scale=SCALE, accum_out=ssum[:, b:b + 1]).then_inc(sem("sprob_raw"), 1)

            for h in range(MH):
                key_cacheT(2 * h)
                act.wait_ge(sem("maxima"), h + 1)
                for i in range(4):
                    last = act.activation(probs[:, i, :], m.ps[2 + i // 2][:, (i % 2) * NM:(i % 2 + 1) * NM], ACT.Exp,
                                          bias=stats[:, i:i + 1], scale=SCALE, accum_out=stats[:, 8 + i:9 + i])
                last.then_inc(sem("scores_read"), 1)
                sample_exp(2 * h)
                key_cacheT(2 * h + 1)
                act.wait_ge(sem("probs_turned"), h + 1)
                for t in range(MT):
                    act.activation(probsT[:, t, :], m.ps[4 + t][:, :], ACT.Copy).then_inc(sem("probsT_ready"), 1)
                act.wait_ge(sem("att_done"), h + 1)
                act.activation(att[:, h, 0:SEQ], m.ps[6][:, :], ACT.Copy).then_inc(sem("att_copied"), 1)
                sample_exp(2 * h + 1)
            for g in range(2):
                act.wait_ge(sem("sprob_turned"), g + 1)
                act.activation(sprobT[:, 2 * g:2 * g + 2].rearrange("p b t n -> p (b t n)"), m.ps[2 + g][:, :], ACT.Copy)\
                   .then_inc(sem("sprobT_ready"), 1)
            for g in range(2):
                act.wait_ge(sem("sample_att"), g + 1)
                act.activation(srows[:, 4 * g:4 * g + 4, :].rearrange("p b d -> p (b d)"), m.ps[g][:, :], ACT.Copy)\
                   .then_inc(sem("sample_att_copied"), 1)
            act.wait_ge(sem("att_zeroed"), 1)
            for g in range(2):
                act.wait_ge(sem("sample_att_turned"), g + 1)
                at = SEQ + 4 * SB * g
                for h in range(MH):
                    act.activation(sample_cols(att[:, h, at:at + 4 * SB]),
                                   m.ps[6 + g][:, :].rearrange("p (b c) -> p b c", b=4)[:, :, (h + 1) * WIN - TS:(h + 1) * WIN],
                                   ACT.Copy)

        @block.vector
        def _(dve):
            def softmax_head(h):
                dve.wait_ge(sem("scores_done"), h + 1)
                for g in range(2):
                    dve.tensor_reduce(stats[:, 4 + 2 * g:6 + 2 * g], m.ps[2 + g][:, :].rearrange("p (k n) -> p k n", k=2),
                                      AX.X, ALU.max)
                dve.drain()
                if h >= 1:
                    dve.wait_ge(sem("probs_turned"), h)
                dve.tensor_scalar(stats[:, 0:4], stats[:, 4:8], -SCALE, None, ALU.mult).then_inc(sem("maxima"), 1)

            def normalise_head(h):
                dve.wait_ge(sem("scores_read"), h + 1)
                dve.reciprocal(stats[:, 12:16], stats[:, 8:12])
                dve.drain()
                for i in range(4):
                    last = dve.tensor_scalar(probs[:, i, :], probs[:, i, :], stats[:, 12 + i:13 + i], None, ALU.mult)
                last.then_inc(sem("probs_ready"), 1)

            def sample_max(b):
                dve.wait_ge(sem("sample_scores"), b + 1)
                dve.tensor_reduce(smax[:, b:b + 1], m.ps[7][:, (b % 2) * NM:(b % 2 + 1) * NM], AX.X, ALU.max)
                dve.drain()
                dve.tensor_scalar(sneg[:, b:b + 1], smax[:, b:b + 1], -SCALE, None, ALU.mult).then_inc(sem("sample_maxima"), 1)

            def sample_normalise(b):
                dve.wait_ge(sem("sprob_raw"), b + 1)
                dve.reciprocal(sinv[:, b:b + 1], ssum[:, b:b + 1])
                dve.drain()
                dve.tensor_scalar(sprob[:, b, :], sprob[:, b, :], sinv[:, b:b + 1], None, ALU.mult).then_inc(sem("sprob_ready"), 1)

            dve.memset(att[:, :, SEQ:NT], 0.0).then_inc(sem("att_zeroed"), 1)
            for h in range(MH):
                softmax_head(h)
                if h >= 1:
                    sample_normalise(2 * h - 1)
                sample_max(2 * h)
                normalise_head(h)
                sample_normalise(2 * h)
                sample_max(2 * h + 1)
            sample_normalise(BS - 1)
            for g in range(2, 4):
                dve.wait_ge(sem("sprob_turned"), g + 1)
                dve.tensor_copy(sprobT[:, 2 * g:2 * g + 2].rearrange("p b t n -> p (b t n)"), m.ps[2 + g][:, :])\
                   .then_inc(sem("sprobT_ready"), 1)
            dve.wait_ge(sem("sample_y_turned"), 1)
            for j in range(KW):
                dve.tensor_copy(sample_cols(yv[:, j, SEQ:NT]),
                                       m.ps[0][:, j * 32:(j + 1) * 32].rearrange("p (b t) -> p b t", b=BS))


O_GW = O_PROJ + T_K * PW
O_OW = O_GW + 2 * D
O_GATE = O_OW + 2 * W
O_GTMP = O_GATE + 2 * NT
assert O_GTMP + NT <= O_PROJ + (T_Q + N_Q) * PW
O_MERGED = O_KKEY
assert O_MERGED + KD * NT <= O_EXT


def prefetch_expert(sp, m, io, e, buf, at, sem):
    w = m.at(at, 3, 2 * D)
    for x, name in enumerate(("w_e1", "w_e3", "w_e2")):
        c = KD if x < 2 else 2
        src = io[name][0][ds(e, 1)].rearrange("e (p c) n -> p (e c n)", c=c)
        sp.dma_start(w[:, x, :], src).then_inc(sem(f"expert_weights_{buf}"), 16)


def stage_merge(nc, m, io):
    xT, proj = m.at(O_XT, KD, NT), m.at(O_PROJ, N_PROJ, PW)
    yv, conv = proj[:, T_R:T_R + KW, 1:PW], m.at(O_CONV, KW, NT)
    bonus, outg = m.at(O_AGATE, KW, NT), m.at(O_OUTG, KW, NT)
    order = ((2, "w_o_c", m.at(O_ATT, KW, NT)), (1, "w_o_b", conv), (0, "w_o_a", yv))
    gw = [m.at(O_GW + u * D, KD, P) for u in range(2)]
    ow = [m.at(O_OW + u * W, KW, P) for u in range(2)]
    gate, gtmp = m.at(O_GATE, 2, NT), m.at(O_GTMP, NT)
    merged = m.at(O_MERGED, KD, NT)
    ysq = m.at(O_EXT, KW, NT)
    csq, means = m.at(O_PROJ, KW, NT), m.at(O_PROJ + KW * NT, KW, NT)
    cdev = means[:, 0, :]
    wout, ws = m.at(O_WOUT, KD, D), m.at(O_WS, 2, KD, DE)
    w_in = io["w_in"][0].rearrange("(k p) n -> p k n", p=P)
    sem = m.sem
    s_g, s_o = sem("gate_product"), sem("branch_product")
    s_sig, s_free, s_m = sem("gates_ready"), sem("merge_banks_free"), sem("branch_merged")
    s_ns, s_nr = sem("norm_sums"), sem("norm_sums_read")
    I = KD // 2

    with nc.Block() as block:
        @block.sync
        def _(sp):
            def load(x, u, tile):
                b, name, _ = order[x]
                w_o = io[name][0].rearrange("(k p) n -> p k n", p=P)
                sp.dma_start(gw[u], w_in[:, :, ds(tile * P + OFF_GATE + b * D, P)]).then_inc(sem(f"branch_weights_{u}"), 16)
                sp.dma_start(ow[u], w_o[:, :, ds(tile * P, P)]).then_inc(sem(f"branch_weights_{u}"), 16)

            for x in range(3):
                if x == 0:
                    load(0, 0, 0)
                    load(0, 1, 1)
                if x == 1:
                    w = io["w_out"][0].rearrange("(k p) n -> p k n", p=P)
                    for k in range(0, KD, 4):
                        sp.dma_start(wout[:, k:k + 4, :], w[:, k:k + 4, :]).then_inc(sem("w_out_loaded"), 16)
                if x == 2:
                    for y, name in enumerate(("w_s1", "w_s3")):
                        sp.dma_start(ws[:, y], io[name][0].rearrange("(k p) n -> p k n", p=P)).then_inc(sem("shared_loaded"), 16)
                with sp.Fori(1 if x == 0 else 0, I) as i:
                    for u in range(2):
                        sp.wait_ge(s_o, 8 * x + 2 * i + u - 1)
                        load(x, u, 2 * i + u)

        @block.tensor
        def _(pe):
            def step(x, i, u):
                pe.wait_ge(sem(f"branch_weights_{u}"), 32 * I * x + 32 * i + 32)
                pe.wait_ge(s_free, 8 * x + 2 * i + u + 1)
                for k in range(KD):
                    for h in range(2):
                        mm = pe.matmul(m.ps[4 * u + h][:, 0:HALF], gw[u][:, k, :], xT[:, k, h * HALF:(h + 1) * HALF],
                                       start=(k == 0), stop=(k == KD - 1))
                mm.then_inc(s_g, 1)
                for k in range(KW):
                    for h in range(2):
                        mm = pe.matmul(m.ps[4 * u + 2 + h][:, 0:HALF], ow[u][:, k, :],
                                       order[x][2][:, k, h * HALF:(h + 1) * HALF], start=(k == 0), stop=(k == KW - 1))
                mm.then_inc(s_o, 1)

            def head_sums(src):
                for j in range(KW):
                    for h in range(2):
                        mm = pe.matmul(m.ps[2 * j + h][:, 0:HALF], m.heads[:, :], src[:, j, h * HALF:(h + 1) * HALF],
                                       start=True, stop=True)
                mm.then_inc(s_ns, 1)

            def channel_sums(src):
                for h in range(2):
                    for j in range(KW):
                        mm = pe.matmul(m.ps[h][:, 0:HALF], m.ones[:, :], src[:, j, h * HALF:(h + 1) * HALF],
                                       start=(j == 0), stop=(j == KW - 1))
                mm.then_inc(s_ns, 1)

            for i in range(I):
                if i >= 1:
                    pe.wait_ge(s_free, 2 * i + 2)
                if i == 0:
                    head_sums(yv)
                elif i == 1:
                    channel_sums(conv)
                elif i == 2:
                    pe.wait_ge(sem("y_squared"), 1)
                    head_sums(ysq)
                else:
                    pe.wait_ge(sem("conv_squared"), 1)
                    channel_sums(csq)
                pe.wait_ge(s_nr, i + 1)
                for u in range(2):
                    step(0, i, u)
            for x in (1, 2):
                pe.wait_ge(sem("conv_ready" if x == 1 else "rwkv_ready"), 1)
                with pe.Fori(0, I) as i:
                    for u in range(2):
                        step(x, i, u)

        @block.scalar
        def _(act):
            def step(x, i, u):
                s = 8 * x + 2 * i + u
                act.wait_ge(s_g, s + 1)
                act.wait_ge(s_free, s + 1)
                for h in range(2):
                    last = act.activation(gate[:, u, h * HALF:(h + 1) * HALF], m.ps[4 * u + h][:, 0:HALF], ACT.Sigmoid)
                last.then_inc(s_sig, 1)

            for i in range(I):
                act.wait_ge(s_ns, i + 1)
                if i == 3:
                    act.wait_ge(sem("conv_centred"), 1)
                for h in range(2):
                    cols = slice(h * HALF, (h + 1) * HALF)
                    if i == 0:
                        for j in range(KW):
                            last = act.activation(means[:, j, cols], m.ps[2 * j + h][:, 0:HALF], ACT.Copy, scale=-1.0 / HD)
                    elif i == 1:
                        if h == 0:
                            act.wait_ge(sem("y_centred"), 1)
                        last = act.activation(cdev[:, cols], m.ps[h][:, 0:HALF], ACT.Copy, scale=-1.0 / W)
                    elif i == 2:
                        for j in range(KW):
                            last = act.activation(ysq[:, j, cols], m.ps[2 * j + h][:, 0:HALF], ACT.Sqrt, scale=1.0 / HD,
                                                  bias=m.eps[:, 0:1])
                    else:
                        last = act.activation(cdev[:, cols], m.ps[h][:, 0:HALF], ACT.Sqrt, scale=1.0 / W, bias=m.eps[:, 1:2])
                last.then_inc(s_nr, 1)
                for u in range(2):
                    step(0, i, u)
            act.wait_ge(sem("conv_normed"), 1)
            for j in range(KW):
                last = act.activation(conv[:, j, :], conv[:, j, :], ACT.Silu, scale=m.vec[:, V_CG + j:V_CG + j + 1],
                                      bias=m.vec[:, V_CBB + j:V_CBB + j + 1])
            last.then_inc(sem("conv_ready"), 1)
            for x in (1, 2):
                with act.Fori(0, I) as i:
                    for u in range(2):
                        step(x, i, u)

        @block.vector
        def _(dve):
            def step(x, i, u):
                s = 8 * x + 2 * i + u
                dst = merged[:, ds(2 * i + u, 1), :].rearrange("p a n -> p (a n)")
                dve.wait_ge(s_sig, s + 1)
                dve.wait_ge(s_o, s + 1)
                for h in range(2):
                    cols = slice(h * HALF, (h + 1) * HALF)
                    last = dve.tensor_tensor(dst[:, cols] if x == 0 else gtmp[:, cols], m.ps[4 * u + 2 + h][:, 0:HALF],
                                             gate[:, u, cols], ALU.mult)
                last.then_inc(s_m, 1)
                dve.wait_ge(s_m, s + 1)
                dve.sem_inc(s_free, 1)
                if x:
                    dve.tensor_tensor(dst, dst, gtmp, ALU.add)
                    dve.drain()

            dve.sem_inc(s_free, 2)
            for i in range(I):
                dve.wait_ge(s_nr, i + 1)
                if i == 0:
                    dve.tensor_tensor(yv, yv, means, ALU.add).then_inc(sem("y_centred"), 1)
                    dve.drain()
                    dve.tensor_tensor(ysq, yv, yv, ALU.mult).then_inc(sem("y_squared"), 1)
                elif i == 1:
                    for j in range(KW):
                        last = dve.tensor_tensor(conv[:, j, :], conv[:, j, :], cdev, ALU.add)
                    last.then_inc(sem("conv_centred"), 1)
                    dve.drain()
                    dve.tensor_tensor(csq, conv, conv, ALU.mult).then_inc(sem("conv_squared"), 1)
                elif i == 3:
                    dve.reciprocal(cdev, cdev)
                    dve.drain()
                    for j in range(KW):
                        last = dve.tensor_tensor(conv[:, j, :], conv[:, j, :], cdev, ALU.mult)
                    last.then_inc(sem("conv_normed"), 1)
                for u in range(2):
                    step(0, i, u)
            with dve.Fori(0, I) as i:
                for u in range(2):
                    step(1, i, u)
                    y, dev = yv[:, ds(i, 1), :], ysq[:, ds(i, 1), :]
                    if u == 0:
                        dve.reciprocal(dev, dev)
                        dve.drain()
                        dve.tensor_tensor(y, y, dev, ALU.mult)
                        dve.drain()
                    else:
                        dve.tensor_scalar(y, y, m.vec[:, ds(i + V_LG, 1)], m.vec[:, ds(i + V_LB, 1)], ALU.mult, ALU.add)
                        dve.drain()
                        dve.tensor_tensor(y, y, bonus[:, ds(i, 1), :], ALU.add)
                        dve.drain()
                        dve.tensor_tensor(y, y, outg[:, ds(i, 1), :], ALU.mult)
                        dve.drain()
            dve.sem_inc(sem("rwkv_ready"), 1)
            with dve.Fori(0, I) as i:
                for u in range(2):
                    step(2, i, u)


O_WOUT = O_TOP
O_WS = O_WOUT + KD * D
assert O_WS + 2 * KD * DE <= ARENA
O_ROWS = O_PROJ + 8 * D
O_LNZ = O_ROWS + 2 * D
O_LNP = O_LNZ + 2 * D
assert O_LNP + 2 * D <= O_RATE
O_JUNK = O_RATE
O_W2S = O_RATE + D
O_WR = O_W2S + 2 * D
O_BR = O_WR + D
O_MSTAT = O_BR + NE
assert O_MSTAT + 64 <= O_MERGED
O_HT = O_MERGED + KD * NT
assert O_HT + KD * NT <= O_TOP
O_SCORE = O_MSTAT + 64
O_WEXP = (O_TOP, O_TOP + WEXP, 0, WEXP)
AHEAD = 3
NEP = NE + AHEAD
O_PLACE = O_SCORE + NTT * NE
O_INFO = O_HT + KD * NT
O_XMORE = (O_INFO + NTT * NEP * 3, O_INFO + NTT * NEP * 3 + D, O_PLACE + NTT * NEP)
O_ROUTE = (O_MERGED + 4 * NT, O_JUNK, O_WR)
assert O_SCORE >= 2 * WEXP and O_XMORE[2] + D <= O_MERGED and O_XMORE[1] + D <= O_TOP
assert O_ROUTE[0] + 3 * NTT * NE + 8 * NTT + 32 <= O_MERGED + KD * NT and O_WEXP[3] + WEXP <= O_ROWS
ABSENT = 4096.0
MAX_ROUNDS = (BS * TS + SEQ + SLOTS - 1) // SLOTS


def stage_mix(nc, m, io):
    merged, hT = m.at(O_MERGED, KD, NT), m.at(O_HT, KD, NT)
    wout, xr, z = m.at(O_WOUT, KD, D), m.at(O_ROWS, 2, D), m.at(O_LNZ, 2, D)
    lnp, junk, w2s, wr = m.at(O_LNP, 2, D), m.at(O_JUNK, D), m.at(O_W2S, 2, D), m.at(O_WR, KD, NE)
    ws = m.at(O_WS, 2, KD, DE)
    sact = m.at(O_MERGED, 2, NT)
    ssil = m.at(O_MERGED + 2 * NT, 2, NT)
    stats, score = m.at(O_MSTAT, NTT, 8), m.at(O_SCORE, NTT, NE)
    xin = [xr[:, 0, :], xr[:, 1, :], *(m.at(o, D) for o in O_XMORE)]
    place, info, bias = m.at(O_PLACE, NTT, NEP), m.at(O_INFO, NTT, NEP, 3), m.at(O_BR, NE)
    sel, rest, picked = (m.at(O_ROUTE[0] + x * NTT * NE, NTT, NE) for x in range(3))
    top8, small = m.at(O_ROUTE[0] + 3 * NTT * NE, NTT, 8), m.at(O_ROUTE[0] + 3 * NTT * NE + 8 * NTT, 32)
    rank, gated = m.at(O_ROUTE[1], NTT, NE), m.at(O_ROUTE[2], NTT, NE)
    s_pick, s_pos = m.sem("experts_picked"), m.sem("queue_places")
    sem = m.sem
    s_z, s_mean, s_sq = sem("z_product"), sem("z_mean"), sem("z_squares")
    s_var, s_dev, s_h, s_zf = sem("z_variance"), sem("z_deviation"), sem("h_rows_ready"), sem("z_banks_read")
    s_ht, s_hc, s_rt, s_rc = sem("h_turned"), sem("h_turned_copied"), sem("router_done"), sem("router_copied")

    with nc.Block() as block:
        @block.sync
        def _(sp):
            sp.dma_start(wr, io["w_router"][0].rearrange("(k p) n -> p k n", p=P)).then_inc(sem("router_loaded"), 16)
            sp.dma_start(w2s, io["w_s2"][0].rearrange("(k p) n -> p k n", p=P)).then_inc(sem("shared_loaded"), 16)
            sp.dma_start(bias, io["b_router"][0:1, :].to_broadcast([P, NE])).then_inc(sem("router_bias_loaded"), 16)
            sp.wait_ge(sem("x_again_1"), 16)
            for e in (2, 3):
                prefetch_expert(sp, m, io, e, e, O_WEXP[e], sem)
            for i, (c0, n) in enumerate(TILES):
                sp.wait_ge(s_h, i + 1)
                sp.dma_start(io["h_rows"][c0:c0 + n, :], z[0:n, i % 2, :]).then_inc(sem(f"h_rows_out_{i % 2}"), 16)
            prefetch_expert(sp, m, io, 0, 0, O_WEXP[0], sem)
            sp.wait_ge(sem("shared_hidden"), 4)
            prefetch_expert(sp, m, io, 1, 1, O_WEXP[1], sem)
            for i, (c0, n) in enumerate(TILES):
                sp.wait_ge(sem("shared_rows_added"), i + 1)
                sp.dma_start(io["residual"][c0:c0 + n, :], xin[i][0:n, :]).then_inc(sem("residual_out"), 16)
            sp.wait_ge(sem("residual_out"), 16 * NTT)
            sp.wait_ge(sem("h_rows_out_0"), 48)
            sp.wait_ge(sem("h_rows_out_1"), 32)

        @block.gpsimd
        def _(pool):
            pool.memset(score[:, NTT - 1, :], 1.0).then_inc(sem("score_zeroed"), 1)
            for x, name in enumerate(("ln1_g", "ln1_b")):
                pool.dma_start(lnp[:, x, :], io[name][0:1, :].to_broadcast([P, D]))\
                    .then_inc(sem("ln1_loaded"), 16)
            for i, (c0, n) in enumerate(TILES[:-1]):
                pool.dma_start(xin[i], io["x_prompt"][0, c0:c0 + n, :]).then_inc(sem(f"x_again_{i}"), 16)
            pool.dma_start(xin[-1][0:NS:SB, :], io["state_shift"][0]).then_inc(sem(f"x_again_{NTT - 1}"), 16)
            for t in range(TS):
                pool.dma_start(xin[-1][1 + t:NS:SB, :], io["x_sample"][:, t, :]).then_inc(sem(f"x_again_{NTT - 1}"), 16)
            for i, (c0, n) in enumerate(TILES):
                pool.wait_ge(s_h, i + 1)
                pool.tensor_scalar(xin[i][0:n, :], z[0:n, i % 2, :], ALPHA, None, ALU.mult).then_inc(sem("h_kept"), 1)

        @block.tensor
        def _(pe):
            def product(i):
                c0, n = TILES[i]
                if i >= 2:
                    pe.wait_ge(s_mean, i - 1)
                for k in range(KD):
                    for h in range(2):
                        mm = pe.matmul(m.ps[2 * (i % 2) + h][0:n, :], merged[:, k, c0:c0 + n],
                                       wout[:, k, h * 512:(h + 1) * 512], start=(k == 0), stop=(k == KD - 1))
                mm.then_inc(s_z, 1)

            def turn(i):
                c0, n = TILES[i]
                pe.wait_ge(s_h, i + 1)
                if i >= 1:
                    pe.wait_ge(s_hc, i)
                for k in range(KD):
                    mm = pe.transpose(m.ps[4 + k // 4][:, (k % 4) * n:(k % 4 + 1) * n], z[0:n, i % 2, k * P:(k + 1) * P],
                                      m.ident[0:n, 0:n])
                mm.then_inc(s_ht, 1)

            def route(i):
                c0, n = TILES[i]
                pe.wait_ge(s_hc, i + 1)
                if i >= 1:
                    pe.wait_ge(s_rc, i)
                for k in range(KD):
                    mm = pe.matmul(m.ps[6][0:n, 0:NE], hT[:, k, c0:c0 + n], wr[:, k, :], start=(k == 0), stop=(k == KD - 1))
                mm.then_inc(s_rt, 1)

            pe.wait_ge(sem("w_out_loaded"), 32)
            pe.wait_ge(sem("router_loaded"), 16)
            product(0)
            for i in range(NTT):
                if i + 1 < NTT:
                    product(i + 1)
                turn(i)
                route(i)
            pe.wait_ge(sem("shared_loaded"), 48)
            pe.wait_ge(s_rc, NTT)
            for j in range(2):
                for x in range(2):
                    for k in range(KD):
                        for h in range(2):
                            mm = pe.matmul(m.ps[4 * j + 2 * x + h][:, 0:HALF], ws[:, x, k, j * P:(j + 1) * P],
                                           hT[:, k, h * HALF:(h + 1) * HALF], start=(k == 0), stop=(k == KD - 1))
                    mm.then_inc(sem("shared_hidden"), 1)
            pe.wait_ge(sem("shared_act"), 2)
            for i in range(NTT):
                out = m.ps[4 + i // 4][:, (i % 4) * NE:(i % 4 + 1) * NE]
                for k in range(i):
                    pe.matmul(out, m.ones[:, :], picked[:, k, :], start=(k == 0), stop=False)
                pe.matmul(out, m.upper[:, 0, :], picked[:, i, :], start=(i == 0), stop=True)
            for k in range(NTT):
                mm = pe.matmul(m.ps[6][:, 0:NE], m.ones[:, :], picked[:, k, :], start=(k == 0), stop=(k == NTT - 1))
            mm.then_inc(s_pos, 1)
            for i, (c0, n) in enumerate(TILES):
                if i >= 2:
                    pe.wait_ge(sem("shared_rows_added"), i - 1)
                for h in range(2):
                    for j in range(2):
                        mm = pe.matmul(m.ps[2 * (i % 2) + h][0:n, :], sact[:, j, c0:c0 + n], w2s[:, j, h * 512:(h + 1) * 512],
                                       start=(j == 0), stop=(j == 1))
                mm.then_inc(sem("shared_rows"), 1)

        @block.scalar
        def _(act):
            def copy_turned(i):
                c0, n = TILES[i]
                act.wait_ge(s_ht, i + 1)
                for g in range(2):
                    last = act.activation(hT[:, 4 * g:4 * g + 4, c0:c0 + n],
                                          m.ps[4 + g][:, 0:4 * n].rearrange("p (k n) -> p k n", k=4), ACT.Copy)
                last.then_inc(s_hc, 1)
                act.wait_ge(s_rt, i + 1)
                act.activation(score[0:n, i, :], m.ps[6][0:n, 0:NE], ACT.Copy).then_inc(s_rc, 1)

            act.wait_ge(sem("score_zeroed"), 1)
            for i, (c0, n) in enumerate(TILES):
                act.wait_ge(s_mean, i + 1)
                act.activation(junk[0:n, :], z[0:n, i % 2, :], ACT.Square, bias=stats[0:n, i, 3:4], accum_out=stats[0:n, i, 4:5])\
                   .then_inc(s_sq, 1)
                act.wait_ge(s_var, i + 1)
                act.activation(stats[0:n, i, 6:7], stats[0:n, i, 5:6], ACT.Sqrt).then_inc(s_dev, 1)
                copy_turned(i)
            act.drain()
            for i, (c0, n) in enumerate(TILES):
                last = act.activation(score[0:n, i, :], score[0:n, i, :], ACT.Sigmoid)
            last.then_inc(sem("scores_ready"), 1)
            for j in range(2):
                act.wait_ge(sem("shared_hidden"), 2 * j + 1)
                for h in range(2):
                    last = act.activation(ssil[:, j, h * HALF:(h + 1) * HALF], m.ps[4 * j + h][:, 0:HALF], ACT.Silu)
                last.then_inc(sem("shared_silu"), 1)

        @block.vector
        def _(dve):
            dve.wait_ge(sem("ln1_loaded"), 32)
            for i, (c0, n) in enumerate(TILES):
                x, zi, st = xin[i][0:n, :], z[0:n, i % 2, :], stats[0:n, i, :]
                dve.wait_ge(s_z, i + 1)
                dve.wait_ge(sem(f"x_again_{i}"), 16 if i < NTT - 1 else 16 * (1 + TS))
                if i >= 2:
                    dve.wait_ge(sem(f"h_rows_out_{i % 2}"), 16 * (i // 2))
                    dve.wait_ge(s_ht, i - 1)
                    dve.wait_ge(sem("h_kept"), i - 1)
                for h in range(2):
                    cols = slice(h * 512, (h + 1) * 512)
                    dve.scalar_tensor_tensor(out=zi[:, cols], in0=x[:, cols], scalar=ALPHA, in1=m.ps[2 * (i % 2) + h][0:n, :],
                                             op0=ALU.mult, op1=ALU.add, accum_out=st[:, h:h + 1])
                dve.drain()
                dve.tensor_tensor(st[:, 2:3], st[:, 0:1], st[:, 1:2], ALU.add)
                dve.drain()
                dve.tensor_scalar(st[:, 3:4], st[:, 2:3], -1.0 / D, None, ALU.mult).then_inc(s_mean, 1)
                dve.wait_ge(s_sq, i + 1)
                dve.tensor_scalar(st[:, 5:6], st[:, 4:5], 1.0 / D, LN_EPS, ALU.mult, ALU.add).then_inc(s_var, 1)
                dve.wait_ge(s_dev, i + 1)
                dve.reciprocal(st[:, 7:8], st[:, 6:7])
                dve.drain()
                dve.tensor_scalar(zi, zi, st[:, 3:4], st[:, 7:8], ALU.add, ALU.mult)
                dve.drain()
                dve.tensor_tensor(zi, zi, lnp[0:n, 0, :], ALU.mult)
                dve.drain()
                dve.tensor_tensor(zi, zi, lnp[0:n, 1, :], ALU.add).then_inc(s_h, 1)
            dve.wait_ge(sem("scores_ready"), 1)
            dve.wait_ge(sem("router_bias_loaded"), 16)
            for i in range(NTT):
                dve.tensor_tensor(sel[:, i, :], score[:, i, :], bias, ALU.add)
            dve.drain()
            for i in range(NTT):
                dve.max(top8[:, i, :], sel[:, i, :])
            dve.drain()
            for i in range(NTT):
                dve.match_replace(rest[:, i, :], top8[:, i, :], sel[:, i, :], -1e30)
            dve.drain()
            dve.tensor_tensor(picked, rest, sel, ALU.not_equal)
            dve.drain()
            dve.tensor_scalar(picked[:, NTT - 1, :], picked[:, NTT - 1, :], m.valid[:, 0:1], None, ALU.mult)
            dve.drain()
            dve.tensor_tensor(gated, picked, score, ALU.mult).then_inc(s_pick, 1)
            for j in range(2):
                dve.wait_ge(sem("shared_silu"), j + 1)
                dve.wait_ge(sem("shared_hidden"), 2 * j + 2)
                for h in range(2):
                    last = dve.tensor_tensor(sact[:, j, h * HALF:(h + 1) * HALF], m.ps[4 * j + 2 + h][:, 0:HALF],
                                             ssil[:, j, h * HALF:(h + 1) * HALF], ALU.mult)
                last.then_inc(sem("shared_act"), 1)
            for i in range(NTT):
                dve.tensor_tensor_scan(rank[:, i, :], m.ones[:, :], picked[:, i, :], 0.0, ALU.mult, ALU.add)
            dve.drain()
            den, scale = small[:, 0:NTT], small[:, 8:8 + NTT]
            dve.tensor_reduce(den, gated, AX.X, ALU.add)
            dve.drain()
            dve.tensor_scalar(den, den, 1e-30, 1.0 / ROUTED, ALU.max, ALU.mult)
            dve.drain()
            dve.reciprocal(scale, den)
            dve.drain()
            rows8 = small[:, 16:16 + NTT]
            dve.tensor_scalar(rows8, m.row[:, :], float(TOPK), -1.0 - FAR, ALU.mult, ALU.add)
            dve.memset(info[:, :, NE:NEP, :], 0.0)
            dve.memset(place[:, :, NE:NEP], ABSENT)
            dve.drain()
            for i in range(NTT):
                dve.tensor_scalar(info[:, i, 0:NE, 0], m.ones[:, :], m.row[:, i:i + 1], -FAR, ALU.mult, ALU.add)
                dve.tensor_scalar(info[:, i, 0:NE, 1], rank[:, i, :], rows8[:, i:i + 1], None, ALU.add)
                dve.tensor_scalar(info[:, i, 0:NE, 2], gated[:, i, :], scale[:, i:i + 1], None, ALU.mult)
            dve.wait_ge(s_pos, 1)
            dve.tensor_scalar(rest, picked, -ABSENT, ABSENT, ALU.mult, ALU.add)
            dve.drain()
            dve.tensor_tensor(place[:, 0:4, 0:NE], m.ps[4][:, :].rearrange("p (a n) -> p a n", a=4), rest[:, 0:4, :], ALU.add)
            dve.tensor_tensor(place[:, 4, 0:NE], m.ps[5][:, 0:NE], rest[:, 4, :], ALU.add)
            most, more = small[:, 24:25], small[:, 25:26]
            dve.tensor_reduce(most, m.ps[6][:, 0:NE], AX.X, ALU.max)
            dve.drain()
            dve.tensor_scalar(top8[:, 0, 0:MAX_ROUNDS - 1], m.slot[:, 1:MAX_ROUNDS], float(SLOTS), most, ALU.mult, ALU.is_lt)
            dve.drain()
            dve.tensor_reduce(more, top8[:, 0, 0:MAX_ROUNDS - 1], AX.X, ALU.add)
            dve.drain()
            dve.tensor_scalar(m.rounds[:, :], more, 1.0, None, ALU.add)
            for i, (c0, n) in enumerate(TILES):
                if i == 0:
                    dve.wait_ge(sem("h_kept"), NTT)
                dve.wait_ge(sem("shared_rows"), i + 1)
                for h in range(2):
                    cols = slice(h * 512, (h + 1) * 512)
                    last = dve.tensor_tensor(xin[i][0:n, cols], xin[i][0:n, cols], m.ps[2 * (i % 2) + h][0:n, :], ALU.add)
                last.then_inc(sem("shared_rows_added"), 1)


O_XG = 2 * WEXP
assert O_XG + 4 * D <= O_SCORE
O_LN2 = 24 * 1024
assert O_PLACE + NTT * NEP <= O_LN2 and O_LN2 + 2 * D <= O_TOP
O_XTE = O_LN2 + 2 * D
O_YG = O_XTE + 2 * KD * SLOTS
O_OH = O_YG + D
O_HE = O_OH + 2 * NTT * 2 * SLOTS
O_SE = O_HE + 2 * 2 * SLOTS
O_SI = O_SE + 2 * 2 * SLOTS
assert O_SI + 4 * 3 <= O_INFO and O_INFO + NTT * NEP * 3 <= O_TOP


def stage_experts(nc, m, io):
    place, info = m.at(O_PLACE, NTT, NEP), m.at(O_INFO, NTT, NEP, 3)
    xg, yg = m.at(O_XG, 4, D), m.at(O_YG, 2, D // 2)
    xt, onehot = m.at(O_XTE, 2, KD, SLOTS), m.at(O_OH, 2, NTT, 2 * SLOTS)
    hid, sil, slots = m.at(O_HE, 2, 2, SLOTS), m.at(O_SE, 2, 2 * SLOTS), m.at(O_SI, 4, 3)
    weights = [m.at(o, 3, 2 * D) for o in O_WEXP]
    w1 = [w[:, 0, :].rearrange("p (c n) -> p c n", c=KD) for w in weights]
    w3 = [w[:, 1, :].rearrange("p (c n) -> p c n", c=KD) for w in weights]
    w2 = [w[:, 2, :].rearrange("p (c n) -> p c n", c=2) for w in weights]
    sem = m.sem
    s_oh, s_slot, s_idx = sem("one_hot_ready"), sem("slots_found"), sem("slot_indices_ready")
    s_in = [sem(f"rows_gathered_{u}") for u in range(4)]
    gathers = [(NEP - u + 3) // 4 for u in range(4)]
    s_out = [sem(f"rows_scattered_{u}") for u in range(2)]
    s_t, s_xt = sem("expert_rows_turned"), sem("expert_rows_copied")
    s_gu, s_sil, s_hid, s_y = sem("expert_products"), sem("expert_silu"), sem("expert_hidden"), sem("expert_output")
    s_yv, s_ya = sem("output_scaled_vector"), sem("output_scaled_scalar")
    S = SLOTS

    def rounds(eng):
        return eng.value_load(m.rounds[0:1, 0:1], min_val=1, max_val=MAX_ROUNDS)

    with nc.Block() as block:
        @block.sync
        def _(sp):
            count = rounds(sp)
            for x, name in enumerate(("ln2_g", "ln2_b")):
                sp.dma_start(m.at(O_LN2, 2, D)[:, x, :], io[name][0:1, :].to_broadcast([P, D])).then_inc(sem("ln2_loaded"), 16)

            def load(r, first, u, e):
                sp.wait_ge(s_y, NE * r + first + u + 1)
                prefetch_expert(sp, m, io, e, u, O_WEXP[u], sem)

            with sp.Fori(0, count) as r:
                with sp.Fori(0, NE // 4 - 1) as i:
                    for u in range(4):
                        load(r, 4 * i, u, 4 * i + 4 + u)
                with sp.If(r < count - 1):
                    for u in range(4):
                        load(r, NE - 4, u, u)

        @block.gpsimd
        def _(pool):
            count = rounds(pool)
            for u in range(4):
                pool.dma_start(xg[0:S, u, :], io["h_rows"][0:S, :]).then_inc(s_out[u % 2], 16)
            for u in range(2):
                pool.wait_ge(s_out[u], 32)

            def gather(r, n, u):
                pool.wait_ge(s_idx, NEP * r + n + 2)
                pool.sem_inc(sem("gathers_begun"), 1)
                pool.indirect_dma_start(xg[0:S, u, :], None, io["h_rows"][:, :],
                                        bass.IndirectOffsetOnAxis(ap=m.index[0:S, u, 0:1], axis=0),
                                        bounds_check=NT - 1, oob_is_err=False).then_inc(s_in[u], 16)

            with pool.Fori(0, count) as r:
                for n in range(AHEAD):
                    gather(r, n, n)
                with pool.Fori(0, NE // 4) as i:
                    for u in range(4):
                        n = 4 * i + u
                        gather(r, n + AHEAD, (u + AHEAD) % 4)
                        pool.wait_ge(s_yv, NE * r + n + 3)
                        pool.wait_ge(s_ya, NE * r + n + 3)
                        pool.sem_inc(sem("scatters_begun"), 1)
                        pool.indirect_dma_start(io["routed_halves"][:, :],
                                                bass.IndirectOffsetOnAxis(ap=m.index[:, u, 1:2], axis=0),
                                                yg[:, u % 2, :], None,
                                                bounds_check=2 * NT * TOPK - 1, oob_is_err=False).then_inc(s_out[u % 2], 16)

        @block.tensor
        def _(pe):
            count = rounds(pe)

            def find_slots(r, n, u):
                pe.wait_ge(s_oh, NEP * r + n + 1)
                pe.wait_ge(s_idx, NEP * r + n + 1)
                for i in range(NTT):
                    mm = pe.matmul(m.ps[0][:, 0:3], onehot[:, u % 2, i, :],
                                   info[:, i, ds(n, 1), :], start=(i == 0), stop=(i == NTT - 1))
                mm.then_inc(s_slot, 1)

            def turn(u):
                for c in range(KD):
                    mm = pe.transpose(m.ps[1][:, c * S:(c + 1) * S], xg[0:S, u % 4, c::KD], m.ident[0:S, 0:S])
                mm.then_inc(s_t, 1)

            with pe.Fori(0, count) as r:
                find_slots(r, 0, 0)
                find_slots(r, 1, 1)
                pe.wait_ge(s_in[0], 16 * gathers[0] * r + 16)
                pe.wait_ge(s_xt, (NE + 1) * r + 1)
                find_slots(r, 2, 2)
                turn(0)
                with pe.Fori(0, NE // 4) as i:
                    for u in range(4):
                        n = 4 * i + u
                        prod = m.ps[2 + u % 2]
                        pe.wait_ge(sem(f"expert_weights_{u}"), (48 * NE // 4) * r + 48 * i + 48)
                        pe.wait_ge(s_xt, (NE + 1) * r + n + 2)
                        for x, w in enumerate((w1[u], w3[u])):
                            for j in range(2):
                                q = 2 * x + j
                                for c in range(KD):
                                    mm = pe.matmul(prod[:, q * S:(q + 1) * S], w[:, c, j::2], xt[:, u % 2, c, :],
                                                   start=(c == 0), stop=(c == KD - 1))
                        mm.then_inc(s_gu, 1)
                        pe.wait_ge(s_in[(u + 1) % 4], 16 * gathers[(u + 1) % 4] * r + 16 * i + 16 * ((u + 1) // 4) + 16)
                        find_slots(r, n + AHEAD, u + AHEAD)
                        turn(u + 1)
                        pe.wait_ge(s_hid, NE * r + n + 1)
                        pe.wait_ge(s_yv, NE * r + n + 1)
                        pe.wait_ge(s_ya, NE * r + n + 1)
                        for j in range(2):
                            for h in range(2):
                                mm = pe.matmul(m.ps[4 + 2 * (u % 2) + h][h * S:(h + 1) * S, :], hid[:, u % 2, j, :],
                                               w2[u][:, j, h * 512:(h + 1) * 512], start=(j == 0), stop=(j == 1))
                        mm.then_inc(s_y, 1)

        @block.scalar
        def _(act):
            count = rounds(act)
            act.sem_inc(s_ya, 2)
            act.sem_inc(s_xt, 1)

            def copy_turned(r, n, u):
                act.wait_ge(s_t, (NE + 1) * r + n + 1)
                act.activation(xt[:, u % 2, :, :], m.ps[1][:, :].rearrange("p (c s) -> p c s", c=KD), ACT.Copy)\
                   .then_inc(s_xt, 1)

            with act.Fori(0, count) as r:
                copy_turned(r, 0, 0)
                with act.Fori(0, NE // 4) as i:
                    for u in range(4):
                        n = 4 * i + u
                        act.wait_ge(s_gu, NE * r + n + 1)
                        act.activation(sil[:, u % 2, :], m.ps[2 + u % 2][:, 0:2 * S], ACT.Silu).then_inc(s_sil, 1)
                        copy_turned(r, n + 1, u + 1)
                        act.wait_ge(s_y, NE * r + n + 1)
                        act.wait_ge(s_out[u % 2], (16 * NE // 2) * r + 32 * i + 16 * (u // 2) + 32)
                        act.activation(yg[S:P, u % 2, :], m.ps[5 + 2 * (u % 2)][S:P, :], ACT.Copy,
                                       scale=slots[S:P, u, 2:3]).then_inc(s_ya, 1)

        @block.vector
        def _(dve):
            count = rounds(dve)
            dve.sem_inc(s_yv, 2)
            dve.sem_inc(s_idx, 1)

            def one_hot(n, u):
                for i in range(NTT):
                    last = dve.tensor_scalar(onehot[:, u % 2, i, :], m.slot[:, :], place[:, i, ds(n, 1)], None, ALU.is_equal)
                last.then_inc(s_oh, 1)

            def slots_out(r, n, u):
                dve.wait_ge(s_slot, NEP * r + n + 1)
                dve.tensor_copy(slots[:, u, :], m.ps[0][:, 0:3])
                dve.tensor_scalar(m.index[0:S, u, 0:1], m.ps[0][0:S, 0:1], FAR, None, ALU.add).then_inc(s_idx, 1)

            with dve.Fori(0, count) as r:
                for n in range(AHEAD):
                    one_hot(n, n)
                    slots_out(r, n, n)
                with dve.Fori(0, NE // 4) as i:
                    for u in range(4):
                        n = 4 * i + u
                        one_hot(n + AHEAD, u + AHEAD)
                        dve.wait_ge(s_sil, NE * r + n + 1)
                        dve.tensor_tensor(hid[:, u % 2, :, :].rearrange("p j s -> p (j s)"), m.ps[2 + u % 2][:, 2 * S:4 * S],
                                          sil[:, u % 2, :], ALU.mult).then_inc(s_hid, 1)
                        dve.wait_ge(s_ya, NE * r + n + 2)
                        slots_out(r, n + AHEAD, (u + AHEAD) % 4)
                        dve.wait_ge(s_out[u % 2], (16 * NE // 2) * r + 32 * i + 16 * (u // 2) + 32)
                        dve.tensor_scalar(m.index[:, u, 1:2], slots[:, u, 1:2], 2.0, m.half[:, 0:1], ALU.mult, ALU.add)
                        dve.wait_ge(s_y, NE * r + n + 1)
                        dve.tensor_scalar(yg[0:S, u % 2, :], m.ps[4 + 2 * (u % 2)][0:S, :], slots[0:S, u, 2:3], None, ALU.mult)\
                           .then_inc(s_yv, 1)
                for u in range(2):
                    dve.wait_ge(s_out[u], (16 * NE // 2) * r + 16 * NE // 2 + 32)
                for u in range(4):
                    dve.wait_ge(s_in[u], 16 * gathers[u] * r + 16 * gathers[u])
                dve.tensor_scalar(place, place, -float(S), None, ALU.add)
                dve.drain()


O_PART = [i * TOPK * D for i in range(3)] + [O_LN2 + 2 * D + i * TOPK * D for i in range(2)]
O_RES = O_PART[-1] + TOPK * D
O_CSTAT = O_RES + NTT * D
ORDER = (0, 1, 2, 4, 3)
assert 3 * TOPK * D <= O_LN2 and O_CSTAT + 8 * NTT <= ARENA


def stage_combine(nc, m, io):
    part, z = [m.at(o, TOPK, D) for o in O_PART], m.at(O_RES, NTT, D)
    lnp, stats = m.at(O_LN2, 2, D), m.at(O_CSTAT, NTT, 8)
    sem = m.sem
    s_sum, s_sq, s_var, s_dev, s_y = (sem(f"final_{x}") for x in ("sum", "squares", "variance", "deviation", "rows"))
    with nc.Block() as block:
        @block.sync
        def _(sp):
            routed = io["routed_rows"].rearrange("(t k) d -> t k d", k=TOPK)
            for i in ORDER:
                c0, n = TILES[i]
                if i < NTT - 1:
                    for k in range(0, TOPK, 4):
                        sp.dma_start(part[i][:, k:k + 4, :], routed[c0:c0 + n, k:k + 4, :]).then_inc(sem(f"parts_loaded_{i}"), 16)
                    sp.dma_start(z[:, i, :], io["residual"][c0:c0 + n, :]).then_inc(sem(f"parts_loaded_{i}"), 16)
                else:
                    sp.wait_ge(sem("rows_cleared"), 1)
                    for t in range(1, SB):
                        sp.dma_start(part[i][t:NS:SB, :, :], routed[SEQ + t:NT:SB, :, :]).then_inc(sem(f"parts_loaded_{i}"), 16)
                    sp.dma_start(z[0:n, i, :], io["residual"][c0:c0 + n, :]).then_inc(sem(f"parts_loaded_{i}"), 16)
            for at, i in enumerate(ORDER):
                c0, n = TILES[i]
                sp.wait_ge(s_y, at + 1)
                if i < NTT - 1:
                    sp.dma_start(io["out_y_p"][0, c0:c0 + n, :], z[:, i, :]).then_inc(sem("outputs_written"), 16)
                else:
                    for t in range(TS):
                        sp.dma_start(io["out_y_s"][:, t, :], z[1 + t:NS:SB, i, :]).then_inc(sem("outputs_written"), 16)
            sp.wait_ge(sem("outputs_written"), 16 * OUT_ALL)

        @block.gpsimd
        def _(pool):
            pool.memset(part[NTT - 1][0:NS, :, :], 0.0).then_inc(sem("rows_cleared"), 1)
            for i in ORDER:
                n = TILES[i][1]
                rows = part[i][0:n, 4:8, :].rearrange("p k d -> p (k d)")
                pool.wait_ge(sem(f"parts_loaded_{i}"), 16 * (3 if i < NTT - 1 else 1 + TS))
                pool.drain()
                pool.tensor_tensor(rows[:, 0:2 * D], rows[:, 0:2 * D], rows[:, 2 * D:4 * D], ALU.add)
                pool.drain()
                pool.tensor_tensor(rows[:, 0:D], rows[:, 0:D], rows[:, D:2 * D], ALU.add).then_inc(sem("high_ranks_summed"), 1)

        @block.scalar
        def _(act):
            for at, i in enumerate(ORDER):
                n = TILES[i][1]
                zi, st = z[0:n, i, :], stats[0:n, i, :]
                act.wait_ge(s_sum, at + 1)
                act.activation(part[i][0:n, 0, :], zi, ACT.Square, bias=st[:, 1:2], accum_out=st[:, 2:3]).then_inc(s_sq, 1)
                act.wait_ge(s_sq, at + 1)
                act.activation(st[:, 4:5], st[:, 2:3], ACT.Sqrt, scale=1.0 / D, bias=m.eps[0:n, 1:2]).then_inc(s_dev, 1)
                act.wait_ge(s_var, at + 1)
                act.activation(zi, zi, ACT.Identity, scale=st[:, 5:6], bias=st[:, 6:7]).then_inc(sem("final_normed"), 1)

        @block.vector
        def _(dve):
            def total(at, i, n):
                zi, st, rows = z[0:n, i, :], stats[0:n, i, :], part[i][0:n, :, :].rearrange("p k d -> p (k d)")
                dve.wait_ge(sem(f"parts_loaded_{i}"), 16 * (3 if i < NTT - 1 else 1 + TS))
                for width in (2 * D, D):
                    dve.tensor_tensor(rows[:, 0:width], rows[:, 0:width], rows[:, width:2 * width], ALU.add)
                    dve.drain()
                dve.tensor_tensor(zi, zi, rows[:, 0:D], ALU.add)
                dve.wait_ge(sem("high_ranks_summed"), at + 1)
                dve.drain()
                dve.scalar_tensor_tensor(out=zi, in0=zi, scalar=1.0, in1=rows[:, 4 * D:5 * D], op0=ALU.mult, op1=ALU.add,
                                         accum_out=st[:, 0:1])
                dve.drain()
                dve.tensor_scalar(st[:, 1:2], st[:, 0:1], -1.0 / D, None, ALU.mult).then_inc(s_sum, 1)

            def scale(at, i, n):
                st = stats[0:n, i, :]
                dve.wait_ge(s_dev, at + 1)
                dve.reciprocal(st[:, 5:6], st[:, 4:5])
                dve.drain()
                dve.tensor_tensor(st[:, 6:7], st[:, 5:6], st[:, 1:2], ALU.mult).then_inc(s_var, 1)

            def affine(at, i, n):
                zi = z[0:n, i, :]
                dve.wait_ge(sem("final_normed"), at + 1)
                if at == 0:
                    dve.wait_ge(sem("ln2_loaded"), 32)
                dve.tensor_tensor(zi, zi, lnp[0:n, 0, :], ALU.mult)
                dve.drain()
                dve.tensor_tensor(zi, zi, lnp[0:n, 1, :], ALU.add).then_inc(s_y, 1)

            for at, i in enumerate(ORDER):
                total(at, i, TILES[i][1])
                if at >= 1:
                    affine(at - 1, ORDER[at - 1], TILES[ORDER[at - 1]][1])
                scale(at, i, TILES[i][1])
            affine(NTT - 1, ORDER[-1], TILES[ORDER[-1]][1])


STAGES = (stage_load, stage_project, stage_prepare, stage_wkv, stage_attend, stage_merge, stage_mix, stage_experts,
          stage_combine)


SHAPES = {
    "x_prompt": (1, SEQ, D), "x_sample": (BS, TS, D), "state_wkv": (1, BS, 8, HD, HD), "state_shift": (1, BS, D),
    "state_conv": (1, BS, BUF, W), "cache_mem_k": (1, BS, NM, MH, P), "cache_mem_v": (1, BS, NM, MH, P),
    "mem_prompt": (1, NM, D), "w_in": (1, D, OFF_GATE + 3 * D), "mu_shift": (1, RW), "w0": (1, W),
    "w_up": (1, 64, W), "a0": (1, W), "a_up": (1, 64, W), "g_up": (1, 128, W), "k_k": (1, W), "k_a": (1, W),
    "r_k": (1, 8, HD), "lnx_g": (1, W), "lnx_b": (1, W), "w_o_a": (1, W, D), "conv_w": (1, TAPS, W),
    "conv_b": (1, W), "cn_g": (1, W), "cn_b": (1, W), "w_o_b": (1, W, D), "w_mem_kv": (1, D, 2 * W),
    "w_o_c": (1, W, D), "w_out": (1, D, D), "ln1_g": (1, D), "ln1_b": (1, D), "ln2_g": (1, D), "ln2_b": (1, D),
    "w_router": (1, D, NE), "b_router": (1, NE), "w_e1": (1, NE, D, DE), "w_e3": (1, NE, D, DE),
    "w_e2": (1, NE, DE, D), "w_s1": (1, D, DE), "w_s3": (1, D, DE), "w_s2": (1, DE, D),
}
OUTPUTS = [
    ("out_y_p", (1, SEQ, D)), ("out_y_s", (BS, TS, D)), ("out_wkv_p", (1, 1, 8, HD, HD)), ("out_shift_p", (1, 1, D)),
    ("out_conv_p", (1, 1, BUF, W)), ("out_mk", (1, 1, NM, MH, P)), ("out_mv", (1, 1, NM, MH, P)),
    ("out_wkv_s", (1, BS, 8, HD, HD)), ("out_shift_s", (1, BS, D)), ("out_conv_s", (1, BS, BUF, W)),
]


def build(nc):
    io = {n: nc.dram_tensor(f"in_{n}", s, F32, kind="ExternalInput").ap() for n, s in SHAPES.items()}
    io |= {n: nc.dram_tensor(n, s, F32, kind="ExternalOutput").ap() for n, s in OUTPUTS}
    io["sample_vectors"] = nc.dram_tensor("sample_vectors", (8, NS, 6, HD), F32, kind="Internal").ap()
    io["sample_y"] = nc.dram_tensor("sample_y", (2, 8, BS, TS, HD // 2), F32, kind="Internal").ap()
    io["h_rows"] = nc.dram_tensor("h_rows", (NT, D), F32, kind="Internal").ap()
    io["residual"] = nc.dram_tensor("residual", (NT, D), F32, kind="Internal").ap()
    io["routed_rows"] = nc.dram_tensor("routed_rows", (NT * TOPK, D), F32, kind="Internal").ap()
    io["routed_halves"] = io["routed_rows"].rearrange("r (h d) -> (r h) d", h=2)
    with ExitStack() as ctx:
        m = Memory(nc, ctx)
        for stage in STAGES:
            stage(nc, m, io)
            if stage is stage_wkv:
                m.recycle(WKV_ONLY)


def kernel(**inputs):
    import numpy as np
    import concourse.bacc as bacc
    from concourse.bass_utils import run_bass_kernel_spmd

    nc = bacc.Bacc("TRN2", target_bir_lowering=False, num_devices=1)
    build(nc)
    arrays = {f"in_{n}": np.ascontiguousarray(inputs[n]) for n in SHAPES}
    got = run_bass_kernel_spmd(nc, [arrays], core_ids=[0]).results[0]
    return tuple(got[n] for n, _ in OUTPUTS)
```
